# Optimizing a Trainium2 kernel written in Bass

```python
import math
import jax, jax.numpy as jnp
from jax import lax
import numpy as np

D_MODEL = 1024
BATCH = 1
SEQ = 512
DEPTH = 1

SSM_WIDTH = D_MODEL
SSM_GROUP = 16
SSM_GROUPS = SSM_WIDTH // SSM_GROUP
SSM_STATE = 64
SSM_CHUNK = 128
DT_MIN = 1e-3
DT_MAX = 1e-1
HEAD_DIM = 64
HEADS_PER_GROUP = D_MODEL // 128
DILATED_GROUPS = ((128, 1), (512, 4), (2048, 16))
N_DIL = len(DILATED_GROUPS)
ATTN_WIDTH = HEADS_PER_GROUP * HEAD_DIM
QKV_WIDTH = N_DIL * ATTN_WIDTH
ROPE_DIM = HEAD_DIM // 4
ROPE_THETA = 500000.0
Q_BLOCK = 128
NEG_INF = -1e30
EPS = 1e-6
SPLITS = (SSM_WIDTH, SSM_WIDTH, QKV_WIDTH, QKV_WIDTH, QKV_WIDTH, ATTN_WIDTH, D_MODEL, D_MODEL)
IN_WIDTH = sum(SPLITS)


def rms_norm(x, w):
    xf = x.astype(jnp.float32)
    y = xf * lax.rsqrt(jnp.mean(xf * xf, axis=-1, keepdims=True) + EPS)
    return y * w.astype(jnp.float32)

def apply_partial_rope(x, positions):
    half = ROPE_DIM // 2
    inv_freq = ROPE_THETA ** (-jnp.arange(0, ROPE_DIM, 2, dtype=jnp.float32) / ROPE_DIM)
    ang = positions.astype(jnp.float32)[..., None] * inv_freq
    cos = jnp.cos(ang)[:, :, None, None, :]
    sin = jnp.sin(ang)[:, :, None, None, :]
    x1 = x[..., :half]
    x2 = x[..., half:ROPE_DIM]
    return jnp.concatenate([x1 * cos - x2 * sin, x2 * cos + x1 * sin, x[..., ROPE_DIM:]], axis=-1)

def _complex_diag_combine(e1, e2):
    a1r, a1i, b1r, b1i = e1
    a2r, a2i, b2r, b2i = e2
    ar = a2r * a1r - a2i * a1i
    ai = a2r * a1i + a2i * a1r
    br = a2r * b1r - a2i * b1i + b2r
    bi = a2r * b1i + a2i * b1r + b2i
    return (ar, ai, br, bi)

def s5_branch(u, lam_re, lam_im, log_dt, b_re, b_im, c_re, c_im, d_skip, w_glu):
    f32 = jnp.float32
    uf = u.astype(f32)
    lr, li = lam_re.astype(f32), lam_im.astype(f32)
    dt = jnp.exp(log_dt.astype(f32))[:, None]
    mag = jnp.exp(lr * dt)
    ab_re = mag * jnp.cos(li * dt)
    ab_im = mag * jnp.sin(li * dt)
    den = lr * lr + li * li
    nr = ab_re - 1.0
    f_re = (nr * lr + ab_im * li) / den
    f_im = (ab_im * lr - nr * li) / den
    br, bi = b_re.astype(f32), b_im.astype(f32)
    bb_re = f_re[..., None] * br - f_im[..., None] * bi
    bb_im = f_re[..., None] * bi + f_im[..., None] * br
    cr, ci = c_re.astype(f32), c_im.astype(f32)

    bsz, length, _ = u.shape
    n_chunks = length // SSM_CHUNK
    uc = uf.reshape(bsz, n_chunks, SSM_CHUNK, SSM_GROUPS, SSM_GROUP).transpose(1, 0, 2, 3, 4)

    def chunk_step(carry, u_c):
        h0_re, h0_im = carry
        bu_re = jnp.einsum('blgp,gnp->blgn', u_c, bb_re)
        bu_im = jnp.einsum('blgp,gnp->blgn', u_c, bb_im)
        a_re = jnp.broadcast_to(ab_re, bu_re.shape)
        a_im = jnp.broadcast_to(ab_im, bu_im.shape)
        pa_re, pa_im, hs_re, hs_im = lax.associative_scan(
            _complex_diag_combine, (a_re, a_im, bu_re, bu_im), axis=1)
        h_re = hs_re + pa_re * h0_re[:, None] - pa_im * h0_im[:, None]
        h_im = hs_im + pa_re * h0_im[:, None] + pa_im * h0_re[:, None]
        y = jnp.einsum('blgn,gpn->blgp', h_re, cr) - jnp.einsum('blgn,gpn->blgp', h_im, ci)
        return (h_re[:, -1], h_im[:, -1]), y

    zeros = jnp.zeros((bsz, SSM_GROUPS, SSM_STATE), f32)
    _, y = lax.scan(chunk_step, (zeros, zeros), uc)
    y = y.transpose(1, 0, 2, 3, 4).reshape(bsz, length, SSM_WIDTH)
    y = y + d_skip.astype(f32) * uf
    g = jax.nn.gelu(y)
    return g * jax.nn.sigmoid(g @ w_glu.astype(f32))

def dilated_attention(q, k, v):
    bsz, length = q.shape[0], q.shape[1]
    n_blocks = length // Q_BLOCK
    scale = 1.0 / math.sqrt(HEAD_DIM)
    k_groups = [k[:, :, g] for g in range(N_DIL)]
    v_groups = [v[:, :, g] for g in range(N_DIL)]

    def one_block(i):
        t = i * Q_BLOCK + jnp.arange(Q_BLOCK)
        q_blk = lax.dynamic_slice_in_dim(q, i * Q_BLOCK, Q_BLOCK, axis=1)
        outs, lses = [], []
        for g, (window, dil) in enumerate(DILATED_GROUPS):
            j = jnp.arange(window // dil + 1)
            idx = t[:, None] - dil * j[None, :]
            valid = idx >= 0
            idxc = jnp.maximum(idx, 0)
            kg = k_groups[g][:, idxc]
            vg = v_groups[g][:, idxc]
            s = jnp.einsum('bqhd,bqjhd->bqhj', q_blk[:, :, g], kg) * scale
            s = jnp.where(valid[None, :, None, :], s, NEG_INF)
            lse = jax.nn.logsumexp(s, axis=-1)
            p = jnp.exp(s - lse[..., None])
            outs.append(jnp.einsum('bqhj,bqjhd->bqhd', p, vg))
            lses.append(lse)
        w = jax.nn.softmax(jnp.stack(lses), axis=0)
        return jnp.einsum('gbqh,gbqhd->bqhd', w, jnp.stack(outs))

    o = lax.map(one_block, jnp.arange(n_blocks))
    return o.transpose(1, 0, 2, 3, 4).reshape(bsz, length, HEADS_PER_GROUP * HEAD_DIM)

def first_inputs(seed: int = 0) -> dict:
    key = jax.random.key(seed)
    ks = jax.random.split(key, 20)
    f32 = jnp.float32
    x = jax.random.normal(ks[0], (BATCH, SEQ, D_MODEL), f32)
    start = jax.random.randint(ks[1], (BATCH, 1), 0, 1024, dtype=jnp.int32)
    positions = (start + jnp.arange(SEQ, dtype=jnp.int32)[None, :]).astype(jnp.int32)
    norm_w = 1.0 + 0.02 * jax.random.normal(ks[2], (DEPTH, D_MODEL), f32)
    w_in = jax.random.normal(ks[3], (DEPTH, D_MODEL, IN_WIDTH), f32) * D_MODEL ** -0.5
    n_idx = jnp.arange(SSM_STATE, dtype=f32)
    lam_re = -0.5 + 0.01 * jax.random.normal(ks[4], (DEPTH, SSM_GROUPS, SSM_STATE), f32)
    lam_im = math.pi * n_idx + 0.01 * jax.random.normal(ks[5], (DEPTH, SSM_GROUPS, SSM_STATE), f32)
    log_dt = jax.random.uniform(ks[6], (DEPTH, SSM_GROUPS), f32, math.log(DT_MIN), math.log(DT_MAX))
    b_scale = (2.0 * SSM_GROUP) ** -0.5
    b_re = jax.random.normal(ks[7], (DEPTH, SSM_GROUPS, SSM_STATE, SSM_GROUP), f32) * b_scale
    b_im = jax.random.normal(ks[8], (DEPTH, SSM_GROUPS, SSM_STATE, SSM_GROUP), f32) * b_scale
    c_scale = (2.0 * SSM_STATE) ** -0.5
    c_re = jax.random.normal(ks[9], (DEPTH, SSM_GROUPS, SSM_GROUP, SSM_STATE), f32) * c_scale
    c_im = jax.random.normal(ks[10], (DEPTH, SSM_GROUPS, SSM_GROUP, SSM_STATE), f32) * c_scale
    d_skip = jax.random.normal(ks[11], (DEPTH, SSM_WIDTH), f32)
    w_glu = jax.random.normal(ks[12], (DEPTH, SSM_WIDTH, SSM_WIDTH), f32) * SSM_WIDTH ** -0.5
    q_norm_w = 1.0 + 0.02 * jax.random.normal(ks[13], (DEPTH, N_DIL, HEAD_DIM), f32)
    k_norm_w = 1.0 + 0.02 * jax.random.normal(ks[14], (DEPTH, N_DIL, HEAD_DIM), f32)
    w_ssm_out = jax.random.normal(ks[15], (DEPTH, SSM_WIDTH, D_MODEL), f32) * SSM_WIDTH ** -0.5
    w_attn_out = jax.random.normal(ks[16], (DEPTH, ATTN_WIDTH, D_MODEL), f32) * ATTN_WIDTH ** -0.5
    w_o = jax.random.normal(ks[17], (DEPTH, D_MODEL, D_MODEL), f32) * D_MODEL ** -0.5
    return {"x": x, "positions": positions, "norm_w": norm_w, "w_in": w_in,
            "lam_re": lam_re, "lam_im": lam_im, "log_dt": log_dt,
            "b_re": b_re, "b_im": b_im, "c_re": c_re, "c_im": c_im,
            "d_skip": d_skip, "w_glu": w_glu, "q_norm_w": q_norm_w, "k_norm_w": k_norm_w,
            "w_ssm_out": w_ssm_out, "w_attn_out": w_attn_out, "w_o": w_o}

def first_block(x, positions, norm_w, w_in, lam_re, lam_im, log_dt, b_re, b_im, c_re, c_im,
              d_skip, w_glu, q_norm_w, k_norm_w, w_ssm_out, w_attn_out, w_o):
    f32 = jnp.float32
    bsz, length, _ = x.shape
    offsets = np.cumsum(SPLITS)[:-1].tolist()
    for layer in range(DEPTH):
        h = rms_norm(x, norm_w[layer])
        proj = h @ w_in[layer].astype(f32)
        u_s, z_s, q, k, v, z_a, r_s, r_a = jnp.split(proj, offsets, axis=-1)

        y_s = s5_branch(u_s, lam_re[layer], lam_im[layer], log_dt[layer], b_re[layer], b_im[layer],
                        c_re[layer], c_im[layer], d_skip[layer], w_glu[layer])
        y_s = (y_s * jax.nn.silu(z_s)) @ w_ssm_out[layer].astype(f32)

        head_shape = (bsz, length, N_DIL, HEADS_PER_GROUP, HEAD_DIM)
        q = rms_norm(q.reshape(head_shape), q_norm_w[layer][None, None, :, None, :])
        k = rms_norm(k.reshape(head_shape), k_norm_w[layer][None, None, :, None, :])
        v = v.reshape(head_shape)
        q = apply_partial_rope(q, positions)
        k = apply_partial_rope(k, positions)
        y_a = dilated_attention(q, k, v)
        y_a = (y_a * jax.nn.silu(z_a)) @ w_attn_out[layer].astype(f32)

        m = jax.nn.sigmoid(r_s) * y_s + jax.nn.sigmoid(r_a) * y_a
        x = (x.astype(f32) + m @ w_o[layer].astype(f32)).astype(x.dtype)
    return x


DEPTH_2 = 2

ROPE_BASE = 10000.0
NORM_EPS = 1e-6
MLA_HEADS = D_MODEL // 128
MLA_QK_NOPE = 128
MLA_QK_ROPE = 64
MLA_V_DIM = 128
MLA_Q_LORA = 3 * D_MODEL // 8
MLA_KV_LORA = D_MODEL // 8
ATTN_Q_BLOCK = 128
POOL_WINDOWS = (2, 4, 8, 16)
POOL_GROUPS = len(POOL_WINDOWS)
POOL_GROUP_DIM = D_MODEL // POOL_GROUPS
MIX_A = MLA_HEADS * MLA_V_DIM
MIX_B = POOL_GROUPS * POOL_GROUP_DIM
EVEN_MIX = MIX_A + MIX_B
EVEN_SPLITS = (MLA_Q_LORA, MLA_Q_LORA + MLA_KV_LORA, MLA_Q_LORA + MLA_KV_LORA + MLA_QK_ROPE,
               MLA_Q_LORA + MLA_KV_LORA + MLA_QK_ROPE + MIX_B)
EVEN_IN = EVEN_SPLITS[-1] + EVEN_MIX
RET_HEADS = D_MODEL // 256
RET_DK = 256
RET_DV = 512
RET_CHUNK = 128
RET_QK = RET_HEADS * RET_DK
RET_V = RET_HEADS * RET_DV
ODD_IN = 2 * RET_QK + 2 * RET_V
N_EVEN = (DEPTH_2 + 1) // 2
N_ODD = DEPTH_2 // 2


def rms_norm_2(x, g):
    xf = x.astype(jnp.float32)
    y = xf * lax.rsqrt(jnp.mean(xf * xf, axis=-1, keepdims=True) + NORM_EPS)
    return (y * g.astype(jnp.float32)).astype(x.dtype)

def rope_tables(positions, dim):
    inv = 1.0 / (ROPE_BASE ** (jnp.arange(0, dim, 2, dtype=jnp.float32) / dim))
    ang = positions.astype(jnp.float32)[..., None] * inv
    return jnp.cos(ang)[:, :, None, :], jnp.sin(ang)[:, :, None, :]

def apply_rope(x, cos, sin):
    half = x.shape[-1] // 2
    xf = x.astype(jnp.float32)
    x1, x2 = xf[..., :half], xf[..., half:]
    return jnp.concatenate([x1 * cos - x2 * sin, x2 * cos + x1 * sin], axis=-1).astype(x.dtype)

def mla(cq, ckv, kr, cos, sin, q_norm_g, w_uq, kv_norm_g, w_ukv):
    B_, T, _ = cq.shape
    dqk = MLA_QK_NOPE + MLA_QK_ROPE
    q = (rms_norm_2(cq, q_norm_g) @ w_uq).reshape(B_, T, MLA_HEADS, dqk)
    q = jnp.concatenate([q[..., :MLA_QK_NOPE], apply_rope(q[..., MLA_QK_NOPE:], cos, sin)], axis=-1)
    kv = (rms_norm_2(ckv, kv_norm_g) @ w_ukv).reshape(B_, T, MLA_HEADS, MLA_QK_NOPE + MLA_V_DIM)
    k_rope = apply_rope(kr[:, :, None, :], cos, sin)
    k = jnp.concatenate([kv[..., :MLA_QK_NOPE],
                         jnp.broadcast_to(k_rope, (B_, T, MLA_HEADS, MLA_QK_ROPE))], axis=-1)
    v = kv[..., MLA_QK_NOPE:]
    nb = T // ATTN_Q_BLOCK
    qb = q.reshape(B_, nb, ATTN_Q_BLOCK, MLA_HEADS, dqk).transpose(1, 0, 2, 3, 4)
    scale = dqk ** -0.5

    def attend(q_blk):
        s = jnp.einsum('bqhd,bkhd->bhqk', q_blk, k, preferred_element_type=jnp.float32) * scale
        p = jax.nn.softmax(s, axis=-1).astype(v.dtype)
        return jnp.einsum('bhqk,bkhd->bqhd', p, v)

    o = lax.map(attend, qb)
    return o.transpose(1, 0, 2, 3, 4).reshape(B_, T, MIX_A)

def multiscale_pool(u, pool_w, pool_scale):
    B_, T, _ = u.shape
    uf = u.reshape(B_, T, POOL_GROUPS, POOL_GROUP_DIM).astype(jnp.float32)
    cs = jnp.concatenate([jnp.zeros_like(uf[:, :1]), jnp.cumsum(uf, axis=1)], axis=1)
    t = jnp.arange(T)
    outs = []
    for g, w in enumerate(POOL_WINDOWS):
        left = w // 2
        right = w - 1 - left
        lo = jnp.clip(t - left, 0, T - 1)
        hi = jnp.clip(t + right, 0, T - 1)
        csg = cs[:, :, g]
        s = jnp.take(csg, hi + 1, axis=1) - jnp.take(csg, lo, axis=1)
        cnt = (hi - lo + 1).astype(jnp.float32)
        outs.append(s / cnt[None, :, None] - uf[:, :, g])
    d = jnp.stack(outs, axis=2).astype(u.dtype)
    y = jnp.einsum('btgc,gcd->btgd', d, pool_w) * pool_scale.reshape(POOL_GROUPS, POOL_GROUP_DIM)
    return y.reshape(B_, T, MIX_B)

def hybrid_attn_pool_layer(x, cos_a, sin_a, norm_g, w_in, q_norm_g, w_uq, kv_norm_g, w_ukv,
                           pool_w, pool_scale, w_out):
    h = rms_norm_2(x, norm_g)
    proj = h @ w_in
    cq, ckv, kr, u, gate = jnp.split(proj, list(EVEN_SPLITS), axis=-1)
    a = mla(cq, ckv, kr, cos_a, sin_a, q_norm_g, w_uq, kv_norm_g, w_ukv)
    b = multiscale_pool(u, pool_w, pool_scale)
    y = jnp.concatenate([a, b], axis=-1) * jax.nn.silu(gate)
    return y @ w_out

def retention_chunkwise(q, k, v, log_g, include_diag):
    B_, T, H, dk = q.shape
    dv = v.shape[-1]
    C = RET_CHUNK
    N = T // C
    to_chunks = lambda a: a.reshape(B_, N, C, H, a.shape[-1]).transpose(1, 0, 3, 2, 4)
    qc, kc, vc = to_chunks(q), to_chunks(k), to_chunks(v)
    idx = jnp.arange(C).astype(jnp.float32)
    diff = idx[:, None] - idx[None, :]
    mask = (diff >= 0) if include_diag else (diff > 0)
    dmat = jnp.where(mask[None], jnp.exp(jnp.where(mask, diff, 0.0)[None] * log_g[:, None, None]), 0.0)
    xi = jnp.exp((idx + 1.0)[None, :] * log_g[:, None])[None, :, :, None]
    zeta = jnp.exp((C - 1.0 - idx)[None, :] * log_g[:, None])[None, :, :, None]
    chunk_decay = jnp.exp(C * log_g)[None, :, None, None]

    def step(state, inp):
        q_i, k_i, v_i = inp
        scores = jnp.einsum('bhid,bhjd->bhij', q_i, k_i) * dmat
        o_in = jnp.einsum('bhij,bhjv->bhiv', scores, v_i)
        o_cross = jnp.einsum('bhid,bhdv->bhiv', q_i, state) * xi
        state = state * chunk_decay + jnp.einsum('bhjd,bhjv->bhdv', k_i * zeta, v_i)
        return state, o_in + o_cross

    s0 = jnp.zeros((B_, H, dk, dv), jnp.float32)
    _, o = lax.scan(step, s0, (qc, kc, vc))
    return o.transpose(1, 0, 3, 2, 4).reshape(B_, T, H, dv)

def retention_layer(x, cos_r, sin_r, norm_g, w_in, decay_fwd, decay_bwd, gn_g, w_out):
    B_, T, _ = x.shape
    h = rms_norm_2(x, norm_g)
    proj = h @ w_in
    q, k, v, gate = jnp.split(proj, [RET_QK, 2 * RET_QK, 2 * RET_QK + RET_V], axis=-1)
    q = apply_rope(q.reshape(B_, T, RET_HEADS, RET_DK), cos_r, sin_r).astype(jnp.float32)
    k = apply_rope(k.reshape(B_, T, RET_HEADS, RET_DK), cos_r, sin_r).astype(jnp.float32) * (RET_DK ** -0.5)
    v = v.reshape(B_, T, RET_HEADS, RET_DV).astype(jnp.float32)
    lf = jax.nn.log_sigmoid(decay_fwd.astype(jnp.float32))
    lb = jax.nn.log_sigmoid(decay_bwd.astype(jnp.float32))
    o_f = retention_chunkwise(q, k, v, lf, True)
    o_b = jnp.flip(retention_chunkwise(jnp.flip(q, 1), jnp.flip(k, 1), jnp.flip(v, 1), lb, False), 1)
    o = o_f + o_b
    mu = jnp.mean(o, axis=-1, keepdims=True)
    var = jnp.mean(jnp.square(o - mu), axis=-1, keepdims=True)
    o = ((o - mu) * lax.rsqrt(var + NORM_EPS)).reshape(B_, T, RET_V) * gn_g.astype(jnp.float32)
    y = o.astype(x.dtype) * jax.nn.silu(gate)
    return y @ w_out

def second_inputs(seed: int = 0) -> dict:
    key = jax.random.key(seed)
    ks = jax.random.split(key, 24)
    f32 = jnp.float32
    nrm = lambda k, shape, scale: jax.random.normal(k, shape, f32) * scale
    gain = lambda k, shape: 1.0 + 0.05 * jax.random.normal(k, shape, f32)
    x = jax.random.normal(ks[0], (BATCH, SEQ, D_MODEL), f32)
    positions = (jnp.arange(SEQ, dtype=jnp.int32)[None, :]
                 + jax.random.randint(ks[1], (BATCH, 1), 0, 4096, dtype=jnp.int32))
    base_decay = jnp.log(2.0 ** (5.0 + jnp.arange(RET_HEADS, dtype=f32)) - 1.0)
    return {
        'x': x,
        'positions': positions,
        'a_norm_g': gain(ks[2], (N_EVEN, D_MODEL)),
        'a_w_in': nrm(ks[3], (N_EVEN, D_MODEL, EVEN_IN), D_MODEL ** -0.5),
        'a_q_norm_g': gain(ks[4], (N_EVEN, MLA_Q_LORA)),
        'a_w_uq': nrm(ks[5], (N_EVEN, MLA_Q_LORA, MLA_HEADS * (MLA_QK_NOPE + MLA_QK_ROPE)), MLA_Q_LORA ** -0.5),
        'a_kv_norm_g': gain(ks[6], (N_EVEN, MLA_KV_LORA)),
        'a_w_ukv': nrm(ks[7], (N_EVEN, MLA_KV_LORA, MLA_HEADS * (MLA_QK_NOPE + MLA_V_DIM)), MLA_KV_LORA ** -0.5),
        'a_pool_w': nrm(ks[8], (N_EVEN, POOL_GROUPS, POOL_GROUP_DIM, POOL_GROUP_DIM), POOL_GROUP_DIM ** -0.5),
        'a_pool_scale': 1.0 + 0.1 * jax.random.normal(ks[9], (N_EVEN, MIX_B), f32),
        'a_w_out': nrm(ks[10], (N_EVEN, EVEN_MIX, D_MODEL), EVEN_MIX ** -0.5),
        'r_norm_g': gain(ks[11], (N_ODD, D_MODEL)),
        'r_w_in': nrm(ks[12], (N_ODD, D_MODEL, ODD_IN), D_MODEL ** -0.5),
        'r_decay_fwd': base_decay[None, :] + 0.1 * jax.random.normal(ks[13], (N_ODD, RET_HEADS), f32),
        'r_decay_bwd': base_decay[None, :] + 0.1 * jax.random.normal(ks[14], (N_ODD, RET_HEADS), f32),
        'r_gn_g': gain(ks[15], (N_ODD, RET_V)),
        'r_w_out': nrm(ks[16], (N_ODD, RET_V, D_MODEL), RET_V ** -0.5),
        'final_norm_g': gain(ks[17], (D_MODEL,)),
    }

def second_block(x, positions, a_norm_g, a_w_in, a_q_norm_g, a_w_uq, a_kv_norm_g, a_w_ukv,
              a_pool_w, a_pool_scale, a_w_out, r_norm_g, r_w_in, r_decay_fwd, r_decay_bwd,
              r_gn_g, r_w_out, final_norm_g):
    cos_a, sin_a = rope_tables(positions, MLA_QK_ROPE)
    cos_r, sin_r = rope_tables(positions, RET_DK)
    for layer in range(DEPTH_2):
        i = layer // 2
        if layer % 2 == 0:
            x = x + hybrid_attn_pool_layer(x, cos_a, sin_a, a_norm_g[i], a_w_in[i], a_q_norm_g[i],
                                           a_w_uq[i], a_kv_norm_g[i], a_w_ukv[i], a_pool_w[i],
                                           a_pool_scale[i], a_w_out[i])
        else:
            x = x + retention_layer(x, cos_r, sin_r, r_norm_g[i], r_w_in[i], r_decay_fwd[i],
                                    r_decay_bwd[i], r_gn_g[i], r_w_out[i])
    return rms_norm_2(x, final_norm_g)


def setup_inputs(seed=0):
    out = dict(first_inputs(seed))
    for name, value in second_inputs(seed + 1).items():
        if name != "x":
            out[name + "_2"] = value
    return out


def reference(
    x, positions, norm_w, w_in, lam_re, lam_im, log_dt, b_re, b_im, c_re, c_im, d_skip, w_glu,
    q_norm_w, k_norm_w, w_ssm_out, w_attn_out, w_o, positions_2, a_norm_g_2, a_w_in_2,
    a_q_norm_g_2, a_w_uq_2, a_kv_norm_g_2, a_w_ukv_2, a_pool_w_2, a_pool_scale_2, a_w_out_2,
    r_norm_g_2, r_w_in_2, r_decay_fwd_2, r_decay_bwd_2, r_gn_g_2, r_w_out_2, final_norm_g_2,
):
    x = first_block(
        x, positions, norm_w, w_in, lam_re, lam_im, log_dt, b_re, b_im, c_re, c_im, d_skip,
        w_glu, q_norm_w, k_norm_w, w_ssm_out, w_attn_out, w_o,
    )
    return second_block(
        x, positions_2, a_norm_g_2, a_w_in_2, a_q_norm_g_2, a_w_uq_2, a_kv_norm_g_2, a_w_ukv_2,
        a_pool_w_2, a_pool_scale_2, a_w_out_2, r_norm_g_2, r_w_in_2, r_decay_fwd_2,
        r_decay_bwd_2, r_gn_g_2, r_w_out_2, final_norm_g_2,
    )


_drawn_inputs = setup_inputs


def setup_inputs(seed=0):
    import zlib

    import numpy as np

    out = dict(_drawn_inputs(seed))
    spreads = {}
    factors = {'norm_w': 8.0,
     'lam_re': 64.0,
     'lam_im': 48.336,
     'log_dt': 49.048,
     'b_re': 64.0,
     'b_im': 64.0,
     'c_re': 64.0,
     'c_im': 64.0,
     'q_norm_w': 8.0,
     'k_norm_w': 8.0,
     'a_q_norm_g_2': 8.0,
     'a_kv_norm_g_2': 8.0,
     'a_pool_w_2': 4.959,
     'a_pool_scale_2': 8.0,
     'r_norm_g_2': 8.0,
     'r_w_in_2': 3.059,
     'r_decay_fwd_2': 8.0,
     'r_decay_bwd_2': 8.0,
     'r_gn_g_2': 8.0,
     'r_w_out_2': 3.071}
    for name, (base, spread) in spreads.items():
        noise = np.random.default_rng([zlib.crc32(name.encode()), seed]).standard_normal(out[name].shape)
        drawn = base * np.exp(spread * noise) if base else spread * noise
        out[name] = __import__('jax').numpy.asarray(drawn.astype(out[name].dtype))
    for name, factor in factors.items():
        out[name] = (out[name] * factor).astype(out[name].dtype)
    return out
```

```python
import concourse.bass as bass
from concourse import mybir
from contextlib import ExitStack
import math
import numpy as np

f32 = mybir.dt.float32
ALU = mybir.AluOpType
ACT = mybir.ActivationFunctionType
AX = mybir.AxisListType

T, D, P = 512, 1024, 128
TT, KT = T // P, D // P
EPS = 1e-6
NEG = -1e30
ROUND = 12582912.0
PI2_A, PI2_B, PI2_C = 6.28125, 0.0019340515136718750, float(2 * math.pi - 6.28125 - 0.0019340515136718750)
TURN = float(np.float32(1.0 / (2 * math.pi)))
PI2_SAFE = 6.283185
PI_SAFE = 3.1415925
GROUPS, GCH, NST = 64, 16, 64
NTILE = GROUPS * NST // P
SPM = 4
PACKW = 512 + SPM * 96 + SPM
DIL = ((128, 1), (512, 4), (2048, 16))
HEADS, HD, NG = 8, 64, 3
NH = NG * HEADS
PH = NH // KT
PC = PH * HD
ROPE1 = 8
SCALE1 = 1.0 / math.sqrt(HD)
QL, KVL, MH, MN, MR, MV = 384, 128, 8, 128, 64, 128
SCALE2 = (MN + MR) ** -0.5
POOLS = (2, 4, 8, 16)
PAD = 8
RH, RK, RV = 4, 256, 512
DELTAS = T + 3 * P
LOOPW = KT * (P + 3 * PC)
PANEL = 2048

COLS = {}
def _cols():
    n = 0
    for name, w in (("norm_w", 8), ("d_skip", 8), ("a_norm", 8), ("q_norm", 3), ("kv_norm", 1), ("pool_scale", 8),
                    ("r_norm", 8), ("gn", 16)):
        COLS[name] = n
        n += w
    return n
NCOLS = _cols()


MLA_STEPS, RET_STEPS = 28, 36


class Steps:

    def __init__(self, eng, sem):
        self.eng, self.sem, self.n, self.i, self.per, self.start = eng, sem, 0, None, 0, 0

    def __call__(self, ins):
        ins.then_inc(self.sem, 1)
        self.n += 1
        return self.n

    def wait(self, tok=None):
        tok = self.n if tok is None else tok
        self.eng.wait_ge(self.sem, tok if self.i is None else self.i * self.per + tok)

    def loop(self, i, per):
        self.i, self.per, self.start = i, per, self.n

    def end(self, count):
        assert self.n - self.start == self.per, f"steps per turn: {self.n - self.start}, said {self.per}"
        self.n = self.start + count * self.per
        self.i = None


def stage_plan():
    plan = []
    for i in range(4):
        plan += [("glu", i), ("zs", i)]
    for i in range(4):
        plan += [("rs", i), ("so", i)]
    plan += [("za", 0), ("za", 1)]
    for i in range(4):
        plan += [("ra", i), ("ao", i)]
    plan += [("wo", i) for i in range(4)]
    plan += [("lo", i) for i in range(3)]
    for i in range(4):
        plan += [("pu", i), ("gb", i)]
    for i in range(4):
        plan += [("uq", i), ("ga", i)]
    for i in range(4):
        plan += [("oa", i), ("ob", i)]
    for h in range(RH):
        plan += [("rq", h), ("rk", h), ("rv", 2 * h), ("rv", 2 * h + 1), ("rg", 2 * h), ("rg", 2 * h + 1)]
    for i in range(4):
        plan += [("ta", i), ("tb", i)]
    return plan


def build(nc, a, out, upto=99):
    ctx = ExitStack()
    with ctx:
        A = ctx.enter_context(nc.sbuf_tensor("arena", [P, 53200], f32))
        ps = [ctx.enter_context(nc.psum_tensor(f"bank{b}", [P, 512], f32)) for b in range(8)]

        def sem(name):
            return ctx.enter_context(nc.semaphore(name))

        def at(off, *dims):
            n = int(np.prod(dims))
            v = A[:, off:off + n]
            if len(dims) == 1:
                return v
            names = [f"d{k}" for k in range(len(dims))]
            return v.rearrange(f"p ({' '.join(names)}) -> p {' '.join(names)}",
                               **{m: d for m, d in zip(names[1:], dims[1:])})

        W = 0
        wl = at(W, LOOPW)
        w_u = wl[:, 0:KT * P].rearrange("p (k c) -> p k c", k=KT)
        w_x = [wl[:, KT * P + x * KT * PC:KT * P + (x + 1) * KT * PC].rearrange("p (k c) -> p k c", k=KT)
               for x in range(3)]
        ring = at(W, 4, PANEL)
        o = LOOPW
        t_a = [at(o, 512), at(o + 512, 512)]; o += 1024
        u_cur = at(o, 512); o += 512
        qk_w = at(o, 2, PC); o += 2 * PC
        hT = at(8192, KT, T)
        QTOK, KTOK, VTOK, GT = 12288, 18432, 24576, 30720
        qkv_tok = [at(b, TT, NH * HD) for b in (QTOK, KTOK, VTOK)]
        gT = at(GT, KT, T)
        pack = at(34816, KT, PACKW)
        lhs_cur = at(42016, 4, P)
        E = at(42528, 2, 2, 512)
        e_t = [at(44576, 512), at(45088, 512)]
        bp = at(45600, 2, 512)
        gs = at(46624, 2, 512)
        hs = at(47648, 2, 2, 512)
        sq = at(49696, TT * PH, HD)
        y_sb = at(50464, 512)
        CB = 52300
        ident = at(CB, P)
        cols = at(CB + 128, 64)
        csA = at(CB + 192, 2, TT, ROPE1)
        rt = [at(CB + 256 + 96 * k, TT, PH, ROPE1) for k in range(4)]
        st = at(CB + 640, 160)
        half_m = st[:, 0:16]

        def col(name, k=0):
            return cols[:, COLS[name] + k:COLS[name] + k + 1]

        const_in = sem("const_in"); x_in = [sem(f"x_in{t}") for t in range(TT)]; ssm_in = sem("ssm_in")
        v_step = sem("v_step"); a_step = sem("a_step"); g_step = sem("g_step")
        x_sq = sem("x_sq"); x_ms = sem("x_ms"); x_rs = sem("x_rs"); x_nrm = sem("x_nrm")
        xt_mm = sem("xt_mm"); xt_ev = sem("xt_ev")
        ang_in = sem("ang_in"); trig_ready = sem("trig_ready"); ssm_exp = sem("ssm_exp"); ssm_dt = sem("ssm_dt")
        bb_ready = sem("bb_ready"); bt_mm = sem("bt_mm"); pack_ready = sem("pack_ready")
        wu_full = sem("wu_full"); wq_full = sem("wq_full"); wk_full = sem("wk_full"); wv_full = sem("wv_full")
        qkw_full = sem("qkw_full")
        u_mm = sem("u_mm"); q_mm = sem("q_mm"); k_mm = sem("k_mm"); v_mm = sem("v_mm")
        u_ev = sem("u_ev"); q_ev = sem("q_ev"); k_ev = sem("k_ev"); v_ev = sem("v_ev"); lhs_ready = sem("lhs_ready")
        bu_mm = sem("bu_mm"); bu_used = sem("bu_used"); c_mm = sem("c_mm"); h_ready = sem("h_ready")
        e_ready = sem("e_ready"); e_used = sem("e_used"); y_ready = sem("y_ready"); gelu_done = sem("gelu_done")
        ss_done = sem("ss_done"); ms_ready = sem("ms_ready"); rs_ready = sem("rs_ready"); scaled = sem("scaled")
        roped = sem("roped")
        w_full = [sem(f"w_full{s}") for s in range(4)]
        panel_mm = sem("panel_mm"); step_free = sem("step_free")
        mask_in = sem("mask_in"); g_ready = sem("g_ready")
        qg_ready = sem("qg_ready"); tr_mm = sem("tr_mm"); tr_ev = sem("tr_ev"); sc_mm = sem("sc_mm")
        sm_done = sem("sm_done"); nm_ready = sem("nm_ready"); p_ready = sem("p_ready"); pt_mm = sem("pt_mm")
        pt_ev = sem("pt_ev"); pv_mm = sem("pv_mm"); o_ev = sem("o_ev")
        glu_sig = sem("glu_sig"); sig_used = sem("sig_used"); ys_ready = sem("ys_ready"); m_ready = sem("m_ready")
        rs_sig = sem("rs_sig"); ot_mm = sem("ot_mm"); za_sig = sem("za_sig"); ya_ready = sem("ya_ready")
        ra_sig = sem("ra_sig"); xr_in = sem("xr_in"); x1_ready = sem("x1_ready")
        out_done = sem("out_done"); passed = sem("passed")

        plan = stage_plan()
        NP = len(plan)
        first_of = {}
        for n, (kind, i) in enumerate(plan):
            first_of.setdefault(kind, n)

        x_tok, xn_tok = at(QTOK, TT, D), at(KTOK, TT, D)
        ssp = at(49696, 24, 32)
        lr, li, ldt = ssp[:, 0, :], ssp[:, 1, :], ssp[:, 2, :]
        tv = at(50464, 48)
        b_nat = at(GT, 2, NTILE, 32)
        bbs = at(GT + 2048, 2, NTILE, 32)
        bt_tmp = at(44576, NTILE, 32)
        tw = [at(VTOK + 1536 * k, NTILE, 48) for k in range(4)]
        angA = at(46624, 4, TT, ROPE1)

        masks = at(34816, 1280)
        qg = at(36096, 6, TT, P)
        qkT = at(39168, 6, T)
        sm = at(42240, 2, 1280)
        pr = at(44800, 2, 1280)
        pT = at(47360, 10, P)
        o_tok = at(48640, TT, HEADS * HD)
        mx = at(50688, 2); nmx = at(50692, 2); den = at(50696, 2); rden = at(50700, 2)
        yT = at(QTOK, KT, T)
        mT = at(KTOK, KT, T)
        sig = at(34816, 2, 4, T)
        prod = at(38912, 4, T)
        oT = at(VTOK, 4, T)
        x_res = at(30720, TT, D)

        xn2 = at(12288, TT, D)
        upad = at(12288, 2, 2, T + 2 * PAD)
        win = at(14400, 2, 2, T + 2 * PAD)
        l_tok = at(16512, TT, QL + KVL)
        kr_tok = at(18560, TT, P)
        cT = at(19072, 4, T)
        krT = at(21120, T)
        y2T = at(21632, 16, T)
        delta = at(29824, DELTAS)
        cosT, sinT = at(41984, 1152), at(43136, 1152)
        ang, turns = at(44288, 1152), at(45440, 1152)
        cosR, sinR = cosT[:, 0:512], sinT[:, 0:512]
        cosM, sinM = cosT[:, 512:1024], sinT[:, 512:1024]
        cosK = cosT[:, 1024:1152].rearrange("p (t c) -> p t c", t=TT)
        sinK = sinT[:, 1024:1152].rearrange("p (t c) -> p t c", t=TT)
        pool_d = at(44288, 2, 2, T)
        decay = at(46592, RH, DELTAS)
        pool_w = at(50176, 4, 2, 256)
        MB = CB + 256
        corr = at(MB, 4, 16)
        inv_cols = at(MB + 64, 3)
        inv_row = at(MB + 67, 32)
        pos2c = at(MB + 99, TT)
        dec = at(MB + 103, 8)
        lsg = at(MB + 111, 6, 8)
        pos2i = at(MB + 160, TT)
        st2 = at(MB + 164, 160)
        qnT, qrT, knT = at(12288, 2, T), at(13312, T), at(13824, 2, T)
        v_m = at(14848, TT, 256)
        p_m = at(15872, 3, T)
        rot = at(17408, 2, T)
        pT_m = at(34816, 2, 4, T)
        gate_m, sig_m = at(38912, 2, T), at(39936, 2, T)
        q_r, k_r = at(12288, 2, T), at(13312, 2, T)
        v_r = at(14336, TT, RV)
        sd = at(16384, TT, T)
        on = at(18432, TT, RV)
        gate_r, sig_r = at(34816, 4, T), at(36864, 4, T)
        rot_r = at(38912, 4, T)
        dt1, dt2 = at(34816, DELTAS), at(34816 + DELTAS, DELTAS)
        gain = at(12288, D)
        squares = at(14336, TT, D)

        misc_in = sem("misc_in"); pos_in = sem("pos_in"); ang2 = sem("ang2"); trig2 = sem("trig2"); tab2 = sem("tab2")
        n_sq = sem("n_sq"); n_ms = sem("n_ms"); n_rs = sem("n_rs"); n_nrm = sem("n_nrm"); nt_mm = sem("nt_mm")
        nt_ev = sem("nt_ev"); lo_sq = sem("lo_sq"); lo_ms = sem("lo_ms"); lo_rs = sem("lo_rs"); lo_ev = sem("lo_ev")
        kr_raw = sem("kr_raw"); kr_rot = sem("kr_rot"); ct_mm = sem("ct_mm"); ct_ev = sem("ct_ev")
        poolw_in = sem("poolw_in"); u_pad = sem("u_pad"); pads = sem("pads"); d_ready = sem("d_ready"); pool_mm = sem("pool_mm")
        gb_sig = sem("gb_sig"); y2_ready = sem("y2_ready")
        pr_mm = sem("pr_mm"); pr_ev = sem("pr_ev"); rot_done = sem("rot_done"); ga_mm = sem("ga_mm"); ga_sig = sem("ga_sig")
        ga_ready = sem("ga_ready"); s_mm = sem("s_mm"); nmax = sem("nmax"); e_done = sem("e_done"); rcp = sem("rcp")
        p_norm = sem("p_norm"); t_mm = sem("t_mm"); t_ev = sem("t_ev"); o_mm = sem("o_mm"); ym_ready = sem("ym_ready")
        delta_in = sem("delta_in"); dec_abs = sem("dec_abs"); dec_exp = sem("dec_exp"); dec_arg = sem("dec_arg")
        dec_ready = sem("dec_ready"); dec_in = sem("dec_in")
        x2_ready = sem("x2_ready"); rp_mm = sem("rp_mm"); rqk_rot = sem("rqk_rot"); v_cp = sem("v_cp"); rs_mm = sem("rs_mm")
        sd_ready = sem("sd_ready"); rg_mm = sem("rg_mm"); rg_sig = sem("rg_sig"); rg_ready = sem("rg_ready")
        ro_mm = sem("ro_mm"); var_ready = sem("var_ready"); rstd = sem("rstd"); on_ready = sem("on_ready")
        rt_mm = sem("rt_mm"); yr_ready = sem("yr_ready"); x3_ready = sem("x3_ready"); gain_in = sem("gain_in")
        f_nrm = sem("f_nrm"); f_out = sem("f_out")
        BLK1 = 30
        PU, UQ, OA, RQ, TA = (first_of[k] for k in ("pu", "uq", "oa", "rq", "ta"))

        NKEY = [min(i + 1, 2) + 2 * (i + 1) for i in range(TT)]
        CH = [(n + 3) // 4 for n in NKEY]
        CHU = [CH[u % 4] for u in range(8)]

        def key_blocks(i):
            return [(0, b) for b in range(max(i - 1, 0), i + 1)] + [(1, b) for b in range(i + 1)] + \
                   [(2, b) for b in range(i + 1)]

        def apart(eng):
            eng.sem_inc(passed, 1)

        block = ctx.enter_context(nc.Block())

        @block.sync
        def _(sp):
            sp.dma_start(ssp[:, 0:3, :], a["ssm_par"]).then_inc(ssm_in, 16)
            sp.dma_start(tv, a["c_t"]).then_inc(ssm_in, 16)
            sp.dma_start(ident, a["c_ident"]).then_inc(const_in, 16)
            sp.dma_start(cols, a["cols"]).then_inc(const_in, 16)
            sp.dma_start(angA[:, 0], a["c_angA"]).then_inc(const_in, 16)
            sp.dma_start(st[:, 20:24].bitcast(mybir.dt.int32), a["pos1"]).then_inc(const_in, 16)
            sp.dma_start(b_nat, a["ssm_b"]).then_inc(ssm_in, 16)
            sp.dma_start(pack[:, :, 256:512], a["ssm_c"]).then_inc(ssm_in, 16)
            def turn(i):
                src = a["loop_w"][bass.ds(i, 1), :, :].rearrange("o p n -> (o p) n")
                for x, (full, done) in enumerate(((wq_full, q_mm), (wk_full, k_mm), (wv_full, v_mm))):
                    sp.wait_ge(done, i * 2 + 1)
                    b = KT * P + x * KT * PC
                    sp.dma_start(wl[:, b:b + KT * PC], src[:, b:b + KT * PC]).then_inc(full, 16)
                sp.wait_ge(scaled, i * 2 + 1)
                sp.dma_start(qk_w, a["qk_w"][bass.ds(i, 1)].rearrange("o x c -> o (x c)").to_broadcast([P, 2 * PC])
                             ).then_inc(qkw_full, 16)

            sp.dma_start(wl[:, 0:KT * P], a["loop_w"][0, :, 0:KT * P]).then_inc(wu_full, 16)
            with sp.Fori(0, KT - 1) as i:
                turn(i)
                sp.wait_ge(u_mm, i + 2)
                sp.dma_start(wl[:, 0:KT * P], a["loop_w"][bass.ds(i + 1, 1), :, 0:KT * P].rearrange("o p n -> (o p) n")
                             ).then_inc(wu_full, 16)
            turn(KT - 1)
            sp.wait_ge(gelu_done, KT + 1)
            sp.dma_start(masks, a["c_masks"]).then_inc(mask_in, 16)
            sp.wait_ge(v_mm, 2 * KT + 1)
            for n in range(NP):
                if upto == 1 and n == BLK1 or upto == 2 and n == RQ:
                    break
                if n >= 4 and not RQ <= n < TA:
                    sp.wait_ge(panel_mm, n - 3)
                if n == 2:
                    sp.wait_ge(scaled, 2 * KT + 1)
                if plan[n] == ("wo", 0):
                    sp.wait_ge(ys_ready, 8)
                    sp.dma_start(x_res, a["x"].rearrange("o (t p) d -> p (o t) d", p=P)).then_inc(xr_in, 16)
                if n == first_of["ra"]:
                    sp.wait_ge(ya_ready, 4)
                    mi = a["c_misc"]
                    sp.dma_start(at(MB, 99), mi).then_inc(misc_in, 16)
                    sp.dma_start(pos2i.bitcast(mybir.dt.int32), a["pos2"]).then_inc(misc_in, 16)
                    sp.dma_start(dec, a["decays"].to_broadcast([P, 8])).then_inc(dec_in, 16)
                    sp.dma_start(turns[:, 0:T].bitcast(mybir.dt.int32), a["positions_2"].to_broadcast([P, T])).then_inc(pos_in, 16)
                    sp.dma_start(pool_w, a["pool_w"]).then_inc(poolw_in, 16)
                if n == BLK1:
                    sp.dma_start(delta, a["c_delta"]).then_inc(delta_in, 16)
                if n == RQ:
                    with sp.Fori(0, 2) as r:
                        for k in range(12):
                            sp.wait_ge(panel_mm, r * 12 + (RQ + k - 3))
                            sp.dma_start(ring[:, (RQ + k) % 4, :], a["panels"][bass.ds(r * 12 + (RQ + k), 1), :, :]
                                         .rearrange("o p n -> (o p) n")).then_inc(w_full[(RQ + k) % 4], 16)
                if RQ <= n < TA:
                    continue
                w = {"ao": 1024, "lo": KT * 64 if plan[n][1] == 2 else PANEL}.get(plan[n][0], PANEL)
                sp.dma_start(ring[:, n % 4, 0:w], a["panels"][n, :, 0:w]).then_inc(w_full[n % 4], 16)
            if upto == 1:
                sp.wait_ge(x1_ready, 8)
                sp.dma_start(out.rearrange("o (t p) d -> p (o t) d", p=P), x_res).then_inc(out_done, 16)
                sp.wait_ge(out_done, 16)
                return
            if upto != 2:
                sp.wait_ge(ro_mm, 17)
                sp.wait_ge(rqk_rot, 8)
                sp.dma_start(gain, a["final_g"].to_broadcast([P, D])).then_inc(gain_in, 16)
            if upto == 2:
                sp.wait_ge(x2_ready, 16)
                sp.dma_start(out.rearrange("o (t p) d -> p (o t) d", p=P), x_res).then_inc(out_done, 16)
                sp.wait_ge(out_done, 16)
                return
            for t in range(TT):
                sp.wait_ge(f_out, t + 1)
                sp.dma_start(out[0, t * P:(t + 1) * P, :], x_res[:, t, :]).then_inc(out_done, 16)
            sp.wait_ge(out_done, 16 * TT)

        @block.tensor
        def _(pe):
            mm = nc.tensor.matmul
            for first in (u_mm, q_mm, k_mm, v_mm, c_mm, tr_mm, sc_mm, pt_mm, pv_mm, s_mm, t_mm, o_mm, ro_mm):
                pe.sem_inc(first, 1)
            pe.wait_ge(const_in, 64)
            for k in range(KT):
                if k == 0:
                    pe.wait_ge(x_nrm, TT)
                for t in range(TT):
                    last = nc.tensor.transpose(ps[k][:, t * P:(t + 1) * P], xn_tok[:, t, k * P:(k + 1) * P], ident)
                last.then_inc(xt_mm, 1)
            pe.wait_ge(bb_ready, 2)
            for m in range(KT):
                pe.wait_ge(xt_ev, m + 1)
                for c in range(2):
                    last = nc.tensor.transpose(ps[m][:, c * P:(c + 1) * P], bbs[:, c, 4 * m:4 * m + 4, :].rearrange("p a b -> p (a b)"), ident)
                last.then_inc(bt_mm, 1)
            pe.wait_ge(pack_ready, KT)

            def qkv(i, x, half, full, bank, done):
                if half == 0:
                    pe.wait_ge(full, i * 16 + 16)
                for t in (2 * half, 2 * half + 1):
                    for k in range(KT):
                        last = mm(ps[bank][:, (t % 2) * PC:(t % 2 + 1) * PC], hT[:, k, t * P:(t + 1) * P], w_x[x][:, k, :],
                                  start=(k == 0), stop=(k == KT - 1))
                last.then_inc(done, 1)

            def bu(i, j):
                if j == 0:
                    pe.wait_ge(u_ev, i + 1 + 1)
                    pe.wait_ge(lhs_ready, i + 1)
                pe.wait_ge(bu_used, i * 4 + j + 1)
                r = slice(32 * j, 32 * j + 32)
                for c in range(2):
                    last = mm(ps[5 + c][:, :], lhs_cur[r, c, :], u_cur[r, :], start=True, stop=True)
                last.then_inc(bu_mm, 1)

            def cy(i, j):
                pe.wait_ge(h_ready, i * 4 + (j + 1))
                if j == 0:
                    pe.wait_ge(y_ready, i + 1)
                for c in range(2):
                    last = mm(ps[7][32 * j:32 * j + 32, :], lhs_cur[:, 2 + c, 32 * j:32 * j + 32], hs[:, j % 2, c, :],
                              start=(c == 0), stop=(c == 1))
                last.then_inc(c_mm, 1)

            def channels(i):
                pe.wait_ge(wu_full, i * 16 + 16)
                pe.wait_ge(u_ev, i + 1)
                for k in range(KT):
                    last = mm(ps[0][:, :], w_u[:, k, :], hT[:, k, :], start=(k == 0), stop=(k == KT - 1))
                last.then_inc(u_mm, 1)

            def turn(i, more):
                pe.wait_ge(v_ev, i * 2 + 1)
                qkv(i, 0, 0, wq_full, 1, q_mm)
                bu(i, 0)
                qkv(i, 0, 1, wq_full, 2, q_mm)
                bu(i, 1)
                pe.wait_ge(k_ev, i * 2 + 1)
                qkv(i, 1, 0, wk_full, 3, k_mm)
                cy(i, 0)
                bu(i, 2)
                qkv(i, 1, 1, wk_full, 4, k_mm)
                cy(i, 1)
                bu(i, 3)
                pe.wait_ge(q_ev, i * 2 + 3)
                qkv(i, 2, 0, wv_full, 1, v_mm)
                cy(i, 2)
                qkv(i, 2, 1, wv_full, 2, v_mm)
                if more:
                    channels(i + 1)
                cy(i, 3)

            channels(0)
            with pe.Fori(0, KT - 1) as i:
                turn(i, True)
            turn(KT - 1, False)

            with pe.Fori(0, 4) as p:
                pe.wait_ge(qg_ready, p + 1)
                pe.wait_ge(o_ev, p * 8 + 1)
                for x in range(6):
                    if x >= 2:
                        pe.wait_ge(tr_ev, p * 6 + (x - 1))
                    for t in range(TT):
                        last = nc.tensor.transpose(ps[6 + x % 2][:, t * P:(t + 1) * P], qg[:, x, t, :], ident)
                    last.then_inc(tr_mm, 1)
                pe.wait_ge(tr_ev, p * 6 + 6)

                def scores(u):
                    hh, i = u // 4, u % 4
                    r = slice(64 * hh, 64 * hh + 64)
                    pe.wait_ge(sm_done, p * 8 + u + 1)
                    lo = max(i - 1, 0) * P
                    q = slice(i * P, (i + 1) * P)
                    mm(ps[0][:, 0:(i + 1) * P - lo], qkT[r, 0, q], qkT[r, 3, lo:(i + 1) * P], start=True, stop=True)
                    for g in (1, 2):
                        last = mm(ps[g][:, 0:(i + 1) * P], qkT[r, g, q], qkT[r, 3 + g, 0:(i + 1) * P], start=True, stop=True)
                    last.then_inc(sc_mm, 1)

                def probs_t(u):
                    pe.wait_ge(p_ready, p * 8 + (u + 2))
                    pe.wait_ge(pt_ev, p * sum(CHU) + sum(CHU[:u]) + 1)
                    n = NKEY[u % 4]
                    for c in range(CHU[u]):
                        for b in range(4 * c, min(4 * c + 4, n)):
                            last = nc.tensor.transpose(ps[3 + c][:, (b % 4) * P:(b % 4 + 1) * P],
                                                       pr[:, u % 2, b * P:(b + 1) * P], ident)
                        last.then_inc(pt_mm, 1)

                def pv(u):
                    hh, i = u // 4, u % 4
                    pe.wait_ge(pt_ev, p * sum(CHU) + sum(CHU[:u + 1]) + 1)
                    if u >= 2:
                        pe.wait_ge(o_ev, p * 8 + (u - 1) + 1)
                    blocks = key_blocks(i)
                    for b, (g, kt) in enumerate(blocks):
                        c0 = p * 128 + g * HEADS * HD
                        last = mm(ps[6 + u % 2][:, 0:P], pT[:, b, :], qkv_tok[2][:, kt, bass.ds(c0, P)],
                                  start=(b == 0), stop=(b == len(blocks) - 1))
                    last.then_inc(pv_mm, 1)

                scores(0)
                for u in range(8):
                    if u < 7:
                        scores(u + 1)
                    probs_t(u)
                    if u >= 1:
                        pv(u - 1)
                pv(7)

            def panel(n, bank0, x, tok=False):
                pe.wait_ge(w_full[n % 4], 16 * (n // 4 + 1))
                kind = plan[n][0]
                kts = 4 if kind == "ao" else 8
                w = ring[:, n % 4, 0:kts * 256].rearrange("p (k c) -> p k c", k=kts)
                if not tok:
                    for h in range(2):
                        for k in range(kts):
                            last = mm(ps[bank0 + h][:, :], w[:, k, h * P:(h + 1) * P], x[:, k, :],
                                      start=(k == 0), stop=(k == kts - 1))
                else:
                    for t in range(TT):
                        for k in range(kts):
                            last = mm(ps[bank0 + t // 2][:, (t % 2) * 256:(t % 2 + 1) * 256], x[:, k, t * P:(t + 1) * P],
                                      w[:, k, :], start=(k == 0), stop=(k == kts - 1))
                last.then_inc(panel_mm, 1)

            pe.wait_ge(o_ev, 33)
            pe.wait_ge(sm_done, 33)
            for s in range(15):
                b = 4 * (s % 2)
                pe.wait_ge(step_free, s + 1)
                if s < 4:
                    x = (gT, hT)
                elif s < 8:
                    x = (hT, yT)
                    pe.wait_ge(ys_ready, 8)
                elif s == 8:
                    x = (hT, hT)
                elif s < 13:
                    x = (hT, oT)
                else:
                    x = (mT, mT)
                    pe.wait_ge(m_ready, 16)
                if s == 9:
                    pe.wait_ge(ya_ready, 4)
                panel(2 * s, b, x[0], tok=s >= 13)
                panel(2 * s + 1, b + 2, x[1], tok=s >= 13)
                if s == 8:
                    pe.wait_ge(step_free, 10)
                    for c in range(4):
                        for t in range(TT):
                            last = nc.tensor.transpose(ps[4 + c][:, t * P:(t + 1) * P], o_tok[:, t, c * P:(c + 1) * P], ident)
                        last.then_inc(ot_mm, 1)

            if upto == 1:
                return

            def transposes(t0, x, evac, n0):
                pe.wait_ge(n_nrm, t0 + TT)
                for k in range(KT):
                    if n0:
                        pe.wait_ge(evac, n0 - KT + k + 1)
                    for t in range(TT):
                        last = nc.tensor.transpose(ps[k][:, t * P:(t + 1) * P], x[:, t, k * P:(k + 1) * P], ident)
                    last.then_inc(nt_mm, 1)
                pe.wait_ge(evac, n0 + KT)

            transposes(0, xn2, nt_ev, 0)

            def slot(n):
                pe.wait_ge(w_full[n % 4], 16 * (n // 4 + 1))
                return ring[:, n % 4, :]

            n = first_of["lo"]
            panel(n, 4, hT, tok=True)
            panel(n + 1, 6, hT, tok=True)
            w = slot(n + 2)[:, 0:KT * 64].rearrange("p (k c) -> p k c", k=KT)
            for t in range(TT):
                for k in range(KT):
                    last = mm(ps[0][:, t * 64:(t + 1) * 64], hT[:, k, t * P:(t + 1) * P], w[:, k, :],
                              start=(k == 0), stop=(k == KT - 1))
            last.then_inc(panel_mm, 1)

            def pool_product(i):
                b = 4 * (i % 2)
                pe.wait_ge(d_ready, i + 1)
                for c in range(2):
                    for k in range(2):
                        last = mm(ps[b + c][:, :], pool_w[:, i, k, c * P:(c + 1) * P], pool_d[:, i % 2, k, :],
                                  start=(k == 0), stop=(k == 1))
                last.then_inc(pool_mm, 1)

            pe.wait_ge(poolw_in, 16)
            for i in range(4):
                b = 4 * (i % 2)
                if i == 0:
                    pe.wait_ge(kr_raw, 1)
                if i == 1:
                    pe.wait_ge(lo_ev, 12)
                    for k in range(4):
                        for t in range(TT):
                            last = nc.tensor.transpose(ps[4 + k][:, t * P:(t + 1) * P], l_tok[:, t, k * P:(k + 1) * P], ident)
                        last.then_inc(ct_mm, 1)
                    pe.wait_ge(ct_ev, 1)
                    pe.wait_ge(kr_rot, 2)
                    for t in range(TT):
                        last = nc.tensor.transpose(ps[4][:, t * P:(t + 1) * P], kr_tok[:, t, :], ident)
                    last.then_inc(ct_mm, 1)
                    pe.wait_ge(ct_ev, 5)
                if i >= 2:
                    pe.wait_ge(step_free, 16 + i + 1)
                panel(PU + 2 * i, b, hT)
                panel(PU + 2 * i + 1, b + 2, hT)
                if i >= 1:
                    pool_product(i - 1)
            pool_product(3)

            with pe.Fori(0, 2) as r:
                for q in range(2):
                    def cnt(c, k):
                        return r * (2 * c) + (q * c + k)

                    n = UQ + 2 * q
                    if q == 0:
                        pe.wait_ge(step_free, 22)
                    pe.wait_ge(ym_ready, cnt(2, 0) + 1)
                    pe.wait_ge(t_ev, cnt(8, 0) + 1)
                    pe.wait_ge(w_full[n % 4], r * 16 + 16 * (n // 4 + 1))
                    w = ring[:, n % 4, 0:3 * 512].rearrange("p (k c) -> p k c", k=3)
                    wkv = ring[:, n % 4, 3 * 512:2048]
                    for c in range(4):
                        for k in range(3):
                            last = mm(ps[c][:, :], w[:, k, c * P:(c + 1) * P], cT[:, k, :], start=(k == 0), stop=(k == 2))
                        last.then_inc(pr_mm, 1)
                    for c in range(2):
                        pe.wait_ge(pr_ev, cnt(6, c + 1))
                        mm(ps[c][:, :], wkv[:, c * P:(c + 1) * P], cT[:, 3, :], start=True, stop=True).then_inc(pr_mm, 1)
                    pe.wait_ge(rot_done, cnt(1, 1))
                    for h in range(2):
                        for t in range(2 * h, 2 * h + 2):
                            last = mm(ps[2 + h][:, (t % 2) * 256:(t % 2 + 1) * 256], cT[:, 3, t * P:(t + 1) * P],
                                      wkv[:, 256:512], start=True, stop=True)
                        if h == 0:
                            last.then_inc(pr_mm, 1)
                    last.then_inc(panel_mm, 1)

                    def s_block(u):
                        h, i = u // 4, u % 4
                        if u < 3:
                            pe.wait_ge(e_done, cnt(8, 0) + 1)
                        else:
                            pe.wait_ge(e_done, cnt(8, u - 2) + 1)
                        b = 4 + u % 3
                        qs = slice(i * P, (i + 1) * P)
                        hr = slice(64 * h, 64 * h + 64)
                        mm(ps[b][:, :], qnT[:, h, qs], knT[:, h, :], start=True, stop=False)
                        mm(ps[b][:, :], qrT[hr, qs], krT[hr, :], start=False, stop=True).then_inc(s_mm, 1)

                    def t_block(u):
                        b = (7, 0)[u % 2]
                        pe.wait_ge(p_norm, cnt(8, u + 2))
                        if u >= 2:
                            pe.wait_ge(t_ev, cnt(8, u - 1) + 1)
                        for k in range(4):
                            last = nc.tensor.transpose(ps[b][:, k * P:(k + 1) * P], p_m[:, u % 3, k * P:(k + 1) * P], ident)
                        last.then_inc(t_mm, 1)

                    def o_block(h):
                        pe.wait_ge(t_ev, cnt(8, 4 * h + 4) + 1)
                        for k in range(4):
                            last = mm(ps[2 + h][:, :], v_m[:, k, h * P:(h + 1) * P], pT_m[:, h, k, :],
                                      start=(k == 0), stop=(k == 3))
                        last.then_inc(o_mm, 1)

                    pe.wait_ge(pr_ev, cnt(6, 4))
                    s_block(0)
                    s_block(1)
                    pe.wait_ge(w_full[(n + 1) % 4], r * 16 + 16 * ((n + 1) // 4 + 1))
                    w = ring[:, (n + 1) % 4, :].rearrange("p (k c) -> p k c", k=KT)
                    for c in range(2):
                        for k in range(KT):
                            last = mm(ps[c][:, :], w[:, k, c * P:(c + 1) * P], hT[:, k, :], start=(k == 0), stop=(k == KT - 1))
                    last.then_inc(panel_mm, 1)
                    s_block(2)
                    t_block(0)
                    pe.wait_ge(ga_ready, cnt(2, 1))
                    for u in range(1, 8):
                        if u < 6:
                            s_block(u + 2)
                        t_block(u)
                        if u == 5:
                            pe.wait_ge(pr_ev, cnt(6, 6))
                            o_block(0)
                    o_block(1)

            def residual(n, s, y, ready):
                b = 4 * (s % 2)
                pe.wait_ge(step_free, s + 1)
                for half in range(2):
                    w = slot(n + half).rearrange("p (k c) -> p k c", k=8)
                    for t in range(TT):
                        for k in range(8):
                            last = mm(ps[b + t][:, 0:256], y[:, 8 * half + k, t * P:(t + 1) * P], w[:, k, :],
                                      start=(half == 0 and k == 0), stop=(half == 1 and k == 7))
                    last.then_inc(panel_mm, 1)

            pe.wait_ge(ym_ready, 9)
            pe.wait_ge(y2_ready, 8)
            for i in range(4):
                residual(OA + 2 * i, 20 + i, y2T, None)
            if upto == 2:
                return

            transposes(TT, xn2, nt_ev, KT)
            with pe.Fori(0, 2) as r:
                for q in range(2):
                    def cnt(c, k):
                        return r * (2 * c) + (q * c + k)

                    def rpanel(x):
                        n = RQ + 6 * q + x
                        pe.wait_ge(w_full[n % 4], r * 48 + 16 * (n // 4 + 1))
                        return ring[:, n % 4, :].rearrange("p (k c) -> p k c", k=KT)

                    def feature(x, bank):
                        w = rpanel(x)
                        for c in range(2):
                            for k in range(KT):
                                last = mm(ps[bank + c][:, :], w[:, k, c * P:(c + 1) * P], hT[:, k, :],
                                          start=(k == 0), stop=(k == KT - 1))
                        last.then_inc(panel_mm, 1)

                    pe.wait_ge(on_ready, cnt(4, 0) + 1)
                    feature(0, 0)
                    pe.wait_ge(rg_ready, cnt(4, 0) + 1)
                    feature(1, 2)
                    pe.wait_ge(yr_ready, cnt(4, 0) + 1)
                    for x in range(2):
                        w = rpanel(2 + x)
                        for t in range(TT):
                            for k in range(KT):
                                last = mm(ps[4 + 2 * x + t // 2][:, (t % 2) * 256:(t % 2 + 1) * 256],
                                          hT[:, k, t * P:(t + 1) * P], w[:, k, :], start=(k == 0), stop=(k == KT - 1))
                        last.then_inc(panel_mm, 1)
                    pe.wait_ge(rqk_rot, cnt(2, 2))
                    for j in range(TT):
                        for k in range(2):
                            last = mm(ps[j][:, :], k_r[:, k, j * P:(j + 1) * P], q_r[:, k, :], start=(k == 0), stop=(k == 1))
                        last.then_inc(rs_mm, 1)
                    pe.wait_ge(v_cp, cnt(4, 2))
                    feature(4, 4)
                    pe.wait_ge(v_cp, cnt(4, 4))
                    pe.wait_ge(sd_ready, cnt(4, 4))
                    for i in range(TT):
                        b = (6, 7, 0, 1)[i]
                        for j in range(TT):
                            last = mm(ps[b][:, :], sd[:, j, i * P:(i + 1) * P], v_r[:, j, :], start=(j == 0), stop=(j == 3))
                        last.then_inc(ro_mm, 1)
                    feature(5, 2)
                    pe.wait_ge(rg_ready, cnt(4, 2) + 1)
                    for i in range(TT):
                        pe.wait_ge(on_ready, cnt(4, i + 2))
                        for c in range(4):
                            last = nc.tensor.transpose(ps[4 + i][:, c * P:(c + 1) * P], on[:, i, c * P:(c + 1) * P], ident)
                        last.then_inc(rt_mm, 1)

            pe.wait_ge(yr_ready, 17)
            for i in range(4):
                residual(TA + 2 * i, 24 + i, y2T, None)

        @block.scalar
        def _(act):
            S = Steps(act, a_step)
            for first in (u_ev, q_ev, k_ev, v_ev, gelu_done, p_ready, pt_ev, e_done, t_ev):
                act.sem_inc(first, 1)
            av = nc.scalar.activation
            for t in range(TT):
                act.dma_start(x_tok[:, t, :], a["x"][0, t * P:(t + 1) * P, :]).then_inc(x_in[t], 16)
            act.wait_ge(ssm_in, 64)
            av(ssp[:, 3, :], ldt, ACT.Exp).then_inc(ssm_exp, 1)
            act.wait_ge(ssm_dt, 1)
            av(ssp[:, 5, :], ssp[:, 4, :], ACT.Exp).then_inc(ssm_exp, 1)
            for t in range(TT):
                act.wait_ge(x_in[t], 16)
                av(xn_tok[:, t, :], x_tok[:, t, :], ACT.Square, accum_out=st[:, 24 + t:25 + t]).then_inc(x_sq, 1)
            act.wait_ge(x_rs, 1)
            act.wait_ge(x_sq, TT)
            for t in range(TT):
                av(xn_tok[:, t, :], x_tok[:, t, :], ACT.Copy, scale=st[:, 32 + t:33 + t]).then_inc(x_nrm, 1)
            for k in range(KT):
                act.wait_ge(xt_mm, k + 1)
                av(hT[:, k, :], ps[k][:, :], ACT.Copy, scale=col("norm_w", k)).then_inc(xt_ev, 1)
            act.wait_ge(ang_in, 1)
            av(tw[1], tw[0], ACT.Sin, scale=PI2_SAFE)
            av(tw[2], tw[0], ACT.Sin, scale=PI_SAFE).then_inc(trig_ready, 1)
            act.wait_ge(ang_in, 2)
            av(angA[:, 1], angA[:, 3], ACT.Sin, scale=PI2_SAFE)
            av(angA[:, 2], angA[:, 3], ACT.Sin, scale=PI_SAFE).then_inc(trig_ready, 1)
            for m in range(KT):
                act.wait_ge(bt_mm, m + 1)
                av(pack[:, m, 0:256], ps[m][:, 0:256], ACT.Copy).then_inc(pack_ready, 1)

            def split(x, i, half, bank, done, evac):
                act.wait_ge(done, i * 2 + (half + 2))
                src = ps[bank][:, 0:2 * PC].rearrange("p (t c) -> p t c", t=2)
                dst = qkv_tok[x][:, 2 * half:2 * half + 2, bass.ds(i * PC, PC)]
                if x == 2:
                    av(dst, src, ACT.Copy).then_inc(evac, 1)
                    return
                av(dst, src, ACT.Copy)
                if half == 0:
                    act.wait_ge(ss_done, i * 2 + x + 1)
                av(sq[:, 2 * half * PH:(2 * half + 2) * PH, :].rearrange("p a b -> p (a b)"), ps[bank][:, 0:2 * PC],
                   ACT.Square).then_inc(evac, 1)

            act.wait_ge(pack_ready, KT)
            act.wait_ge(bb_ready, 3)
            with act.Fori(0, KT) as i:
                act.wait_ge(u_mm, i + 1 + 1)
                act.wait_ge(y_ready, i + 1)
                av(u_cur, ps[0][:, :], ACT.Copy).then_inc(u_ev, 1)
                act.wait_ge(c_mm, i * 4 + 1)
                av(lhs_cur.rearrange("p a b -> p (a b)"), pack[:, bass.ds(i, 1), 0:512].rearrange("p o n -> p (o n)"),
                   ACT.Copy).then_inc(lhs_ready, 1)
                split(0, i, 0, 1, q_mm, q_ev)
                split(0, i, 1, 2, q_mm, q_ev)
                split(1, i, 0, 3, k_mm, k_ev)
                split(1, i, 1, 4, k_mm, k_ev)
                split(2, i, 0, 1, v_mm, v_ev)
                split(2, i, 1, 2, v_mm, v_ev)
                act.wait_ge(y_ready, i + 1 + 1)
                av(gT[:, bass.ds(i, 1), :].rearrange("p o n -> p (o n)"), y_sb, ACT.Gelu_apprx_tanh).then_inc(gelu_done, 1)

            with act.Fori(0, 4) as p:
                act.wait_ge(sc_mm, p * 8 + 1)
                for x in range(6):
                    act.wait_ge(tr_mm, p * 6 + (x + 2))
                    av(qkT[:, x, :], ps[6 + x % 2][:, :], ACT.Copy).then_inc(tr_ev, 1)

                def exps(u):
                    act.wait_ge(nm_ready, p * 8 + (u + 1))
                    if u >= 2:
                        act.wait_ge(pt_mm, p * sum(CHU) + sum(CHU[:u - 1]) + 1)
                    if u < 2:
                        act.wait_ge(pt_mm, p * sum(CHU) + 1)
                        act.wait_ge(o_ev, p * 8 + 1)
                    else:
                        act.wait_ge(o_ev, p * 8 + (u - 1) + 1)
                    n = NKEY[u % 4] * P
                    av(pr[:, u % 2, 0:n], sm[:, u % 2, 0:n], ACT.Exp, bias=nmx[:, u % 2:u % 2 + 1],
                       accum_out=den[:, u % 2:u % 2 + 1]).then_inc(p_ready, 1)

                def probs_evac(u):
                    act.wait_ge(pv_mm, p * 8 + u + 1)
                    for c in range(CHU[u]):
                        n = min(4, NKEY[u % 4] - 4 * c)
                        act.wait_ge(pt_mm, p * sum(CHU) + (sum(CHU[:u]) + c + 1) + 1)
                        av(pT[:, 4 * c:4 * c + n, :].rearrange("p a b -> p (a b)"), ps[3 + c][:, 0:n * P],
                           ACT.Copy).then_inc(pt_ev, 1)

                exps(0)
                for u in range(8):
                    if u < 7:
                        exps(u + 1)
                    probs_evac(u)

            act.wait_ge(sm_done, 33)
            for s in range(13):
                act.wait_ge(step_free, s + 1)
                b = 4 * (s % 2)
                sg = sig[:, s % 2]
                if s < 4 or s == 8:
                    for c in range(4):
                        if c % 2 == 0:
                            act.wait_ge(panel_mm, 2 * s + 1 + c // 2)
                        av(sg[:, c, :], ps[b + c][:, :], ACT.Sigmoid).then_inc(glu_sig, 1)
                else:
                    for c in range(2):
                        act.wait_ge(panel_mm, 2 * s + 1)
                        av(sg[:, c, :], ps[b + c][:, :], ACT.Sigmoid).then_inc(rs_sig, 1)
                if s == 9:
                    act.wait_ge(ang2, 1)
                    av(sinT, ang, ACT.Sin, scale=PI2_SAFE)
                    av(cosT, ang, ACT.Sin, scale=PI_SAFE).then_inc(trig2, 1)
            if upto == 1:
                return

            def norm(t0, ready, count, cname):
                for t in range(TT):
                    act.wait_ge(ready, count)
                    av(xn2[:, t, :], x_res[:, t, :], ACT.Square, accum_out=st2[:, 8 + t:9 + t]).then_inc(n_sq, 1)
                act.wait_ge(n_rs, t0 // TT + 1)
                act.wait_ge(n_sq, t0 + TT)
                for t in range(TT):
                    av(xn2[:, t, :], x_res[:, t, :], ACT.Copy, scale=st2[:, 16 + t:17 + t]).then_inc(n_nrm, 1)
                for k in range(KT):
                    act.wait_ge(nt_mm, 2 * t0 + k + 1)
                    av(hT[:, k, :], ps[k][:, :], ACT.Copy, scale=col(cname, k)).then_inc(nt_ev, 1)

            norm(0, x1_ready, 8, "a_norm")
            n = first_of["lo"]
            junk = rot
            for h in range(2):
                act.wait_ge(panel_mm, n + 1 + h)
                for t in range(TT):
                    src = ps[4 + 2 * h + t // 2][:, (t % 2) * 256:(t % 2 + 1) * 256]
                    if h == 0:
                        av(l_tok[:, t, 0:256], src, ACT.Square, accum_out=st2[:, 32 + t:33 + t]).then_inc(lo_sq, 1)
                    else:
                        av(l_tok[:, t, 256:384], src[:, 0:P], ACT.Square, accum_out=st2[:, 36 + t:37 + t]).then_inc(lo_sq, 1)
                        av(l_tok[:, t, 384:512], src[:, P:2 * P], ACT.Square, accum_out=st2[:, 44 + t:45 + t]).then_inc(lo_sq, 1)
            act.wait_ge(lo_rs, 1)
            act.wait_ge(lo_sq, 12)
            for t in range(TT):
                a0 = ps[4 + t // 2][:, (t % 2) * 256:(t % 2 + 1) * 256]
                a1 = ps[6 + t // 2][:, (t % 2) * 256:(t % 2 + 1) * 256]
                av(l_tok[:, t, 0:256], a0, ACT.Copy, scale=st2[:, 56 + t:57 + t]).then_inc(lo_ev, 1)
                av(l_tok[:, t, 256:384], a1[:, 0:P], ACT.Copy, scale=st2[:, 56 + t:57 + t]).then_inc(lo_ev, 1)
                av(l_tok[:, t, 384:512], a1[:, P:2 * P], ACT.Copy, scale=st2[:, 60 + t:61 + t]).then_inc(lo_ev, 1)
            for k in range(5):
                act.wait_ge(ct_mm, k + 1)
                if k < 4:
                    av(cT[:, k, :], ps[4 + k][:, :], ACT.Copy, scale=col("q_norm", k) if k < 3 else col("kv_norm")).then_inc(ct_ev, 1)
                else:
                    av(krT, ps[4][:, :], ACT.Copy).then_inc(ct_ev, 1)
            act.wait_ge(pads, 1)
            for i in range(4):
                b = 4 * (i % 2)
                act.wait_ge(step_free, 16 + i + 1)
                act.wait_ge(panel_mm, PU + 2 * i + 1)
                for c in range(2):
                    av(upad[:, i % 2, c, PAD:PAD + T], ps[b + c][:, :], ACT.Copy).then_inc(u_pad, 1)
                act.wait_ge(panel_mm, PU + 2 * i + 2)
                for c in range(2):
                    av(sig[:, i % 2, c, :], ps[b + 2 + c][:, :], ACT.Sigmoid).then_inc(gb_sig, 1)

            act.wait_ge(y2_ready, 8)
            with act.Fori(0, 2) as r:
                for q in range(2):
                    def cnt(c, k):
                        return r * (2 * c) + (q * c + k)

                    act.wait_ge(s_mm, cnt(8, 0) + 1)
                    for c in range(2):
                        act.wait_ge(pr_mm, cnt(7, c + 1))
                        av(qnT[:, c, :], ps[c][:, :], ACT.Copy).then_inc(pr_ev, 1)
                    for c in range(2):
                        act.wait_ge(pr_mm, cnt(7, 4 + c + 1))
                        av(knT[:, c, :], ps[c][:, :], ACT.Copy).then_inc(pr_ev, 1)
                    act.wait_ge(o_mm, cnt(2, 0) + 1)
                    for h in range(2):
                        if h == 0:
                            act.wait_ge(pr_mm, cnt(7, 7))
                        else:
                            act.wait_ge(panel_mm, r * 4 + (UQ + 2 * q + 1))
                        av(v_m[:, 2 * h:2 * h + 2, :], ps[2 + h][:, :].rearrange("p (t c) -> p t c", t=2), ACT.Copy).then_inc(pr_ev, 1)

                    def exps(u):
                        act.wait_ge(nmax, cnt(8, u + 1))
                        if u < 3:
                            act.wait_ge(t_mm, cnt(8, 0) + 1)
                        else:
                            act.wait_ge(t_mm, cnt(8, u - 2) + 1)
                        av(p_m[:, u % 3, :], ps[4 + u % 3][:, :], ACT.Exp, scale=SCALE2, bias=st2[:, 72 + u:73 + u],
                           accum_out=st2[:, 80 + u:81 + u]).then_inc(e_done, 1)

                    def evac(u):
                        b = (7, 0)[u % 2]
                        h, i = u // 4, u % 4
                        if i == 0:
                            act.wait_ge(o_mm, cnt(2, h - 1 + 2))
                        act.wait_ge(t_mm, cnt(8, u + 2))
                        av(pT_m[:, h, :, i * P:(i + 1) * P], ps[b][:, :].rearrange("p (k c) -> p k c", k=4), ACT.Copy).then_inc(t_ev, 1)

                    exps(0)
                    exps(1)
                    act.wait_ge(panel_mm, r * 4 + (UQ + 2 * q + 2))
                    for c in range(2):
                        av(sig_m[:, c, :], ps[c][:, :], ACT.Exp, scale=-1.0).then_inc(ga_sig, 1)
                    for u in range(2, 8):
                        exps(u)
                        evac(u - 2)
                    evac(6)
                    evac(7)
            act.wait_ge(dec_in, 16)
            av(lsg[:, 0, :], dec, ACT.Abs).then_inc(dec_abs, 1)
            act.wait_ge(dec_abs, 1)
            av(lsg[:, 1, :], lsg[:, 0, :], ACT.Exp, scale=-1.0).then_inc(dec_abs, 1)
            for h in range(RH):
                act.wait_ge(dec_arg, h + 1)
                av(decay[:, h, :], decay[:, h, :], ACT.Exp).then_inc(dec_exp, 1)
            if upto == 2:
                return

            norm(TT, x2_ready, 16, "r_norm")
            with act.Fori(0, 2) as r:
                for q in range(2):
                    def cnt(c, k):
                        return r * (2 * c) + (q * c + k)

                    act.wait_ge(ro_mm, cnt(4, 0) + 1)
                    for x in range(2):
                        act.wait_ge(panel_mm, r * 12 + (RQ + 6 * q + 3 + x))
                        for b in range(2):
                            av(v_r[:, 2 * b:2 * b + 2, x * 256:(x + 1) * 256],
                               ps[4 + 2 * x + b][:, :].rearrange("p (t c) -> p t c", t=2), ACT.Copy).then_inc(v_cp, 1)
                    for x in range(2):
                        act.wait_ge(panel_mm, r * 12 + (RQ + 6 * q + 5 + x))
                        act.wait_ge(rg_ready, cnt(4, 0) + 1)
                        for c in range(2):
                            av(sig_r[:, 2 * x + c, :], ps[(4, 2)[x] + c][:, :], ACT.Sigmoid).then_inc(rg_sig, 1)
            act.wait_ge(x3_ready, 16)
            for t in range(TT):
                av(squares[:, t, :], x_res[:, t, :], ACT.Square, accum_out=st2[:, 8 + t:9 + t]).then_inc(n_sq, 1)

        @block.vector
        def _(dve):
            V = Steps(dve, v_step)
            for first in (e_used, bu_used, ss_done, scaled, y_ready, sm_done, o_ev, step_free, ym_ready, rg_ready, on_ready, yr_ready):
                dve.sem_inc(first, 1)
            v = nc.vector
            MUL, ADD, SUB = ALU.mult, ALU.add, ALU.subtract
            V(v.memset(half_m, -0.5))
            V(v.memset(st[:, 36:40], 0.0))
            v.memset(st[:, 40:41], 0.0).then_inc(e_used, 1)

            def chain(ins):
                V(ins)
                V.wait()

            s_ = lambda k: ssp[:, k, :]
            dve.wait_ge(ssm_in, 64)
            dve.wait_ge(ssm_exp, 1)
            v.tensor_tensor(s_(4), lr, s_(3), MUL).then_inc(ssm_dt, 1)
            chain(v.tensor_tensor(s_(6), li, s_(3), MUL))
            chain(v.tensor_scalar(s_(7), s_(6), TURN, ROUND, MUL, ADD))
            chain(v.tensor_scalar(s_(7), s_(7), ROUND, None, SUB))
            chain(v.scalar_tensor_tensor(s_(6), s_(7), -PI2_A, s_(6), MUL, ADD))
            chain(v.scalar_tensor_tensor(s_(6), s_(7), -PI2_B, s_(6), MUL, ADD))
            chain(v.scalar_tensor_tensor(s_(6), s_(7), -PI2_C, s_(6), MUL, ADD))
            chain(v.tensor_scalar(s_(8), s_(6), TURN * 4096, ROUND, MUL, ADD))
            chain(v.tensor_scalar(s_(8), s_(8), ROUND, 1.0 / 4096, SUB, MUL))
            chain(v.scalar_tensor_tensor(s_(9), s_(8), -PI2_A, s_(6), MUL, ADD))
            chain(v.scalar_tensor_tensor(s_(9), s_(8), -(PI2_B + PI2_C), s_(9), MUL, ADD))
            chain(v.tensor_scalar(s_(9), s_(9), TURN, None, MUL))
            dve.wait_ge(x_sq, TT)
            v.tensor_scalar(st[:, 28:32], st[:, 24:28], 1.0 / D, EPS, MUL, ADD).then_inc(x_ms, 1)
            tvb = tv.unsqueeze(1).to_broadcast([P, NTILE, 48])

            def wide(k):
                return s_(k).unsqueeze(2).to_broadcast([P, NTILE, 48])

            V(v.tensor_tensor(tw[0], tvb, wide(8), MUL))
            chain(v.tensor_tensor(tw[1], tvb, wide(9), MUL))
            chain(v.tensor_scalar(tw[2], tw[0], ROUND, ROUND, ADD, SUB))
            chain(v.tensor_tensor(tw[0], tw[0], tw[2], SUB))
            chain(v.tensor_tensor(tw[0], tw[0], tw[1], ADD))
            chain(v.tensor_scalar(tw[2], tw[0], ROUND, ROUND, ADD, SUB))
            v.tensor_tensor(tw[0], tw[0], tw[2], SUB).then_inc(ang_in, 1)
            dve.wait_ge(const_in, 64)
            chain(v.tensor_copy(st[:, 16:20], st[:, 20:24].bitcast(mybir.dt.int32)))
            for t in range(TT):
                V(v.tensor_scalar(angA[:, 1, t, :], angA[:, 0, t, :], st[:, 16 + t:17 + t], None, MUL))
            V.wait()
            chain(v.tensor_scalar(angA[:, 2], angA[:, 1], TURN, ROUND, MUL, ADD))
            chain(v.tensor_scalar(angA[:, 2], angA[:, 2], ROUND, None, SUB))
            for part in (PI2_A, PI2_B, PI2_C):
                chain(v.scalar_tensor_tensor(angA[:, 1], angA[:, 2], -part, angA[:, 1], MUL, ADD))
            chain(v.tensor_scalar(angA[:, 3], angA[:, 1], TURN, 0.5, MUL, ALU.min))
            v.tensor_scalar(angA[:, 3], angA[:, 3], -0.5, None, ALU.max).then_inc(ang_in, 1)
            dve.wait_ge(trig_ready, 1)
            ptab = pack[:, :, 512:896].rearrange("p m (j c) -> p m j c", j=4)
            tw4 = [x.rearrange("p (m j) c -> p m j c", j=4) for x in tw]
            V(v.tensor_copy(ptab[:, :, :, 48:96], tw4[1]))
            chain(v.tensor_tensor(tw[3], tw[2], tw[2], MUL))
            chain(v.tensor_scalar(ptab[:, :, :, 0:48], tw4[3], -2.0, 1.0, MUL, ADD))
            dve.wait_ge(ssm_exp, 2)
            V(v.tensor_copy(pack[:, :, 896:900], s_(5).rearrange("p (m j) -> p m j", j=4)))
            pt32 = pack[:, :, 512:896].rearrange("p m (j c) -> p m j c", j=4)
            s4 = lambda k: s_(k).rearrange("p (m j) -> p m j", j=4)
            V(v.tensor_tensor(s4(10), s4(5), pt32[:, :, :, 33], MUL))
            V(v.tensor_tensor(s4(11), s4(5), pt32[:, :, :, 48 + 33], MUL))
            V(v.tensor_tensor(s_(12), lr, lr, MUL))
            chain(v.tensor_tensor(s_(13), li, li, MUL))
            chain(v.tensor_tensor(s_(12), s_(12), s_(13), ADD))
            V(v.reciprocal(s_(12), s_(12)))
            chain(v.tensor_scalar(s_(10), s_(10), -1.0, None, ADD))
            V(v.tensor_tensor(s_(13), s_(10), lr, MUL))
            V(v.tensor_tensor(s_(14), s_(11), li, MUL))
            V(v.tensor_tensor(s_(15), s_(11), lr, MUL))
            chain(v.tensor_tensor(s_(16), s_(10), li, MUL))
            V(v.tensor_tensor(s_(13), s_(13), s_(14), ADD))
            chain(v.tensor_tensor(s_(15), s_(15), s_(16), SUB))
            V(v.tensor_tensor(s_(13), s_(13), s_(12), MUL))
            chain(v.tensor_tensor(s_(15), s_(15), s_(12), MUL))
            fb = lambda k: s_(k).unsqueeze(2).to_broadcast([P, NTILE, 32])
            V(v.tensor_tensor(bbs[:, 0], b_nat[:, 0], fb(13), MUL))
            chain(v.tensor_tensor(bt_tmp, b_nat[:, 1], fb(15), MUL))
            v.tensor_tensor(bbs[:, 0], bbs[:, 0], bt_tmp, SUB).then_inc(bb_ready, 1)
            dve.wait_ge(bb_ready, 1)
            V(v.tensor_tensor(bbs[:, 1], b_nat[:, 1], fb(13), MUL))
            chain(v.tensor_tensor(bt_tmp, b_nat[:, 0], fb(15), MUL))
            v.tensor_tensor(bbs[:, 1], bbs[:, 1], bt_tmp, ADD).then_inc(bb_ready, 1)
            dve.wait_ge(trig_ready, 2)
            V(v.tensor_copy(csA[:, 1], angA[:, 1]))
            chain(v.tensor_tensor(angA[:, 3], angA[:, 2], angA[:, 2], MUL))
            chain(v.tensor_scalar(csA[:, 0], angA[:, 3], -2.0, 1.0, MUL, ADD))
            v.memset(st[:, 41:42], 0.0).then_inc(bb_ready, 1)

            def tile_step(i, j):
                n = i * 4 + (j + 1)
                dve.wait_ge(bu_mm, n)
                dve.wait_ge(e_ready, n)
                c, s = E[:, j % 2, 0], E[:, j % 2, 1]
                bre, bim = ps[5][:, :], ps[6][:, :]
                V(v.tensor_tensor(t_a[0], bre, c, MUL))
                k2 = V(v.tensor_tensor(t_a[1], bim, s, MUL))
                V(v.tensor_tensor(gs[:, 0], bim, c, MUL))
                v.tensor_tensor(gs[:, 1], bre, s, MUL).then_inc(bu_used, 1)
                V.wait(k2)
                k3 = V(v.tensor_tensor(bp[:, 0], t_a[0], t_a[1], ADD))
                dve.wait_ge(bu_used, n + 1)
                k4 = V(v.tensor_tensor(bp[:, 1], gs[:, 0], gs[:, 1], SUB))
                mag = pack[:, bass.ds(i, 1), 896 + j:897 + j].rearrange("p o n -> p (o n)").to_broadcast([P, 512])
                V.wait(k4)
                k5 = V(v.tensor_tensor_scan(gs[:, 0], mag, bp[:, 0], 0.0, MUL, ADD))
                k6 = V(v.tensor_tensor_scan(gs[:, 1], mag, bp[:, 1], 0.0, MUL, ADD))
                V.wait(k5)
                V(v.tensor_tensor(t_a[0], gs[:, 0], c, MUL))
                V.wait(k6)
                V(v.tensor_tensor(t_a[1], gs[:, 1], s, MUL))
                V(v.tensor_tensor(bp[:, 0], gs[:, 1], c, MUL))
                v.tensor_tensor(bp[:, 1], gs[:, 0], s, MUL).then_inc(e_used, 1)
                if j == 0:
                    dve.wait_ge(c_mm, i * 4 + 1)
                else:
                    dve.wait_ge(c_mm, i * 4 + (j - 1) + 1)
                dve.wait_ge(e_used, n + 1 + 1)
                V(v.tensor_tensor(hs[:, j % 2, 0], t_a[0], t_a[1], SUB))
                v.scalar_tensor_tensor(hs[:, j % 2, 1], bp[:, 0], -1.0, bp[:, 1], MUL, SUB).then_inc(h_ready, 1)
                dve.wait_ge(h_ready, n)

            def heads_ms(i, x):
                dve.wait_ge((q_ev, k_ev)[x], i * 2 + 2 + 1)
                so = 48 + 36 * x
                v.tensor_reduce(st[:, so:so + 12], sq, AX.X, ADD).then_inc(ss_done, 1)
                dve.wait_ge(ss_done, i * 2 + (x + 2))
                dve.wait_ge(rs_ready, i * 2 + x + 1)
                v.tensor_scalar(st[:, so + 12:so + 24], st[:, so:so + 12], 1.0 / HD, EPS, MUL, ADD).then_inc(ms_ready, 1)

            def heads_scale(i, x):
                so = 48 + 36 * x
                q = qkv_tok[x][:, :, bass.ds(i * PC, PC)]
                dve.wait_ge(rs_ready, i * 2 + (x + 2))
                rs = st[:, so + 24:so + 36].rearrange("p (t h) -> p t h", t=TT).unsqueeze(3).to_broadcast([P, TT, PH, HD])
                q4 = q.rearrange("p t (h d) -> p t h d", h=PH)
                kk = V(v.tensor_tensor(q4, q4, rs, MUL))
                dve.wait_ge(qkw_full, i * 16 + 16)
                V.wait(kk)
                v.tensor_tensor(q, q, qk_w[:, x, :].unsqueeze(1).to_broadcast([P, TT, PC]), MUL).then_inc(scaled, 1)

            with dve.Fori(0, KT) as i:
                V.loop(i, 46)
                tile_step(i, 0)
                tile_step(i, 1)
                heads_ms(i, 0)
                tile_step(i, 2)
                heads_scale(i, 0)
                tile_step(i, 3)
                heads_ms(i, 1)
                dve.wait_ge(c_mm, i * 4 + 4 + 1)
                dve.wait_ge(gelu_done, i + 1)
                v.scalar_tensor_tensor(y_sb, u_cur, cols[:, bass.ds(i + COLS["d_skip"], 1)], ps[7][:, :], MUL, ADD).then_inc(y_ready, 1)
                heads_scale(i, 1)
            V.end(KT)

            dve.wait_ge(mask_in, 16)
            with dve.Fori(0, 4) as p:
                V.loop(p, 32)

                def soft(u):
                    i = u % 4
                    dve.wait_ge(sc_mm, p * 8 + (u + 2))
                    dve.wait_ge(p_ready, p * 8 + max(u - 1, 0) + 1)
                    w0, w1 = min(i + 1, 2) * P, (i + 1) * P
                    b = u % 2
                    mask_at = [masks[:, 256 - w0:256], masks[:, 256 + 512 - w1:768], masks[:, 768 + 512 - w1:1280]]
                    x0 = 0
                    for g, w in enumerate((w0, w1, w1)):
                        ins = v.scalar_tensor_tensor(sm[:, b, x0:x0 + w], ps[g][:, 0:w], SCALE1, mask_at[g], MUL, ADD)
                        x0 += w
                        if g < 2:
                            V(ins)
                    ins.then_inc(sm_done, 1)
                    dve.wait_ge(sm_done, p * 8 + (u + 2))
                    k = V(v.tensor_reduce(mx[:, b:b + 1], sm[:, b, 0:x0], AX.X, ALU.max))
                    V.wait(k)
                    v.tensor_scalar(nmx[:, b:b + 1], mx[:, b:b + 1], -1.0, None, MUL).then_inc(nm_ready, 1)

                def o_out(u):
                    b = u % 2
                    dve.wait_ge(p_ready, p * 8 + (u + 2))
                    k = V(v.reciprocal(rden[:, b:b + 1], den[:, b:b + 1]))
                    dve.wait_ge(pv_mm, p * 8 + (u + 2))
                    V.wait(k)
                    v.tensor_scalar(o_tok[:, u % 4, bass.ds(p * 128 + (u // 4) * HD, HD)], ps[6 + b][:, (u // 4) * HD:(u // 4 + 1) * HD],
                                    rden[:, b:b + 1], None, MUL).then_inc(o_ev, 1)

                soft(0)
                for u in range(8):
                    if u < 7:
                        soft(u + 1)
                    if u >= 1:
                        o_out(u - 1)
                o_out(7)
            V.end(4)

            def angles2():
                dve.wait_ge(misc_in, 32)
                dve.wait_ge(pos_in, 16)
                V(v.tensor_copy(pos2c, pos2i.bitcast(mybir.dt.int32)))
                V.wait()
                pi = turns[:, 0:T].bitcast(mybir.dt.int32)
                for k in range(2):
                    V(v.tensor_scalar(ang[:, k * T:(k + 1) * T], pi, inv_cols[:, k:k + 1], None, MUL))
                for t in range(TT):
                    V(v.tensor_scalar(ang[:, 1024 + 32 * t:1056 + 32 * t], inv_row, pos2c[:, t:t + 1], None, MUL))
                V.wait()
                chain(v.tensor_scalar(turns, ang, TURN, ROUND, MUL, ADD))
                chain(v.tensor_scalar(turns, turns, ROUND, None, SUB))
                for part in (PI2_A, PI2_B, PI2_C):
                    chain(v.scalar_tensor_tensor(ang, turns, -part, ang, MUL, ADD))
                chain(v.tensor_scalar(ang, ang, TURN, 0.5, MUL, ALU.min))
                v.tensor_scalar(ang, ang, -0.5, None, ALU.max).then_inc(ang2, 1)

            def tables2():
                dve.wait_ge(trig2, 1)
                chain(v.tensor_tensor(cosT, cosT, cosT, MUL))
                chain(v.tensor_scalar(cosT, cosT, -2.0, 1.0, MUL, ADD))
                chain(v.tensor_scalar(sinM, sinM, inv_cols[:, 2:3], None, MUL))

            for s in range(13):
                b = 4 * (s % 2)
                sg = sig[:, s % 2]
                if s == 0:
                    v.memset(st[:, 42:43], 0.0).then_inc(step_free, 1)
                if s < 4:
                    for c in range(2):
                        dve.wait_ge(glu_sig, 4 * s + 3 + c)
                        k1 = V(v.tensor_tensor(prod[:, c, :], gT[:, 2 * s + c, :], sg[:, c, :], MUL))
                        k2 = V(v.tensor_tensor(prod[:, 2 + c, :], ps[b + 2 + c][:, :], sg[:, 2 + c, :], MUL))
                        V.wait(k2)
                        v.tensor_tensor(yT[:, 2 * s + c, :], prod[:, c, :], prod[:, 2 + c, :], MUL).then_inc(ys_ready, 1)
                    dve.wait_ge(ys_ready, 2 * s + 2)
                elif s < 8:
                    for c in range(2):
                        dve.wait_ge(rs_sig, 2 * (s - 4) + c + 1)
                        dve.wait_ge(panel_mm, 2 * s + 2)
                        v.tensor_tensor(mT[:, 2 * (s - 4) + c, :], ps[b + 2 + c][:, :], sg[:, c, :], MUL).then_inc(m_ready, 1)
                elif s == 8:
                    for c in range(4):
                        dve.wait_ge(glu_sig, 16 + c + 1)
                        k = V(v.tensor_tensor(prod[:, c, :], ps[b + c][:, :], sg[:, c, :], MUL))
                        V.wait(k)
                        dve.wait_ge(ot_mm, c + 1)
                        v.tensor_tensor(oT[:, c, :], ps[4 + c][:, :], prod[:, c, :], MUL).then_inc(ya_ready, 1)
                    dve.wait_ge(ya_ready, 4)
                else:
                    for c in range(2):
                        if s == 9 and c == 0:
                            angles2()
                        if s == 10 and c == 0:
                            tables2()
                        dve.wait_ge(rs_sig, 8 + 2 * (s - 9) + c + 1)
                        dve.wait_ge(panel_mm, 2 * s + 2)
                        k = V(v.tensor_tensor(prod[:, c, :], ps[b + 2 + c][:, :], sg[:, c, :], MUL))
                        V.wait(k)
                        m = mT[:, 2 * (s - 9) + c, :]
                        v.tensor_tensor(m, m, prod[:, c, :], ADD).then_inc(m_ready, 1)
                    dve.wait_ge(m_ready, 8 + 2 * (s - 9) + 2)
                v.memset(st[:, 43:44], 0.0).then_inc(step_free, 1)
                dve.wait_ge(step_free, s + 2 + 1)
            dve.wait_ge(xr_in, 16)
            for s in (13, 14):
                for h in range(2):
                    n = 2 * s + h
                    dve.wait_ge(panel_mm, n + 1)
                    i = n - 26
                    for q in range(2):
                        xs = x_res[:, 2 * q:2 * q + 2, i * 256:(i + 1) * 256]
                        v.tensor_tensor(xs, ps[4 * (s % 2) + 2 * h + q][:, :].rearrange("p (t c) -> p t c", t=2), xs,
                                        ADD).then_inc(x1_ready, 1)
                v.memset(st[:, 43:44], 0.0).then_inc(step_free, 1)
                dve.wait_ge(step_free, s + 2 + 1)

            if upto == 1:
                return

            def mean_square(t0):
                dve.wait_ge(n_sq, t0 + TT)
                v.tensor_scalar(st2[:, 12:16], st2[:, 8:12], 1.0 / D, EPS, MUL, ADD).then_inc(n_ms, 1)

            mean_square(0)
            dve.wait_ge(nt_mm, KT)
            V(v.memset(upad[:, :, :, 0:PAD], 0.0))
            v.memset(upad[:, :, :, PAD + T:2 * PAD + T], 0.0).then_inc(pads, 1)
            dve.wait_ge(pads, 1)
            n = first_of["lo"]
            dve.wait_ge(panel_mm, n + 3)
            raw = rot.rearrange("p a b -> p (a b)")[:, 0:0]
            kr = kr_tok[:, :, 64:128]
            v.tensor_copy(kr, ps[0][:, 0:256].rearrange("p (t c) -> p t c", t=TT)).then_inc(kr_raw, 1)
            dve.wait_ge(kr_raw, 1)
            tk = y2T[:, 0, :].rearrange("p (x t c) -> p x t c", x=4, t=TT)
            V(v.tensor_tensor(tk[:, 0], kr[:, :, 0:32], cosK, MUL))
            V(v.tensor_tensor(tk[:, 1], kr[:, :, 32:64], sinK, MUL))
            V(v.tensor_tensor(tk[:, 2], kr[:, :, 32:64], cosK, MUL))
            chain(v.tensor_tensor(tk[:, 3], kr[:, :, 0:32], sinK, MUL))
            V(v.tensor_tensor(kr_tok[:, :, 0:32], tk[:, 0], tk[:, 1], SUB))
            v.tensor_tensor(kr_tok[:, :, 32:64], tk[:, 2], tk[:, 3], ADD).then_inc(kr_rot, 1)
            dve.wait_ge(kr_rot, 1)
            v.tensor_copy(kr_tok[:, :, 64:128], kr_tok[:, :, 0:64]).then_inc(kr_rot, 1)
            dve.wait_ge(lo_sq, 12)
            chain(v.tensor_tensor(st2[:, 40:44], st2[:, 32:36], st2[:, 36:40], ADD))
            chain(v.tensor_scalar(st2[:, 48:52], st2[:, 40:44], 1.0 / QL, EPS, MUL, ADD))
            v.tensor_scalar(st2[:, 52:56], st2[:, 44:48], 1.0 / KVL, EPS, MUL, ADD).then_inc(lo_ms, 1)
            dve.wait_ge(lo_ev, 12)
            v.memset(st2[:, 0:1], 0.0).then_inc(step_free, 1)
            dve.wait_ge(step_free, 18)

            def pool_gate(i):
                b = 4 * (i % 2)
                for c in range(2):
                    dve.wait_ge(gb_sig, 2 * i + c + 1)
                    k = V(v.tensor_tensor(prod[:, c, :], ps[b + 2 + c][:, :], sig[:, i % 2, c, :], MUL))
                    dve.wait_ge(pool_mm, i + 1)
                    V.wait(k)
                    v.scalar_tensor_tensor(y2T[:, 8 + 2 * i + c, :], ps[b + c][:, :], col("pool_scale", 2 * i + c),
                                           prod[:, c, :], MUL, MUL).then_inc(y2_ready, 1)
                dve.wait_ge(y2_ready, 2 * i + 2)
                v.memset(st2[:, 0:1], 0.0).then_inc(step_free, 1)
                dve.wait_ge(step_free, 18 + i + 1)

            for i, wd in enumerate(POOLS):
                dve.wait_ge(u_pad, 2 * i + 2)
                src, n = upad[:, i % 2], T + 2 * PAD
                for k in range(i + 1):
                    n -= 1 << k
                    dst = win[:, k % 2]
                    chain(v.tensor_tensor(dst[:, :, 0:n], src[:, :, 0:n], src[:, :, (1 << k):(1 << k) + n], ADD))
                    src = dst
                x0 = PAD - wd // 2
                sums = src[:, :, x0:x0 + T]
                for e in range(2):
                    edge = sums[:, :, e * (T - 8):e * (T - 8) + 8]
                    V(v.tensor_tensor(edge, edge, corr[:, i, 8 * e:8 * e + 8].unsqueeze(1).to_broadcast([P, 2, 8]), MUL))
                V.wait()
                if i >= 2:
                    dve.wait_ge(pool_mm, i - 1)
                v.scalar_tensor_tensor(pool_d[:, i % 2], sums, 1.0 / wd, upad[:, i % 2, :, PAD:PAD + T], MUL, SUB
                                       ).then_inc(d_ready, 1)
                dve.wait_ge(d_ready, i + 1)
                if i >= 1:
                    pool_gate(i - 1)
            pool_gate(3)

            with dve.Fori(0, 2) as r:
                V.loop(r, MLA_STEPS)
                for q in range(2):
                    def cnt(c, k):
                        return r * (2 * c) + (q * c + k)

                    for c in range(2):
                        dve.wait_ge(pr_mm, cnt(7, 3 + c))
                        V(v.tensor_tensor(rot[:, c, :], ps[2 + c][:, :], (cosM, sinM)[c], MUL))
                    V.wait()
                    dve.wait_ge(s_mm, cnt(8, 0) + 1)
                    v.tensor_tensor(qrT, rot[:, 0, :], rot[:, 1, :], ADD).then_inc(rot_done, 1)
                    dve.wait_ge(rot_done, cnt(1, 1))

                    def row_max(u):
                        dve.wait_ge(s_mm, cnt(8, u + 2))
                        k = V(v.tensor_reduce(st2[:, 88 + u:89 + u], ps[4 + u % 3][:, :], AX.X, ALU.max))
                        V.wait(k)
                        if u == 0:
                            dve.wait_ge(e_done, cnt(8, 0) + 1)
                        v.tensor_scalar(st2[:, 72 + u:73 + u], st2[:, 88 + u:89 + u], -SCALE2, None, MUL).then_inc(nmax, 1)

                    def recip(u):
                        dve.wait_ge(e_done, cnt(8, u + 2))
                        if u == 0:
                            dve.wait_ge(p_norm, cnt(8, 0) + 1)
                        v.reciprocal(st2[:, 96 + u:97 + u], st2[:, 80 + u:81 + u]).then_inc(rcp, 1)

                    def gate():
                        for c in range(2):
                            dve.wait_ge(ga_sig, cnt(2, c + 1))
                            k = V(v.tensor_scalar(sig_m[:, c, :], sig_m[:, c, :], 1.0, None, ADD))
                            V.wait(k)
                            k = V(v.reciprocal(sig_m[:, c, :], sig_m[:, c, :]))
                            V.wait(k)
                            v.tensor_tensor(gate_m[:, c, :], ps[c][:, :], sig_m[:, c, :], MUL).then_inc(ga_ready, 1)

                    def gated(h):
                        dve.wait_ge(ga_ready, cnt(2, h + 1))
                        dve.wait_ge(o_mm, cnt(2, h + 2))
                        v.tensor_tensor(y2T[:, bass.ds(r * 4 + (2 * q + h), 1), :].rearrange("p o n -> p (o n)"),
                                        ps[2 + h][:, :], gate_m[:, h, :], MUL).then_inc(ym_ready, 1)

                    row_max(0)
                    row_max(1)
                    recip(0)
                    recip(1)
                    gate()
                    for u in range(2, 8):
                        row_max(u)
                        recip(u)
                        if u == 7:
                            gated(0)
                    gated(1)
                    dve.wait_ge(ym_ready, cnt(2, 2) + 1)
            V.end(2)

            dve.wait_ge(dec_abs, 2)
            dve.wait_ge(delta_in, 16)
            L = lambda k: lsg[:, k, :]
            chain(v.tensor_scalar(L(2), L(1), 2.0, None, ADD))
            chain(v.reciprocal(L(2), L(2)))
            chain(v.tensor_tensor(L(2), L(2), L(1), MUL))
            chain(v.tensor_tensor(L(3), L(2), L(2), MUL))
            chain(v.tensor_scalar(L(4), L(3), 1.0 / 15, None, MUL))
            for d in (13, 11, 9, 7, 5, 3):
                chain(v.scalar_tensor_tensor(L(4), L(4), 1.0 / d, L(3), ADD, MUL))
            chain(v.scalar_tensor_tensor(L(4), L(4), 1.0, L(2), ADD, MUL))
            chain(v.tensor_scalar(L(5), dec, 0.0, None, ALU.min))
            chain(v.scalar_tensor_tensor(L(5), L(4), -2.0, L(5), MUL, ADD))
            chain(v.tensor_scalar(L(4), L(5), -1.0, None, MUL))
            dve.wait_ge(t_ev, 33)
            dve.wait_ge(o_mm, 9)
            for h in range(RH):
                V(v.tensor_scalar(dt1, delta, 0.0, L(5)[:, h:h + 1], ALU.max, MUL))
                chain(v.tensor_scalar(dt2, delta, 0.0, L(4)[:, 4 + h:5 + h], ALU.min, MUL))
                v.tensor_tensor(decay[:, h, :], dt1, dt2, ADD).then_inc(dec_arg, 1)
                dve.wait_ge(dec_arg, h + 1)

            def residual(n0, s, ready):
                b = 4 * (s % 2)
                i = (s - 20) % 4
                dve.wait_ge(panel_mm, n0 + 2)
                for t in range(TT):
                    xs = x_res[:, t, i * 256:(i + 1) * 256]
                    v.tensor_tensor(xs, ps[b + t][:, 0:256], xs, ADD).then_inc(ready, 1)
                v.memset(st2[:, 0:1], 0.0).then_inc(step_free, 1)
                dve.wait_ge(step_free, s + 2 + 1)

            for i in range(4):
                residual(OA + 2 * i, 20 + i, x2_ready)
            if upto == 2:
                return
            mean_square(TT)
            dve.wait_ge(dec_exp, RH)
            with dve.Fori(0, 2) as r:
                V.loop(r, RET_STEPS)
                for q in range(2):
                    def cnt(c, k):
                        return r * (2 * c) + (q * c + k)

                    for x, dst in enumerate((q_r, k_r)):
                        dve.wait_ge(panel_mm, r * 12 + (RQ + 6 * q + 1 + x))
                        x1, x2 = ps[2 * x][:, :], ps[2 * x + 1][:, :]
                        V(v.tensor_tensor(rot_r[:, 0, :], x1, cosR, MUL))
                        V(v.tensor_tensor(rot_r[:, 1, :], x2, sinR, MUL))
                        V(v.tensor_tensor(rot_r[:, 2, :], x2, cosR, MUL))
                        V(v.tensor_tensor(rot_r[:, 3, :], x1, sinR, MUL))
                        V.wait()
                        V(v.tensor_tensor(dst[:, 0, :], rot_r[:, 0, :], rot_r[:, 1, :], SUB))
                        v.tensor_tensor(dst[:, 1, :], rot_r[:, 2, :], rot_r[:, 3, :], ADD).then_inc(rqk_rot, 1)
                        dve.wait_ge(rqk_rot, cnt(2, x + 1))
                    for j in range(TT):
                        dve.wait_ge(rs_mm, cnt(4, j + 1))
                        x0 = 3 * P - j * P
                        dj = decay[:, bass.ds(r * 2 + q, 1), x0:x0 + T].rearrange("p o n -> p (o n)")
                        v.scalar_tensor_tensor(sd[:, j, :], ps[j][:, :], RK ** -0.5, dj, MUL, MUL).then_inc(sd_ready, 1)

                    def gates(x):
                        for c in range(2):
                            k = 2 * x + c
                            dve.wait_ge(rg_sig, cnt(4, k + 1))
                            gcol = cols[:, bass.ds(r * 8 + (COLS["gn"] + 4 * q + k), 1)]
                            v.scalar_tensor_tensor(gate_r[:, k, :], ps[(4, 2)[x] + c][:, :], gcol, sig_r[:, k, :], MUL, MUL
                                                   ).then_inc(rg_ready, 1)

                    gates(0)
                    for i in range(TT):
                        dve.wait_ge(ro_mm, cnt(4, i + 2))
                        k = V(v.bn_stats(st2[:, 104 + 6 * i:110 + 6 * i], ps[(6, 7, 0, 1)[i]][:, :]))
                    V.wait(k)
                    apart(dve)
                    for i in range(TT):
                        k = V(v.bn_aggr(st2[:, 128 + 2 * i:130 + 2 * i], st2[:, 104 + 6 * i:110 + 6 * i]))
                    V.wait(k)
                    mv = st2[:, 128:136].rearrange("p (i x) -> p i x", x=2)
                    v.tensor_scalar(st2[:, 136:140], mv[:, :, 1], EPS, None, ADD).then_inc(var_ready, 1)
                    dve.wait_ge(rstd, cnt(1, 1))
                    for i in range(TT):
                        v.tensor_scalar(on[:, i, :], ps[(6, 7, 0, 1)[i]][:, :], mv[:, i, 0:1], st2[:, 140 + i:141 + i], SUB, MUL
                                        ).then_inc(on_ready, 1)
                    gates(1)
                    dve.wait_ge(rg_ready, cnt(4, 4) + 1)
                    for i in range(TT):
                        dve.wait_ge(rt_mm, cnt(4, i + 1))
                        v.tensor_tensor(y2T[:, bass.ds(r * 8 + 4 * q, 4), i * P:(i + 1) * P],
                                        ps[4 + i][:, :].rearrange("p (k c) -> p k c", k=4),
                                        gate_r[:, :, i * P:(i + 1) * P], MUL).then_inc(yr_ready, 1)
                    dve.wait_ge(yr_ready, cnt(4, 4) + 1)
            V.end(2)
            for i in range(4):
                residual(TA + 2 * i, 24 + i, x3_ready)
            mean_square(2 * TT)
            dve.wait_ge(gain_in, 16)
            dve.wait_ge(n_rs, 3)
            for t in range(TT):
                v.scalar_tensor_tensor(x_res[:, t, :], x_res[:, t, :], st2[:, 16 + t:17 + t], gain, MUL, MUL).then_inc(f_out, 1)

        @block.gpsimd
        def _(pool):
            G = Steps(pool, g_step)
            for first in (rs_ready, p_norm):
                pool.sem_inc(first, 1)
            g = nc.gpsimd
            MUL, ADD, SUB = ALU.mult, ALU.add, ALU.subtract
            pool.wait_ge(v_step, 2)
            pool.wait_ge(x_ms, 1)
            g.tensor_tensor(st[:, 32:36], st[:, 28:32], half_m[:, 0:4], ALU.pow).then_inc(x_rs, 1)
            pool.wait_ge(bb_ready, 3)

            def phases(i, j):
                n = i * 4 + (j + 1)
                tab = pack[:, bass.ds(i, 1), 512 + 96 * j:608 + 96 * j].rearrange("p o n -> p (o n)")
                hi = lambda x: tab[:, 48 * x:48 * x + 32].unsqueeze(2).to_broadcast([P, 32, 16])
                lo = lambda x: tab[:, 48 * x + 32:48 * x + 48].unsqueeze(1).to_broadcast([P, 32, 16])
                r = lambda x: x.rearrange("p (a b) -> p a b", a=32)
                c, s = E[:, j % 2, 0], E[:, j % 2, 1]
                pool.wait_ge(e_used, i * 4 + j + 1)
                apart(pool)
                G(g.tensor_tensor(r(e_t[0]), hi(0), lo(0), MUL))
                k = G(g.tensor_tensor(r(e_t[1]), hi(1), lo(1), MUL))
                G.wait(k)
                k = G(g.tensor_tensor(c, e_t[0], e_t[1], SUB))
                G.wait(k)
                apart(pool)
                G(g.tensor_tensor(r(e_t[0]), hi(1), lo(0), MUL))
                k = G(g.tensor_tensor(r(e_t[1]), hi(0), lo(1), MUL))
                G.wait(k)
                g.tensor_tensor(s, e_t[0], e_t[1], ADD).then_inc(e_ready, 1)
                pool.wait_ge(e_ready, n)

            def power(i, x):
                so = 48 + 36 * x
                pool.wait_ge(ms_ready, i * 2 + (x + 1))
                g.tensor_tensor(st[:, so + 24:so + 36], st[:, so + 12:so + 24], half_m[:, 0:12], ALU.pow
                                ).then_inc(rs_ready, 1)

            def rope(i, x):
                pool.wait_ge(scaled, i * 2 + (x + 2))
                apart(pool)
                q = qkv_tok[x][:, :, bass.ds(i * PC, PC)].rearrange("p t (h d) -> p t h d", h=PH)
                x1, x2 = q[:, :, :, 0:ROPE1], q[:, :, :, ROPE1:2 * ROPE1]
                cb = csA[:, 0].unsqueeze(2).to_broadcast([P, TT, PH, ROPE1])
                sb = csA[:, 1].unsqueeze(2).to_broadcast([P, TT, PH, ROPE1])
                G(g.tensor_tensor(rt[0], x1, cb, MUL))
                G(g.tensor_tensor(rt[1], x2, sb, MUL))
                G(g.tensor_tensor(rt[2], x2, cb, MUL))
                k = G(g.tensor_tensor(rt[3], x1, sb, MUL))
                G.wait(k)
                apart(pool)
                G(g.tensor_tensor(x1, rt[0], rt[1], SUB))
                g.tensor_tensor(x2, rt[2], rt[3], ADD).then_inc(roped, 1)
                pool.wait_ge(roped, i * 2 + (x + 1))

            def turn(i, more):
                phases(i, 2)
                power(i, 0)
                phases(i, 3)
                rope(i, 0)
                if more:
                    phases(i + 1, 0)
                power(i, 1)
                if more:
                    phases(i + 1, 1)
                rope(i, 1)

            phases(0, 0)
            phases(0, 1)
            with pool.Fori(0, KT - 1) as i:
                G.loop(i, 30)
                turn(i, True)
            G.end(KT - 1)
            turn(KT - 1, False)
            pool.wait_ge(gelu_done, KT + 1)
            pool.wait_ge(c_mm, 4 * KT + 1)
            with pool.Fori(0, 4) as p:
                pool.wait_ge(tr_mm, p * 6 + 1)
                apart(pool)
                for x in range(6):
                    src = qkv_tok[x // 3][:, :, bass.ds(p * 128 + (x % 3) * 512, P)]
                    ins = g.tensor_copy(qg[:, x], src)
                ins.then_inc(qg_ready, 1)
            if upto == 1:
                return

            def power2(k):
                pool.wait_ge(n_ms, k + 1)
                g.tensor_tensor(st2[:, 16:20], st2[:, 12:16], half_m[:, 0:4], ALU.pow).then_inc(n_rs, 1)

            power2(0)
            pool.wait_ge(lo_ms, 1)
            g.tensor_tensor(st2[:, 56:64], st2[:, 48:56], half_m[:, 0:8], ALU.pow).then_inc(lo_rs, 1)
            with pool.Fori(0, 4) as p:
                for u in range(8):
                    pool.wait_ge(rcp, p * 8 + (u + 1))
                    apart(pool)
                    g.tensor_scalar(p_m[:, u % 3, :], p_m[:, u % 3, :], st2[:, 96 + u:97 + u], None, MUL).then_inc(p_norm, 1)
            if upto == 2:
                return
            power2(1)
            with pool.Fori(0, 4) as h:
                pool.wait_ge(var_ready, h + 1)
                g.tensor_tensor(st2[:, 140:144], st2[:, 136:140], half_m[:, 0:4], ALU.pow).then_inc(rstd, 1)
            power2(2)
def constants():
    p = np.arange(P)
    t = np.concatenate([16 * np.arange(32), np.arange(16)]).astype(np.float32)
    invA = (np.float32(500000.0) ** (-np.arange(0, 16, 2, dtype=np.float32) / np.float32(16))).astype(np.float32)
    k = np.arange(256)[None, :] - P
    q = p[:, None]
    m0 = (k <= q) & (k >= q - P)
    k = np.arange(512)[None, :] - 384
    masks = [m0] + [(k <= q) & ((q - k) % d == 0) for d in (4, 16)]
    masks = np.where(np.concatenate(masks, 1), 0.0, NEG).astype(np.float32)
    half = np.arange(0, 64, 2, dtype=np.float32) / np.float32(64)
    inv_m = np.float32(1.0) / np.float32(10000.0) ** half
    inv_r = np.float32(1.0) / np.float32(10000.0) ** (np.arange(0, RK, 2, dtype=np.float32) / np.float32(RK))
    misc = np.zeros((P, 99), np.float32)
    tt = np.arange(T)
    for g, w in enumerate(POOLS):
        count = np.clip(tt + w // 2 - 1, 0, T - 1) - np.clip(tt - w // 2, 0, T - 1) + 1
        c = w / count
        misc[:, 16 * g:16 * g + 16] = np.concatenate([c[:8], c[-8:]])
    misc[:, 64], misc[:, 65] = inv_r, inv_m[p % 32]
    misc[:, 66] = np.where(p % 64 < 32, -1.0, 1.0)
    misc[:, 67:99] = inv_m
    return {
        "c_misc": misc,
        "c_delta": (np.arange(DELTAS)[None, :] - 3 * P - p[:, None]).astype(np.float32),
        "c_ident": np.eye(P, dtype=np.float32),
        "c_t": np.tile(t, (P, 1)),
        "c_angA": np.ascontiguousarray(np.tile(invA, (P, TT, 1))),
        "c_masks": masks,
    }


def columns_of(w):
    return w.reshape(-1, P, w.shape[1]).transpose(1, 0, 2)


def layout(x):
    w_in = x["w_in"][0]
    at = {"u": 0, "zs": 1024, "q": 2048, "k": 3584, "v": 5120, "za": 6656, "rs": 7168, "ra": 8192}
    d = {"x": x["x"]}
    loop_w = []
    for m in range(KT):
        parts = [columns_of(w_in[:, at["u"] + m * P:at["u"] + (m + 1) * P])]
        parts += [columns_of(w_in[:, at[n] + m * PC:at[n] + (m + 1) * PC]) for n in "qkv"]
        loop_w.append(np.concatenate([v.reshape(P, -1) for v in parts], 1))
    d["loop_w"] = np.stack(loop_w)
    src = {"glu": x["w_glu"][0], "so": x["w_ssm_out"][0], "ao": x["w_attn_out"][0], "wo": x["w_o"][0]}
    for n in ("zs", "za", "rs", "ra"):
        src[n] = w_in[:, at[n]:]
    a_in, r_in = x["a_w_in_2"][0], x["r_w_in_2"][0]
    lora = QL + KVL + MR
    src.update(pu=a_in[:, lora:], ga=a_in[:, lora + D:], gb=a_in[:, lora + 2 * D:], rq=r_in, rk=r_in[:, D:], rv=r_in[:, 2 * D:],
               rg=r_in[:, 4 * D:])
    for n, w in (("o", x["a_w_out_2"][0]), ("t", x["r_w_out_2"][0])):
        src[n + "a"], src[n + "b"] = w[:D], w[D:]
    src["lo"] = a_in[:, :lora]
    uq = x["a_w_uq_2"][0].reshape(QL, MH, MN + MR)
    ukv = x["a_w_ukv_2"][0].reshape(KVL, MH, MN + MV)
    panels = []
    for kind, i in stage_plan():
        if kind == "uq":
            h = slice(2 * i, 2 * i + 2)
            rope = uq[:, h, MN:]
            swap = np.concatenate([rope[:, :, MR // 2:], rope[:, :, :MR // 2]], 2)
            q = np.concatenate([v.reshape(QL, -1) for v in (uq[:, h, :MN], rope, swap)], 1)
            kv = np.concatenate([ukv[:, h, :MN].reshape(KVL, -1), ukv[:, h, MN:].reshape(KVL, -1)], 1)
            panels.append(np.concatenate([columns_of(q).reshape(P, -1), kv], 1))
            continue
        v = columns_of(src[kind][:, i * 256:(i + 1) * 256]).reshape(P, -1)
        panels.append(np.pad(v, ((0, 0), (0, PANEL - v.shape[1]))))
    d["panels"] = np.stack(panels)
    lam = [x["lam_re"][0], x["lam_im"][0], np.repeat(x["log_dt"][0][:, None], NST, 1)]
    d["ssm_par"] = np.stack([v.reshape(NTILE, P).T for v in lam], 1)
    b = np.zeros((P, 2, NTILE, 2, GCH), np.float32)
    c = np.zeros((P, KT, 2, SPM, 2, GCH), np.float32)
    for n, (bx, cx) in enumerate(((x["b_re"][0], x["c_re"][0]), (x["b_im"][0], x["c_im"][0]))):
        b2 = bx.reshape(NTILE, 2, NST, GCH)
        c2 = cx.reshape(KT, SPM, 2, GCH, NST)
        for g in range(2):
            b[g * NST:(g + 1) * NST, n, :, g, :] = b2[:, g].transpose(1, 0, 2)
            c[g * NST:(g + 1) * NST, :, n, :, g, :] = c2[:, :, g].transpose(3, 0, 1, 2)
    d["ssm_b"] = b.reshape(P, 2, NTILE, 32)
    d["ssm_c"] = c.reshape(P, KT, 256)
    qk = [np.repeat(x[n][0], HEADS, 0).reshape(KT, PC) for n in ("q_norm_w", "k_norm_w")]
    d["qk_w"] = np.stack(qk, 1)
    d["pool_w"] = x["a_pool_w_2"][0].reshape(4, 2, P, 256).transpose(2, 0, 1, 3)
    d["positions_2"] = x["positions_2"].reshape(1, T)
    d["pos2"] = x["positions_2"].reshape(TT, P).T
    d["decays"] = np.concatenate([x["r_decay_fwd_2"], x["r_decay_bwd_2"]], 1)
    d["final_g"] = x["final_norm_g_2"].reshape(1, D)
    d["pos1"] = x["positions"].reshape(TT, P).T
    vec = {"norm_w": "norm_w", "d_skip": "d_skip", "a_norm": "a_norm_g_2", "q_norm": "a_q_norm_g_2",
           "kv_norm": "a_kv_norm_g_2", "pool_scale": "a_pool_scale_2", "r_norm": "r_norm_g_2", "gn": "r_gn_g_2"}
    cols = np.zeros((P, 64), np.float32)
    for n, at_ in COLS.items():
        v = x[vec[n]].reshape(-1, P).T
        cols[:, at_:at_ + v.shape[1]] = v
    d["cols"] = cols
    d.update(constants())
    return {n: np.ascontiguousarray(v) for n, v in d.items()}


def kernel(**inputs):
    import concourse.bacc as bacc
    from concourse.bass_utils import run_bass_kernel_spmd

    arrays = layout({n: np.asarray(v) for n, v in inputs.items()})
    nc = bacc.Bacc("TRN2", target_bir_lowering=False, num_devices=1)
    a = {n: nc.dram_tensor(n, v.shape, mybir.dt.from_np(v.dtype), kind="ExternalInput").ap() for n, v in arrays.items()}
    out = nc.dram_tensor("out", (1, T, D), f32, kind="ExternalOutput").ap()
    build(nc, a, out)
    r = run_bass_kernel_spmd(nc, [arrays], core_ids=[0])
    return r.results[0]["out"]
```

```python
import concourse.bass as bass
from concourse import mybir
from contextlib import ExitStack
import math
import numpy as np

f32, f32r = mybir.dt.float32, mybir.dt.float32r
ALU = mybir.AluOpType
ACT = mybir.ActivationFunctionType
AX = mybir.AxisListType

T, D, P = 512, 1024, 128
TT, KT = T // P, D // P
EPS = 1e-6
NEG = -1e30
ROUND = 12582912.0
PI2_A, PI2_B, PI2_C = 6.28125, 0.0019340515136718750, float(2 * math.pi - 6.28125 - 0.0019340515136718750)
TURN = float(np.float32(1.0 / (2 * math.pi)))
PI2_SAFE = 6.283185
PI_SAFE = 3.1415925
GROUPS, GCH, NST = 64, 16, 64
NTILE = GROUPS * NST // P
SPM = 4
PACKW = 512 + SPM * 96 + SPM
DIL = ((128, 1), (512, 4), (2048, 16))
HEADS, HD, NG = 8, 64, 3
NH = NG * HEADS
PH = NH // KT
PC = PH * HD
ROPE1 = 8
SCALE1 = 1.0 / math.sqrt(HD)
QL, KVL, MH, MN, MR, MV = 384, 128, 8, 128, 64, 128
SCALE2 = (MN + MR) ** -0.5
POOLS = (2, 4, 8, 16)
PAD = 8
RH, RK, RV = 4, 256, 512
DELTAS = T + 3 * P
LOOPW = KT * (P + 3 * PC)
ARENA = 53200
PANEL = 2048

COLS = {}
def _cols():
    n = 0
    for name, w in (("norm_w", 8), ("d_skip", 8), ("a_norm", 8), ("q_norm", 3), ("kv_norm", 1), ("pool_scale", 8),
                    ("r_norm", 8), ("gn", 16)):
        COLS[name] = n
        n += w
    return n
NCOLS = _cols()


HALVES = (5, 7)
MLA_STEPS, RET_STEPS = 26, 36


class Steps:

    def __init__(self, eng, sem):
        self.eng, self.sem, self.n, self.i, self.per, self.start = eng, sem, 0, None, 0, 0

    def __call__(self, ins):
        ins.then_inc(self.sem, 1)
        self.n += 1
        return self.n

    def wait(self, tok=None):
        tok = self.n if tok is None else tok
        self.eng.wait_ge(self.sem, tok if self.i is None else self.i * self.per + tok)

    def loop(self, i, per):
        self.i, self.per, self.start = i, per, self.n

    def end(self, count):
        assert self.n - self.start == self.per, f"steps per turn: {self.n - self.start}, said {self.per}"
        self.n = self.start + count * self.per
        self.i = None


def stage_plan():
    plan = []
    for i in range(4):
        plan += [("zs", i), ("glu", i)]
    for i in range(4):
        plan += [("rs", i), ("so", i)]
    plan += [("za", 0), ("za", 1)]
    for i in range(4):
        plan += [("ra", i), ("ao", i)]
    plan += [("wo", i) for i in range(4)]
    plan += [("lo", i) for i in range(3)]
    for i in range(4):
        plan += [("pu", i), ("gb", i)]
    for i in range(4):
        plan += [("uq", i), ("ga", i)]
    for i in range(4):
        plan += [("oa", i), ("ob", i)]
    for h in range(RH):
        plan += [("rq", h), ("rk", h), ("rv", 2 * h), ("rv", 2 * h + 1), ("rg", 2 * h), ("rg", 2 * h + 1)]
    for i in range(4):
        plan += [("ta", i), ("tb", i)]
    return plan


def build(nc, a, out, upto=99):
    ctx = ExitStack()
    with ctx:
        ctx.enter_context(nc.sbuf_tensor("arena", [P, ARENA], f32))
        base, placed = nc.sbuf_base - 4 * ARENA, {}
        ps = [ctx.enter_context(nc.psum_tensor(f"bank{b}", [P, 512], f32)) for b in range(8)]

        def sem(name):
            return ctx.enter_context(nc.semaphore(name))

        def at(off, *dims):
            return view("words", f32, off, dims)

        def parts_at(off, *dims):
            return view("parts", f32r, off, dims)

        def view(kind, dtype, off, dims):
            n, skip = int(np.prod(dims)), off % 8
            key = f"{kind}_{off}_{n}"
            if key not in placed:
                placed[key] = nc.alloc_sbuf_tensor_at(key, [P, skip + n], dtype, offset=base + 4 * (off - skip))
            v = placed[key][:, skip:skip + n]
            if len(dims) == 1:
                return v
            names = [f"d{k}" for k in range(len(dims))]
            return v.rearrange(f"p ({' '.join(names)}) -> p {' '.join(names)}",
                               **{m: d for m, d in zip(names[1:], dims[1:])})

        W = 0
        wl = at(W, LOOPW)
        w_u = wl[:, 0:KT * P].rearrange("p (k c) -> p k c", k=KT)
        w_x = [wl[:, KT * P + x * KT * PC:KT * P + (x + 1) * KT * PC].rearrange("p (k c) -> p k c", k=KT)
               for x in range(3)]
        raw = at(W, 2, PANEL)
        split_w = parts_at(4096, 2, 2, PANEL)
        o = LOOPW
        t_a = [at(o, 512), at(o + 512, 512)]; o += 1024
        u_cur = at(o, 512); o += 512
        qk_w = at(o, 2, PC); o += 2 * PC
        hT = at(8192, KT, T)
        QTOK, KTOK, VTOK, GT = 12288, 18432, 24576, 30720
        qkv_tok = [at(b, TT, NH * HD) for b in (QTOK, KTOK, VTOK)]
        gT = at(GT, KT, T)
        pack = at(34816, KT, PACKW)
        lhs_cur = at(42016, 4, P)
        E = at(42528, 2, 2, 512)
        e_t = [at(44576, 512), at(45088, 512)]
        bp = at(45600, 2, 512)
        gs = at(46624, 2, 512)
        hs = at(47648, 2, 2, 512)
        sq = at(49696, TT * PH, HD)
        y_sb = at(50464, 512)
        CB = 52300
        ident = at(CB, P)
        cols = at(CB + 128, 64)
        csA = at(CB + 192, 2, TT, ROPE1)
        rt = [at(CB + 256 + 96 * k, TT, PH, ROPE1) for k in range(4)]
        st = at(CB + 640, 160)
        half_m = st[:, 0:16]

        def col(name, k=0):
            return cols[:, COLS[name] + k:COLS[name] + k + 1]

        const_in = sem("const_in"); x_in = [sem(f"x_in{t}") for t in range(TT)]; par_in = sem("par_in"); ssm_in = sem("ssm_in")
        v_step = sem("v_step"); a_step = sem("a_step"); g_step = sem("g_step")
        x_sq = sem("x_sq"); x_ms = sem("x_ms"); x_rs = sem("x_rs"); x_nrm = sem("x_nrm")
        xt_mm = sem("xt_mm"); xt_ev = sem("xt_ev")
        ang_in = sem("ang_in"); trig_ready = sem("trig_ready"); ssm_exp = sem("ssm_exp"); ssm_dt = sem("ssm_dt")
        bb_ready = sem("bb_ready"); bt_mm = sem("bt_mm"); pack_ready = sem("pack_ready")
        wu_full = sem("wu_full"); wq_full = sem("wq_full"); wk_full = sem("wk_full"); wv_full = sem("wv_full")
        qkw_full = sem("qkw_full")
        u_mm = sem("u_mm"); q_mm = sem("q_mm"); k_mm = sem("k_mm"); v_mm = sem("v_mm")
        u_ev = sem("u_ev"); q_ev = sem("q_ev"); k_ev = sem("k_ev"); v_ev = sem("v_ev"); lhs_ready = sem("lhs_ready")
        bu_mm = sem("bu_mm"); bu_used = sem("bu_used"); c_mm = sem("c_mm"); h_ready = sem("h_ready")
        e_ready = sem("e_ready"); e_used = sem("e_used"); y_ready = sem("y_ready"); gelu_done = sem("gelu_done")
        ss_done = sem("ss_done"); ms_ready = sem("ms_ready"); rs_ready = sem("rs_ready"); scaled = sem("scaled")
        roped = sem("roped")
        w_full = [sem(f"w_full{s}") for s in range(2)]
        w_high = sem("w_high"); w_low = sem("w_low"); w_first = sem("w_first")
        h_split = sem("h_split"); g_high = sem("g_high"); g_low = sem("g_low"); nt_low = sem("nt_low")
        panel_mm = sem("panel_mm"); step_free = sem("step_free")
        mask_in = sem("mask_in"); g_ready = sem("g_ready")
        qg_ready = sem("qg_ready"); tr_mm = sem("tr_mm"); tr_ev = sem("tr_ev"); sc_mm = sem("sc_mm")
        sm_done = sem("sm_done"); nm_ready = sem("nm_ready"); p_ready = sem("p_ready"); pt_mm = sem("pt_mm")
        pt_ev = sem("pt_ev"); pv_mm = sem("pv_mm"); o_ev = sem("o_ev")
        glu_sig = sem("glu_sig"); sig_used = sem("sig_used"); ys_ready = sem("ys_ready"); m_ready = sem("m_ready")
        rs_sig = sem("rs_sig"); ot_mm = sem("ot_mm"); za_sig = sem("za_sig"); ya_ready = sem("ya_ready")
        ra_sig = sem("ra_sig"); xr_in = sem("xr_in"); x1_ready = sem("x1_ready")
        out_done = sem("out_done"); passed = sem("passed")

        plan = stage_plan()
        NP = len(plan)
        first_of = {}
        for n, (kind, i) in enumerate(plan):
            first_of.setdefault(kind, n)

        x_tok, xn_tok = at(QTOK, TT, D), at(KTOK, TT, D)
        ssp = at(49696, 24, 32)
        lr, li, ldt = ssp[:, 0, :], ssp[:, 1, :], ssp[:, 2, :]
        tv = at(50464, 48)
        b_nat = at(GT, 2, NTILE, 32)
        bbs = at(GT + 2048, 2, NTILE, 32)
        bt_tmp = at(44576, NTILE, 32)
        tw = [at(VTOK + 1536 * k, NTILE, 48) for k in range(4)]
        angA = at(46624, 4, TT, ROPE1)

        masks = at(34816, 1280)
        qg = at(36096, 6, TT, P)
        qkT = at(39168, 6, T)
        sm = at(42240, 2, 1280)
        pr = at(44800, 2, 1280)
        pT = at(47360, 10, P)
        o_tok = at(48640, TT, HEADS * HD)
        mx, nmx, den, rden = (at(50688 + 8 * k, n) for k, n in enumerate((2, 2, 8, 8)))
        def pair_at(off, kts):
            return parts_at(off, kts, T), parts_at(off + kts * T, kts, T)

        hS = pair_at(12288, KT)
        gS = pair_at(20480, KT)
        prod = at(28672, 4, T)
        yS = pair_at(35072, KT)
        sig = at(43264, 2, 4, T)
        mT = at(20480, KT, T)
        oS = pair_at(24576, 4)
        mS = pair_at(35072, KT)
        x_res = at(28672, TT, D)

        y2T = at(20480, 16, T)
        cosT, sinT = at(32768, 1152), at(33920, 1152)
        xn2 = at(35072, TT, D)
        upad = at(35072, 2, 2, T + 2 * PAD)
        win = at(37184, 2, 2, T + 2 * PAD)
        l_tok = at(39296, TT, QL + KVL)
        kr_tok = at(41344, TT, P)
        sig2 = at(41856, 2, 2, T)
        prod2 = at(43904, 2, T)
        pool_d = at(44928, 2, 2, T)
        cT = at(47360, 4, T)
        krT = at(49408, T)
        pool_w = at(49920, 4, 2, 256)
        ang, turns = at(47360, 1152), at(48512, 1152)
        cosR, sinR = cosT[:, 0:512], sinT[:, 0:512]
        cosM, sinM = cosT[:, 512:1024], sinT[:, 512:1024]
        cosK = cosT[:, 1024:1152].rearrange("p (t c) -> p t c", t=TT)
        sinK = sinT[:, 1024:1152].rearrange("p (t c) -> p t c", t=TT)
        delta = at(50944, DELTAS)
        decay = at(47360, RH, DELTAS)
        MB = CB + 256
        misc = at(MB, 99)
        corr = misc[:, 0:64].rearrange("p (i e) -> p i e", i=4)
        inv_cols = misc[:, 64:67]
        inv_row = misc[:, 67:99]
        pos2c = at(MB + 99, TT)
        dec = at(MB + 103, 8)
        lsg = at(MB + 111, 6, 8)
        pos2i = at(MB + 160, TT)
        st2 = at(MB + 164, 160)
        qnT, qrT, knT = at(35072, 2, T), at(36096, T), at(36608, 2, T)
        v_m = at(37632, TT, 256)
        p_m = at(38656, 3, T)
        rot = at(40192, 2, T)
        pT_m = at(41216, 2, 4, T)
        gate_m, sig_m = at(45312, 2, T), at(46336, 2, T)
        q_r, k_r = at(35072, 2, T), at(36096, 2, T)
        v_r = at(37120, TT, RV)
        sd = at(39168, TT, T)
        on = at(41216, TT, RV)
        rot_r = at(41216, 4, T)
        gate_r, sig_r = at(43264, 4, T), at(45312, 4, T)
        dt1, dt2 = at(35072, DELTAS), at(35072 + DELTAS, DELTAS)
        gain = at(35072, D)
        squares = at(37120, TT, D)

        misc_in = sem("misc_in"); pos_in = sem("pos_in"); ang2 = sem("ang2"); trig2 = sem("trig2"); tab2 = sem("tab2")
        n_sq = sem("n_sq"); n_ms = sem("n_ms"); n_rs = sem("n_rs"); n_nrm = sem("n_nrm"); nt_mm = sem("nt_mm")
        nt_ev = sem("nt_ev"); lo_sq = sem("lo_sq"); lo_ms = sem("lo_ms"); lo_rs = sem("lo_rs"); lo_ev = sem("lo_ev")
        kr_raw = sem("kr_raw"); kr_rot = sem("kr_rot"); ct_mm = sem("ct_mm"); ct_ev = sem("ct_ev")
        poolw_in = sem("poolw_in"); u_pad = sem("u_pad"); pads = sem("pads"); d_ready = sem("d_ready"); pool_mm = sem("pool_mm")
        gb_sig = sem("gb_sig"); y2_ready = sem("y2_ready")
        pr_mm = sem("pr_mm"); pr_ev = sem("pr_ev"); rot_done = sem("rot_done"); ga_mm = sem("ga_mm"); ga_sig = sem("ga_sig")
        ga_ready = sem("ga_ready"); ga_done = sem("ga_done"); s_mm = sem("s_mm"); nmax = sem("nmax"); e_done = sem("e_done"); rcp = sem("rcp")
        p_norm = sem("p_norm"); t_mm = sem("t_mm"); t_ev = sem("t_ev"); o_mm = sem("o_mm"); ym_ready = sem("ym_ready")
        delta_in = sem("delta_in"); dec_abs = sem("dec_abs"); dec_exp = sem("dec_exp"); dec_arg = sem("dec_arg")
        dec_ready = sem("dec_ready"); dec_in = sem("dec_in")
        x2_ready = sem("x2_ready"); rp_mm = sem("rp_mm"); rqk_rot = sem("rqk_rot"); v_cp = sem("v_cp"); rs_mm = sem("rs_mm")
        sd_ready = sem("sd_ready"); rg_mm = sem("rg_mm"); rg_sig = sem("rg_sig"); rg_ready = sem("rg_ready")
        ro_mm = sem("ro_mm"); var_ready = sem("var_ready"); rstd = sem("rstd"); on_ready = sem("on_ready")
        rt_mm = sem("rt_mm"); yr_ready = sem("yr_ready"); x3_ready = sem("x3_ready"); gain_in = sem("gain_in")
        f_nrm = sem("f_nrm"); f_out = sem("f_out")
        BLK1 = 30
        PU, UQ, OA, RQ, TA = (first_of[k] for k in ("pu", "uq", "oa", "rq", "ta"))

        NKEY = [min(i + 1, 2) + 2 * (i + 1) for i in range(TT)]
        CH = [(n + 3) // 4 for n in NKEY]
        CHU = [CH[u % 4] for u in range(8)]

        def key_blocks(i):
            return [(0, b) for b in range(max(i - 1, 0), i + 1)] + [(1, b) for b in range(i + 1)] + \
                   [(2, b) for b in range(i + 1)]

        whole = ("uq", "oa", "ob", "ta", "tb")
        is_split = [kind not in whole or n in (TA, TA + 1) for n, (kind, _) in enumerate(plan)]
        order = [sum(is_split[:n]) for n in range(NP)]
        splits = [n for n in range(NP) if is_split[n]]

        def width(n):
            kind, i = plan[n]
            return {"ao": 1024, "lo": KT * 64 if i == 2 else PANEL}.get(kind, PANEL)

        def full_at(n):
            return 16 * (n // 2 + 1)

        def high_part(act, n, r=None, per=0):
            k = order[n]
            if r is None:
                act.wait_ge(w_full[n % 2], full_at(n))
                act.wait_ge(panel_mm, splits[k - 2] + 1) if k >= 2 else None
            else:
                act.wait_ge(w_full[n % 2], r * (8 * per) + full_at(n))
                act.wait_ge(panel_mm, r * per + (splits[k - 2] + 1 if per == 12 else n - 1))
            w = width(n)
            nc.scalar.activation(split_w[:, k % 2, 0, 0:w], raw[:, n % 2, 0:w], ACT.Copy).then_inc(w_high, 1)

        def low_part(dve, n, r=None, per=0):
            k, w = order[n], width(n)
            c = {0: 0, 4: 2, 12: 12}[per]
            if r is None:
                dve.wait_ge(w_full[n % 2], full_at(n))
                dve.wait_ge(w_high, k)
            else:
                dve.wait_ge(w_full[n % 2], r * (8 * per) + full_at(n))
                dve.wait_ge(w_high, r * c + k)
            nc.vector.tensor_tensor(split_w[:, k % 2, 1, 0:w], raw[:, n % 2, 0:w], split_w[:, k % 2, 0, 0:w],
                                    ALU.subtract).then_inc(w_low, 1)

        def apart(eng):
            eng.sem_inc(passed, 1)

        block = ctx.enter_context(nc.Block())

        @block.sync
        def _(sp):
            sp.dma_start(ssp[:, 0:3, :], a["ssm_par"]).then_inc(par_in, 16)
            sp.dma_start(tv, a["c_t"]).then_inc(par_in, 16)
            sp.dma_start(ident, a["c_ident"]).then_inc(const_in, 16)
            sp.dma_start(cols, a["cols"]).then_inc(const_in, 16)
            sp.dma_start(angA[:, 0], a["c_angA"]).then_inc(const_in, 16)
            sp.dma_start(st[:, 20:24].bitcast(mybir.dt.int32), a["pos1"]).then_inc(const_in, 16)
            def turn(i):
                src = a["loop_w"][bass.ds(i, 1), :, :].rearrange("o p n -> (o p) n")
                for x, (full, done) in enumerate(((wq_full, q_mm), (wk_full, k_mm), (wv_full, v_mm))):
                    sp.wait_ge(done, i * 2 + 1)
                    b = KT * P + x * KT * PC
                    sp.dma_start(wl[:, b:b + KT * PC], src[:, b:b + KT * PC]).then_inc(full, 16)
                sp.wait_ge(scaled, i * 2 + 1)
                sp.dma_start(qk_w, a["qk_w"][bass.ds(i, 1)].rearrange("o x c -> o (x c)").to_broadcast([P, 2 * PC])
                             ).then_inc(qkw_full, 16)

            sp.dma_start(wl[:, 0:KT * P], a["loop_w"][0, :, 0:KT * P]).then_inc(wu_full, 16)
            sp.dma_start(b_nat, a["ssm_b"]).then_inc(ssm_in, 16)
            sp.dma_start(pack[:, :, 256:512], a["ssm_c"]).then_inc(ssm_in, 16)
            with sp.Fori(0, KT - 1) as i:
                turn(i)
                sp.wait_ge(u_mm, i + 2)
                sp.dma_start(wl[:, 0:KT * P], a["loop_w"][bass.ds(i + 1, 1), :, 0:KT * P].rearrange("o p n -> (o p) n")
                             ).then_inc(wu_full, 16)
            turn(KT - 1)
            sp.wait_ge(gelu_done, KT + 1)
            sp.dma_start(masks, a["c_masks"]).then_inc(mask_in, 16)
            sp.wait_ge(v_mm, 2 * KT + 1)
            for n in range(NP):
                if upto == 1 and n == BLK1 or upto == 2 and n == RQ:
                    break
                if RQ <= n < TA:
                    if n > RQ:
                        continue
                    sp.wait_ge(panel_mm, RQ)
                    with sp.Fori(0, 2) as r:
                        for k in range(12):
                            sp.wait_ge(w_low, r * 12 + (order[RQ] + k - 2))
                            sp.dma_start(raw[:, (RQ + k) % 2, :], a["panels"][bass.ds(r * 12 + (RQ + k), 1), :, :]
                                         .rearrange("o p n -> (o p) n")).then_inc(w_full[(RQ + k) % 2], 16)
                    continue
                if n == 2:
                    sp.wait_ge(w_first, 2)
                elif n > 2 and is_split[n - 2]:
                    sp.wait_ge(w_low, order[n - 2])
                if n > 2 and plan[n - 2][0] in whole:
                    sp.wait_ge(panel_mm, n - 1)
                if plan[n] == ("wo", 3):
                    sp.wait_ge(m_ready, 16)
                    sp.dma_start(x_res, a["x"].rearrange("o (t p) d -> p (o t) d", p=P)).then_inc(xr_in, 16)
                if n == first_of["ra"] + 2:
                    sp.wait_ge(ya_ready, 4)
                    sp.dma_start(misc, a["c_misc"]).then_inc(misc_in, 16)
                    sp.dma_start(pos2i.bitcast(mybir.dt.int32), a["pos2"]).then_inc(misc_in, 16)
                    sp.dma_start(dec, a["decays"].to_broadcast([P, 8])).then_inc(dec_in, 16)
                    sp.dma_start(turns[:, 0:T].bitcast(mybir.dt.int32), a["positions_2"].to_broadcast([P, T])).then_inc(pos_in, 16)
                    sp.dma_start(pool_w, a["pool_w"]).then_inc(poolw_in, 16)
                if n == UQ + 3:
                    sp.wait_ge(pool_mm, 4)
                    sp.dma_start(delta, a["c_delta"]).then_inc(delta_in, 16)
                w = width(n)
                sp.dma_start(raw[:, n % 2, 0:w], a["panels"][n, :, 0:w]).then_inc(w_full[n % 2], 16)
            if upto == 1:
                sp.wait_ge(x1_ready, 8)
                sp.dma_start(out.rearrange("o (t p) d -> p (o t) d", p=P), x_res).then_inc(out_done, 16)
                sp.wait_ge(out_done, 16)
                return
            if upto != 2:
                sp.wait_ge(ro_mm, 17)
                sp.wait_ge(rqk_rot, 8)
                sp.dma_start(gain, a["final_g"].to_broadcast([P, D])).then_inc(gain_in, 16)
            if upto == 2:
                sp.wait_ge(x2_ready, 16)
                sp.dma_start(out.rearrange("o (t p) d -> p (o t) d", p=P), x_res).then_inc(out_done, 16)
                sp.wait_ge(out_done, 16)
                return
            for t in range(TT):
                sp.wait_ge(f_out, t + 1)
                sp.dma_start(out[0, t * P:(t + 1) * P, :], x_res[:, t, :]).then_inc(out_done, 16)
            sp.wait_ge(out_done, 16 * TT)

        @block.tensor
        def _(pe):
            mm = nc.tensor.matmul
            for first in (u_mm, q_mm, k_mm, v_mm, c_mm, tr_mm, sc_mm, pt_mm, pv_mm, s_mm, t_mm, o_mm, ro_mm):
                pe.sem_inc(first, 1)
            pe.wait_ge(const_in, 64)
            for k in range(KT):
                if k == 0:
                    pe.wait_ge(x_nrm, TT)
                for t in range(TT):
                    last = nc.tensor.transpose(ps[k][:, t * P:(t + 1) * P], xn_tok[:, t, k * P:(k + 1) * P], ident)
                last.then_inc(xt_mm, 1)
            def input_matrices():
                pe.wait_ge(bb_ready, 2)
                for m in range(KT):
                    for c in range(2):
                        last = nc.tensor.transpose(ps[3 + m // 2][:, (m % 2) * 256 + c * P:(m % 2) * 256 + (c + 1) * P],
                                                   bbs[:, c, 4 * m:4 * m + 4, :].rearrange("p a b -> p (a b)"), ident)
                    if m % 2:
                        last.then_inc(bt_mm, 1)
                pe.wait_ge(pack_ready, KT // 2)

            def qkv(i, x, half, full, bank, done):
                if half == 0:
                    pe.wait_ge(full, i * 16 + 16)
                for t in (2 * half, 2 * half + 1):
                    for k in range(KT):
                        last = mm(ps[bank][:, (t % 2) * PC:(t % 2 + 1) * PC], hT[:, k, t * P:(t + 1) * P], w_x[x][:, k, :],
                                  start=(k == 0), stop=(k == KT - 1))
                last.then_inc(done, 1)

            def bu(i, j):
                if j == 0:
                    pe.wait_ge(u_ev, i + 1 + 1)
                    pe.wait_ge(lhs_ready, i + 1)
                pe.wait_ge(bu_used, i * 4 + j + 1)
                r = slice(32 * j, 32 * j + 32)
                for c in range(2):
                    last = mm(ps[5 + c][:, :], lhs_cur[r, c, :], u_cur[r, :], start=True, stop=True)
                last.then_inc(bu_mm, 1)

            def cy(i, j):
                pe.wait_ge(h_ready, i * 4 + (j + 1))
                if j == 0:
                    pe.wait_ge(y_ready, i + 1)
                for c in range(2):
                    last = mm(ps[7][32 * j:32 * j + 32, :], lhs_cur[:, 2 + c, 32 * j:32 * j + 32], hs[:, j % 2, c, :],
                              start=(c == 0), stop=(c == 1))
                last.then_inc(c_mm, 1)

            def channels(i):
                pe.wait_ge(wu_full, i * 16 + 16)
                pe.wait_ge(u_ev, i + 1)
                for k in range(KT):
                    last = mm(ps[0][:, :], w_u[:, k, :], hT[:, k, :], start=(k == 0), stop=(k == KT - 1))
                last.then_inc(u_mm, 1)

            def turn(i, more, first=False):
                pe.wait_ge(v_ev, i * 2 + 1)
                qkv(i, 0, 0, wq_full, 1, q_mm)
                if first:
                    qkv(i, 0, 1, wq_full, 2, q_mm)
                    input_matrices()
                bu(i, 0)
                if not first:
                    qkv(i, 0, 1, wq_full, 2, q_mm)
                bu(i, 1)
                pe.wait_ge(k_ev, i * 2 + 1)
                qkv(i, 1, 0, wk_full, 3, k_mm)
                cy(i, 0)
                bu(i, 2)
                qkv(i, 1, 1, wk_full, 4, k_mm)
                cy(i, 1)
                bu(i, 3)
                pe.wait_ge(q_ev, i * 2 + 3)
                qkv(i, 2, 0, wv_full, 1, v_mm)
                cy(i, 2)
                qkv(i, 2, 1, wv_full, 2, v_mm)
                if more:
                    channels(i + 1)
                cy(i, 3)

            pe.wait_ge(xt_ev, KT)
            channels(0)
            turn(0, True, first=True)
            with pe.Fori(1, KT - 1) as i:
                turn(i, True)
            turn(KT - 1, False)

            def heads_t(p, x):
                if x == 0:
                    pe.wait_ge(qg_ready, p + 1)
                    pe.wait_ge(sm_done, p * 8 + 1)
                if x >= 3:
                    pe.wait_ge(tr_ev, p * 6 + (x - 2))
                for t in range(TT):
                    last = nc.tensor.transpose(ps[x % 3][:, t * P:(t + 1) * P], qg[:, x, t, :], ident)
                last.then_inc(tr_mm, 1)

            def head_pair(p, more):
                pe.wait_ge(tr_ev, p * 6 + 6)

                def scores(u):
                    hh, i = u // 4, u % 4
                    r = slice(64 * hh, 64 * hh + 64)
                    pe.wait_ge(sm_done, p * 8 + u + 1)
                    lo = max(i - 1, 0) * P
                    q = slice(i * P, (i + 1) * P)
                    mm(ps[0][:, 0:(i + 1) * P - lo], qkT[r, 0, q], qkT[r, 3, lo:(i + 1) * P], start=True, stop=True)
                    for g in (1, 2):
                        last = mm(ps[g][:, 0:(i + 1) * P], qkT[r, g, q], qkT[r, 3 + g, 0:(i + 1) * P], start=True, stop=True)
                    last.then_inc(sc_mm, 1)

                def probs_t(u):
                    pe.wait_ge(p_ready, p * 8 + (u + 2))
                    pe.wait_ge(pt_ev, p * sum(CHU) + sum(CHU[:u]) + 1)
                    n = NKEY[u % 4]
                    for c in range(CHU[u]):
                        for b in range(4 * c, min(4 * c + 4, n)):
                            last = nc.tensor.transpose(ps[3 + c][:, (b % 4) * P:(b % 4 + 1) * P],
                                                       pr[:, u % 2, b * P:(b + 1) * P], ident)
                        last.then_inc(pt_mm, 1)

                def pv(u):
                    hh, i = u // 4, u % 4
                    pe.wait_ge(pt_ev, p * sum(CHU) + sum(CHU[:u + 1]) + 1)
                    pe.wait_ge(o_ev, p * 8 + max(u - 1, 0) + 1)
                    blocks = key_blocks(i)
                    for b, (g, kt) in enumerate(blocks):
                        c0 = p * 128 + g * HEADS * HD
                        last = mm(ps[6 + u % 2][:, 0:P], pT[:, b, :], qkv_tok[2][:, kt, bass.ds(c0, P)],
                                  start=(b == 0), stop=(b == len(blocks) - 1))
                    last.then_inc(pv_mm, 1)

                scores(0)
                scores(1)
                for u in range(8):
                    if u < 6:
                        scores(u + 2)
                    probs_t(u)
                    if u >= 1:
                        pv(u - 1)
                    if more and u >= 6:
                        for x in range(3 * (u - 6), 3 * (u - 5)):
                            heads_t(p + 1, x)
                pv(7)

            for x in range(6):
                heads_t(0, x)
            with pe.Fori(0, 3) as p:
                head_pair(p, True)
            head_pair(3, False)

            def mm3(dst, lhs, rhs, start, stop):
                mm(dst, lhs[0], rhs[0], start=start, stop=False)
                mm(dst, lhs[0], rhs[1], start=False, stop=False)
                return mm(dst, lhs[1], rhs[0], start=False, stop=stop)

            def parts(slot, kts):
                w = kts if isinstance(kts, tuple) else (kts, 256)
                return [split_w[:, slot, h, 0:w[0] * w[1]].rearrange("p (k c) -> p k c", k=w[0]) for h in range(2)]

            def split_panel(n, kts):
                if n == 0:
                    pe.wait_ge(w_first, 2)
                else:
                    pe.wait_ge(w_low, order[n])
                return parts(order[n] % 2, kts)

            def panel(n, bank0, x):
                kts = 4 if plan[n][0] == "ao" else 8
                w = split_panel(n, kts)
                for h in range(2):
                    for k in range(kts):
                        last = mm3(ps[bank0 + h][:, :], [v[:, k, h * P:(h + 1) * P] for v in w], [v[:, k, :] for v in x],
                                   start=(k == 0), stop=(k == kts - 1))
                last.then_inc(panel_mm, 1)

            def token_panel(n, bank0, x, k0, first, last_one):
                w = split_panel(n, (4, 512))
                for t in range(TT):
                    for k in range(4):
                        last = mm3(ps[bank0 + t][:, :], [v[:, k0 + k, t * P:(t + 1) * P] for v in x], [v[:, k, :] for v in w],
                                   start=(first and k == 0), stop=(last_one and k == 3))
                last.then_inc(panel_mm, 1)

            pe.wait_ge(o_ev, 33)
            pe.wait_ge(sm_done, 33)
            pe.wait_ge(h_split, 2)
            for s in range(15):
                b = 4 * (s % 2)
                pe.wait_ge(step_free, s + 1)
                if s < 13:
                    x = (hS, gS) if s < 4 else (hS, yS) if s < 8 else (hS, hS) if s == 8 else (hS, oS)
                    if s == 9:
                        pe.wait_ge(ya_ready, 2)
                    panel(2 * s, b, x[0])
                    if s == 0:
                        pe.wait_ge(g_low, 2)
                    if s == 4:
                        pe.wait_ge(ys_ready, 8)
                    if s == 9:
                        pe.wait_ge(ya_ready, 4)
                    if s == 8:
                        pe.wait_ge(step_free, 10)
                        for c in range(4):
                            for t in range(TT):
                                last = nc.tensor.transpose(ps[4 + c][:, t * P:(t + 1) * P], o_tok[:, t, c * P:(c + 1) * P], ident)
                            last.then_inc(ot_mm, 1)
                    panel(2 * s + 1, b + 2, x[1])
                else:
                    for h in range(2):
                        pe.wait_ge(m_ready, 8 + 4 * (h + 1))
                        token_panel(2 * s + h, b, mS, 4 * h, h == 0, h == 1)

            if upto == 1:
                return

            def transposes(t0, x, evac, n0):
                pe.wait_ge(n_nrm, t0 + TT)
                for k in range(KT):
                    if n0:
                        pe.wait_ge(evac, n0 - KT + k + 1)
                    for t in range(TT):
                        last = nc.tensor.transpose(ps[k][:, t * P:(t + 1) * P], x[:, t, k * P:(k + 1) * P], ident)
                    last.then_inc(nt_mm, 1)
                pe.wait_ge(nt_low, n0 + KT)

            transposes(0, xn2, nt_low, 0)

            def slot(n):
                pe.wait_ge(w_full[n % 2], full_at(n))
                return raw[:, n % 2, :]

            n = first_of["lo"]
            for x, (bank, cols_of) in enumerate(((4, 256), (6, 256), (0, 64))):
                w = split_panel(n + x, (KT, cols_of))
                for t in range(TT):
                    c0 = (t * cols_of) % 512
                    for k in range(KT):
                        last = mm3(ps[bank + t * cols_of // 512][:, c0:c0 + cols_of],
                                   [v[:, k, t * P:(t + 1) * P] for v in hS], [v[:, k, :] for v in w],
                                   start=(k == 0), stop=(k == KT - 1))
                last.then_inc(panel_mm, 1)

            def pool_product(i):
                b = 4 * (i % 2)
                pe.wait_ge(d_ready, i + 1)
                for c in range(2):
                    for k in range(2):
                        last = mm(ps[b + c][:, :], pool_w[:, i, k, c * P:(c + 1) * P], pool_d[:, i % 2, k, :],
                                  start=(k == 0), stop=(k == 1))
                last.then_inc(pool_mm, 1)

            pe.wait_ge(poolw_in, 16)
            for i in range(4):
                b = 4 * (i % 2)
                if i == 0:
                    pe.wait_ge(kr_raw, 1)
                if i == 1:
                    pe.wait_ge(lo_ev, 12)
                    for k in range(4):
                        for t in range(TT):
                            last = nc.tensor.transpose(ps[4 + k][:, t * P:(t + 1) * P], l_tok[:, t, k * P:(k + 1) * P], ident)
                        last.then_inc(ct_mm, 1)
                    pe.wait_ge(ct_ev, 1)
                    pe.wait_ge(kr_rot, 2)
                    for t in range(TT):
                        last = nc.tensor.transpose(ps[4][:, t * P:(t + 1) * P], kr_tok[:, t, :], ident)
                    last.then_inc(ct_mm, 1)
                    pe.wait_ge(ct_ev, 5)
                if i >= 2:
                    pe.wait_ge(step_free, 16 + i + 1)
                panel(PU + 2 * i, b, hS)
                if i >= 1:
                    pool_product(i - 1)
                panel(PU + 2 * i + 1, b + 2, hS)
            pool_product(3)

            with pe.Fori(0, 2) as r:
                for q in range(2):
                    def cnt(c, k):
                        return r * (2 * c) + (q * c + k)

                    n = UQ + 2 * q
                    if q == 0:
                        pe.wait_ge(step_free, 22)
                    pe.wait_ge(ym_ready, cnt(2, 0) + 1)
                    pe.wait_ge(t_ev, cnt(8, 0) + 1)
                    pe.wait_ge(w_full[n % 2], r * 32 + full_at(n))
                    w = raw[:, n % 2, 0:3 * 512].rearrange("p (k c) -> p k c", k=3)
                    wkv = raw[:, n % 2, 3 * 512:2048]
                    for c in range(4):
                        for k in range(3):
                            last = mm(ps[c][:, :], w[:, k, c * P:(c + 1) * P], cT[:, k, :], start=(k == 0), stop=(k == 2))
                        last.then_inc(pr_mm, 1)
                    for c in range(2):
                        pe.wait_ge(pr_ev, cnt(6, c + 1))
                        mm(ps[c][:, :], wkv[:, c * P:(c + 1) * P], cT[:, 3, :], start=True, stop=True).then_inc(pr_mm, 1)
                    pe.wait_ge(rot_done, cnt(1, 1))
                    for h in range(2):
                        for t in range(2 * h, 2 * h + 2):
                            last = mm(ps[2 + h][:, (t % 2) * 256:(t % 2 + 1) * 256], cT[:, 3, t * P:(t + 1) * P],
                                      wkv[:, 256:512], start=True, stop=True)
                        if h == 0:
                            last.then_inc(pr_mm, 1)
                    last.then_inc(panel_mm, 1)

                    def s_block(u):
                        h, i = u // 4, u % 4
                        if u < 3:
                            pe.wait_ge(e_done, cnt(8, 0) + 1)
                        else:
                            pe.wait_ge(e_done, cnt(8, u - 2) + 1)
                        b = 4 + u % 3
                        qs = slice(i * P, (i + 1) * P)
                        hr = slice(64 * h, 64 * h + 64)
                        mm(ps[b][:, :], qnT[:, h, qs], knT[:, h, :], start=True, stop=False)
                        mm(ps[b][:, :], qrT[hr, qs], krT[hr, :], start=False, stop=True).then_inc(s_mm, 1)

                    def t_block(u):
                        b = (7, 0)[u % 2]
                        pe.wait_ge(p_norm, cnt(8, u + 2))
                        if u >= 2:
                            pe.wait_ge(t_ev, cnt(8, u - 1) + 1)
                        for k in range(4):
                            last = nc.tensor.transpose(ps[b][:, k * P:(k + 1) * P], p_m[:, u % 3, k * P:(k + 1) * P], ident)
                        last.then_inc(t_mm, 1)

                    def o_block(h):
                        pe.wait_ge(t_ev, cnt(8, 4 * h + 4) + 1)
                        for k in range(4):
                            last = mm(ps[2 + h][:, :], v_m[:, k, h * P:(h + 1) * P], pT_m[:, h, k, :],
                                      start=(k == 0), stop=(k == 3))
                        last.then_inc(o_mm, 1)

                    pe.wait_ge(pr_ev, cnt(6, 4))
                    s_block(0)
                    s_block(1)
                    pe.wait_ge(w_low, r * 2 + order[n + 1])
                    w = parts(order[n + 1] % 2, KT)
                    for c in range(2):
                        for k in range(KT):
                            last = mm3(ps[c][:, :], [v[:, k, c * P:(c + 1) * P] for v in w], [v[:, k, :] for v in hS],
                                       start=(k == 0), stop=(k == KT - 1))
                    last.then_inc(panel_mm, 1)
                    s_block(2)
                    t_block(0)
                    pe.wait_ge(ga_ready, cnt(2, 2))
                    for u in range(1, 8):
                        if u < 6:
                            s_block(u + 2)
                        t_block(u)
                        if u == 5:
                            pe.wait_ge(pr_ev, cnt(6, 6))
                            o_block(0)
                    o_block(1)

            def residual(n, s, y, ready):
                b = 4 * (s % 2)
                pe.wait_ge(step_free, s + 1)
                for half in range(2):
                    w = slot(n + half).rearrange("p (k c) -> p k c", k=8)
                    for t in range(TT):
                        for k in range(8):
                            last = mm(ps[b + t][:, 0:256], y[:, 8 * half + k, t * P:(t + 1) * P], w[:, k, :],
                                      start=(half == 0 and k == 0), stop=(half == 1 and k == 7))
                    last.then_inc(panel_mm, 1)

            pe.wait_ge(ym_ready, 9)
            pe.wait_ge(y2_ready, 8)
            for i in range(4):
                residual(OA + 2 * i, 20 + i, y2T, None)
            if upto == 2:
                return

            transposes(TT, xn2, nt_low, KT)
            with pe.Fori(0, 2) as r:
                for q in range(2):
                    def cnt(c, k):
                        return r * (2 * c) + (q * c + k)

                    def rpanel(x, kts):
                        n = RQ + 6 * q + x
                        pe.wait_ge(w_low, r * 12 + order[n])
                        return parts(order[n] % 2, kts)

                    def feature(x, bank):
                        w = rpanel(x, KT)
                        for c in range(2):
                            for k in range(KT):
                                last = mm3(ps[bank + c][:, :], [v[:, k, c * P:(c + 1) * P] for v in w],
                                           [v[:, k, :] for v in hS], start=(k == 0), stop=(k == KT - 1))
                        last.then_inc(panel_mm, 1)

                    pe.wait_ge(on_ready, cnt(4, 0) + 1)
                    feature(0, 0)
                    pe.wait_ge(rg_ready, cnt(4, 0) + 1)
                    feature(1, 2)
                    pe.wait_ge(yr_ready, cnt(4, 0) + 1)
                    for x in range(2):
                        w = rpanel(2 + x, (4, 512))
                        for t in range(TT):
                            for k in range(4):
                                last = mm3(ps[4 + t][:, :], [v[:, 4 * x + k, t * P:(t + 1) * P] for v in hS],
                                           [v[:, k, :] for v in w], start=(x == 0 and k == 0), stop=(x == 1 and k == 3))
                        last.then_inc(panel_mm, 1)
                    pe.wait_ge(rqk_rot, cnt(2, 2))
                    for j in range(TT):
                        for k in range(2):
                            last = mm(ps[j][:, :], k_r[:, k, j * P:(j + 1) * P], q_r[:, k, :], start=(k == 0), stop=(k == 1))
                        last.then_inc(rs_mm, 1)
                    pe.wait_ge(v_cp, cnt(4, 2))
                    feature(4, 4)
                    pe.wait_ge(v_cp, cnt(4, 4))
                    pe.wait_ge(sd_ready, cnt(4, 4))
                    for i in range(TT):
                        b = (6, 7, 0, 1)[i]
                        for j in range(TT):
                            last = mm(ps[b][:, :], sd[:, j, i * P:(i + 1) * P], v_r[:, j, :], start=(j == 0), stop=(j == 3))
                        last.then_inc(ro_mm, 1)
                    feature(5, 2)
                    pe.wait_ge(rg_ready, cnt(4, 2) + 1)
                    for i in range(TT):
                        pe.wait_ge(on_ready, cnt(4, i + 2))
                        for c in range(4):
                            last = nc.tensor.transpose(ps[4 + i][:, c * P:(c + 1) * P], on[:, i, c * P:(c + 1) * P], ident)
                        last.then_inc(rt_mm, 1)

            pe.wait_ge(yr_ready, 17)
            for i in range(4):
                residual(TA + 2 * i, 24 + i, y2T, None)

        @block.scalar
        def _(act):
            S = Steps(act, a_step)
            for first in (u_ev, q_ev, k_ev, v_ev, gelu_done, p_ready, pt_ev, e_done, t_ev):
                act.sem_inc(first, 1)
            av = nc.scalar.activation
            for t in range(TT):
                act.dma_start(x_tok[:, t, :], a["x"][0, t * P:(t + 1) * P, :]).then_inc(x_in[t], 16)
            act.wait_ge(par_in, 32)
            av(ssp[:, 3, :], ldt, ACT.Exp).then_inc(ssm_exp, 1)
            act.wait_ge(ssm_dt, 1)
            av(ssp[:, 5, :], ssp[:, 4, :], ACT.Exp).then_inc(ssm_exp, 1)
            for t in range(TT):
                act.wait_ge(x_in[t], 16)
                av(xn_tok[:, t, :], x_tok[:, t, :], ACT.Square, accum_out=st[:, 24 + t:25 + t]).then_inc(x_sq, 1)
            act.wait_ge(x_rs, 1)
            act.wait_ge(x_sq, TT)
            for t in range(TT):
                av(xn_tok[:, t, :], x_tok[:, t, :], ACT.Copy, scale=st[:, 32 + t:33 + t]).then_inc(x_nrm, 1)
            for k in range(KT):
                act.wait_ge(xt_mm, k + 1)
                av(hT[:, k, :], ps[k][:, :], ACT.Copy, scale=col("norm_w", k)).then_inc(xt_ev, 1)
            act.wait_ge(ang_in, 1)
            av(tw[1], tw[0], ACT.Sin, scale=PI2_SAFE)
            av(tw[2], tw[0], ACT.Sin, scale=PI_SAFE).then_inc(trig_ready, 1)
            act.wait_ge(ang_in, 2)
            av(angA[:, 1], angA[:, 3], ACT.Sin, scale=PI2_SAFE)
            av(angA[:, 2], angA[:, 3], ACT.Sin, scale=PI_SAFE).then_inc(trig_ready, 1)

            def split(x, i, half, bank, done, evac):
                act.wait_ge(done, i * 2 + (half + 2))
                src = ps[bank][:, 0:2 * PC].rearrange("p (t c) -> p t c", t=2)
                dst = qkv_tok[x][:, 2 * half:2 * half + 2, bass.ds(i * PC, PC)]
                if x == 2:
                    av(dst, src, ACT.Copy).then_inc(evac, 1)
                    return
                av(dst, src, ACT.Copy)
                if half == 0:
                    act.wait_ge(ss_done, i * 2 + x + 1)
                av(sq[:, 2 * half * PH:(2 * half + 2) * PH, :].rearrange("p a b -> p (a b)"), ps[bank][:, 0:2 * PC],
                   ACT.Square).then_inc(evac, 1)

            for m in range(KT // 2):
                act.wait_ge(bt_mm, m + 1)
                av(pack[:, 2 * m:2 * m + 2, 0:256], ps[3 + m][:, :].rearrange("p (m c) -> p m c", m=2), ACT.Copy).then_inc(pack_ready, 1)
            act.wait_ge(pack_ready, KT // 2)
            act.wait_ge(bb_ready, 3)
            with act.Fori(0, KT) as i:
                act.wait_ge(u_mm, i + 1 + 1)
                act.wait_ge(y_ready, i + 1)
                av(u_cur, ps[0][:, :], ACT.Copy).then_inc(u_ev, 1)
                act.wait_ge(c_mm, i * 4 + 1)
                av(lhs_cur.rearrange("p a b -> p (a b)"), pack[:, bass.ds(i, 1), 0:512].rearrange("p o n -> p (o n)"),
                   ACT.Copy).then_inc(lhs_ready, 1)
                split(0, i, 0, 1, q_mm, q_ev)
                split(0, i, 1, 2, q_mm, q_ev)
                split(1, i, 0, 3, k_mm, k_ev)
                split(1, i, 1, 4, k_mm, k_ev)
                split(2, i, 0, 1, v_mm, v_ev)
                split(2, i, 1, 2, v_mm, v_ev)
                act.wait_ge(y_ready, i + 1 + 1)
                av(gT[:, bass.ds(i, 1), :].rearrange("p o n -> p (o n)"), y_sb, ACT.Gelu_apprx_tanh).then_inc(gelu_done, 1)

            act.wait_ge(gelu_done, KT + 1)
            act.wait_ge(y_ready, KT + 1)
            for x in range(6):
                act.wait_ge(roped, 2 * KT - 1 + x // 3)
                ins = av(qg[:, x], qkv_tok[x // 3][:, :, (x % 3) * 512:(x % 3) * 512 + P], ACT.Copy)
            ins.then_inc(qg_ready, 1)
            def heads_evac(p, x):
                if x == 0:
                    act.wait_ge(sc_mm, p * 8 + 1)
                act.wait_ge(tr_mm, p * 6 + (x + 2))
                av(qkT[:, x, :], ps[x % 3][:, :], ACT.Copy).then_inc(tr_ev, 1)

            def head_pair(p, more):
                def exps(u):
                    act.wait_ge(nm_ready, p * 8 + (u + 1))
                    if u >= 2:
                        act.wait_ge(pt_mm, p * sum(CHU) + sum(CHU[:u - 1]) + 1)
                    if u < 2:
                        act.wait_ge(pt_mm, p * sum(CHU) + 1)
                    if u == 0:
                        act.wait_ge(o_ev, p * 8 + 1)
                    n = NKEY[u % 4] * P
                    av(pr[:, u % 2, 0:n], sm[:, u % 2, 0:n], ACT.Exp, bias=nmx[:, u % 2:u % 2 + 1],
                       accum_out=den[:, u:u + 1]).then_inc(p_ready, 1)

                def probs_evac(u):
                    act.wait_ge(pv_mm, p * 8 + u + 1)
                    for c in range(CHU[u]):
                        n = min(4, NKEY[u % 4] - 4 * c)
                        act.wait_ge(pt_mm, p * sum(CHU) + (sum(CHU[:u]) + c + 1) + 1)
                        av(pT[:, 4 * c:4 * c + n, :].rearrange("p a b -> p (a b)"), ps[3 + c][:, 0:n * P],
                           ACT.Copy).then_inc(pt_ev, 1)

                exps(0)
                for u in range(8):
                    if u < 7:
                        exps(u + 1)
                    probs_evac(u)
                    if more and u >= 6:
                        for x in range(3 * (u - 6), 3 * (u - 5)):
                            heads_evac(p + 1, x)

            for x in range(6):
                heads_evac(0, x)
            with act.Fori(0, 3) as p:
                head_pair(p, True)
            head_pair(3, False)

            act.wait_ge(sm_done, 33)
            act.wait_ge(o_ev, 33)
            gR = gT.rearrange("p a b -> p (a b)")
            for h in range(2):
                av(gS[0][:, 4 * h:4 * h + 4, :].rearrange("p a b -> p (a b)"), gR[:, 2048 * h:2048 * h + 2048], ACT.Copy).then_inc(g_high, 1)
            act.wait_ge(h_split, 2)
            high_part(act, 1)
            for s in range(13):
                act.wait_ge(step_free, s + 1)
                b = 4 * (s % 2)
                sg = sig[:, s % 2]
                if s < 4 or s == 8:
                    for c in range(4):
                        if c % 2 == 0:
                            act.wait_ge(panel_mm, 2 * s + 1 + c // 2)
                            high_part(act, 2 * s + 2 + c // 2)
                        av(sg[:, c, :], ps[b + c][:, :], ACT.Sigmoid).then_inc(glu_sig, 1)
                else:
                    for c in range(2):
                        act.wait_ge(panel_mm, 2 * s + 1)
                        if c == 0:
                            high_part(act, 2 * s + 2)
                        av(sg[:, c, :], ps[b + c][:, :], ACT.Sigmoid).then_inc(rs_sig, 1)
                    high_part(act, 2 * s + 3)
                if s == 10:
                    act.wait_ge(ang2, 1)
                    av(sinT, ang, ACT.Sin, scale=PI2_SAFE)
                    av(cosT, ang, ACT.Sin, scale=PI_SAFE).then_inc(trig2, 1)
            if upto == 1:
                return
            for n in (28, 29, 30):
                high_part(act, n)

            def norm(t0, ready, count, cname, ahead):
                for t in range(TT):
                    act.wait_ge(ready, count)
                    av(xn2[:, t, :], x_res[:, t, :], ACT.Square, accum_out=st2[:, 8 + t:9 + t]).then_inc(n_sq, 1)
                for n in ahead:
                    high_part(act, n)
                act.wait_ge(n_rs, t0 // TT + 1)
                act.wait_ge(n_sq, t0 + TT)
                for t in range(TT):
                    av(xn2[:, t, :], x_res[:, t, :], ACT.Copy, scale=st2[:, 16 + t:17 + t]).then_inc(n_nrm, 1)
                for k in range(KT):
                    act.wait_ge(nt_mm, 2 * t0 + k + 1)
                    av(hS[0][:, k, :], ps[k][:, :], ACT.Copy, scale=col(cname, k)).then_inc(nt_ev, 1)

            norm(0, x1_ready, 8, "a_norm", (31,))
            n = first_of["lo"]
            for h in range(2):
                act.wait_ge(panel_mm, n + 1 + h)
                high_part(act, n + 2 + h)
                for t in range(TT):
                    src = ps[4 + 2 * h + t // 2][:, (t % 2) * 256:(t % 2 + 1) * 256]
                    if h == 0:
                        av(l_tok[:, t, 0:256], src, ACT.Square, accum_out=st2[:, 32 + t:33 + t]).then_inc(lo_sq, 1)
                    else:
                        av(l_tok[:, t, 256:384], src[:, 0:P], ACT.Square, accum_out=st2[:, 36 + t:37 + t]).then_inc(lo_sq, 1)
                        av(l_tok[:, t, 384:512], src[:, P:2 * P], ACT.Square, accum_out=st2[:, 44 + t:45 + t]).then_inc(lo_sq, 1)
            high_part(act, PU + 1)
            act.wait_ge(lo_rs, 1)
            act.wait_ge(lo_sq, 12)
            for t in range(TT):
                a0 = ps[4 + t // 2][:, (t % 2) * 256:(t % 2 + 1) * 256]
                a1 = ps[6 + t // 2][:, (t % 2) * 256:(t % 2 + 1) * 256]
                av(l_tok[:, t, 0:256], a0, ACT.Copy, scale=st2[:, 56 + t:57 + t]).then_inc(lo_ev, 1)
                av(l_tok[:, t, 256:384], a1[:, 0:P], ACT.Copy, scale=st2[:, 56 + t:57 + t]).then_inc(lo_ev, 1)
                av(l_tok[:, t, 384:512], a1[:, P:2 * P], ACT.Copy, scale=st2[:, 60 + t:61 + t]).then_inc(lo_ev, 1)
            for k in range(5):
                act.wait_ge(ct_mm, k + 1)
                if k < 4:
                    av(cT[:, k, :], ps[4 + k][:, :], ACT.Copy, scale=col("q_norm", k) if k < 3 else col("kv_norm")).then_inc(ct_ev, 1)
                else:
                    av(krT, ps[4][:, :], ACT.Copy).then_inc(ct_ev, 1)
            act.wait_ge(pads, 1)
            for i in range(4):
                b = 4 * (i % 2)
                act.wait_ge(step_free, 16 + i + 1)
                act.wait_ge(panel_mm, PU + 2 * i + 1)
                if i < 3:
                    high_part(act, PU + 2 * i + 2)
                for c in range(2):
                    av(upad[:, i % 2, c, PAD:PAD + T], ps[b + c][:, :], ACT.Copy).then_inc(u_pad, 1)
                act.wait_ge(panel_mm, PU + 2 * i + 2)
                if i < 3:
                    high_part(act, PU + 2 * i + 3)
                for c in range(2):
                    av(sig2[:, i % 2, c, :], ps[b + 2 + c][:, :], ACT.Sigmoid).then_inc(gb_sig, 1)

            act.wait_ge(y2_ready, 8)
            with act.Fori(0, 2) as r:
                for q in range(2):
                    def cnt(c, k):
                        return r * (2 * c) + (q * c + k)

                    high_part(act, UQ + 2 * q + 1, r, 4)
                    act.wait_ge(s_mm, cnt(8, 0) + 1)
                    for c in range(2):
                        act.wait_ge(pr_mm, cnt(7, c + 1))
                        av(qnT[:, c, :], ps[c][:, :], ACT.Copy).then_inc(pr_ev, 1)
                    for c in range(2):
                        act.wait_ge(pr_mm, cnt(7, 4 + c + 1))
                        av(knT[:, c, :], ps[c][:, :], ACT.Copy).then_inc(pr_ev, 1)
                    act.wait_ge(o_mm, cnt(2, 0) + 1)
                    for h in range(2):
                        if h == 0:
                            act.wait_ge(pr_mm, cnt(7, 7))
                        else:
                            act.wait_ge(panel_mm, r * 4 + (UQ + 2 * q + 1))
                        av(v_m[:, 2 * h:2 * h + 2, :], ps[2 + h][:, :].rearrange("p (t c) -> p t c", t=2), ACT.Copy).then_inc(pr_ev, 1)

                    def exps(u):
                        act.wait_ge(nmax, cnt(8, u + 1))
                        if u < 3:
                            act.wait_ge(t_mm, cnt(8, 0) + 1)
                        else:
                            act.wait_ge(t_mm, cnt(8, u - 2) + 1)
                        av(p_m[:, u % 3, :], ps[4 + u % 3][:, :], ACT.Exp, scale=SCALE2, bias=st2[:, 72 + u:73 + u],
                           accum_out=st2[:, 80 + u:81 + u]).then_inc(e_done, 1)

                    def evac(u):
                        b = (7, 0)[u % 2]
                        h, i = u // 4, u % 4
                        if i == 0:
                            act.wait_ge(o_mm, cnt(2, 0) + 1)
                        act.wait_ge(t_mm, cnt(8, u + 2))
                        av(pT_m[:, h, :, i * P:(i + 1) * P], ps[b][:, :].rearrange("p (k c) -> p k c", k=4), ACT.Copy).then_inc(t_ev, 1)

                    exps(0)
                    exps(1)
                    act.wait_ge(panel_mm, r * 4 + (UQ + 2 * q + 2))
                    for c in range(2):
                        av(sig_m[:, c, :], ps[c][:, :], ACT.Exp, scale=-1.0).then_inc(ga_sig, 1)
                    for u in range(2, 8):
                        exps(u)
                        evac(u - 2)
                    evac(6)
                    evac(7)
            act.wait_ge(dec_in, 16)
            av(lsg[:, 0, :], dec, ACT.Abs).then_inc(dec_abs, 1)
            act.wait_ge(dec_abs, 1)
            av(lsg[:, 1, :], lsg[:, 0, :], ACT.Exp, scale=-1.0).then_inc(dec_abs, 1)
            for h in range(RH):
                act.wait_ge(dec_arg, h + 1)
                av(decay[:, h, :], decay[:, h, :], ACT.Exp).then_inc(dec_exp, 1)
            if upto == 2:
                return

            norm(TT, x2_ready, 16, "r_norm", (RQ, RQ + 1))
            with act.Fori(0, 2) as r:
                for q in range(2):
                    def cnt(c, k):
                        return r * (2 * c) + (q * c + k)

                    n = RQ + 6 * q
                    for x in range(4):
                        act.wait_ge(panel_mm, r * 12 + (n + x + 1))
                        high_part(act, n + x + 2, r, 12)
                    act.wait_ge(ro_mm, cnt(4, 0) + 1)
                    for t in range(TT):
                        av(v_r[:, t, :], ps[4 + t][:, :], ACT.Copy).then_inc(v_cp, 1)
                    for x in range(2):
                        act.wait_ge(panel_mm, r * 12 + (n + 5 + x))
                        high_part(act, n + 6 + x, r, 12)
                        act.wait_ge(rg_ready, cnt(4, 0) + 1)
                        for c in range(2):
                            av(sig_r[:, 2 * x + c, :], ps[(4, 2)[x] + c][:, :], ACT.Sigmoid).then_inc(rg_sig, 1)
            act.wait_ge(x3_ready, 16)
            for t in range(TT):
                av(squares[:, t, :], x_res[:, t, :], ACT.Square, accum_out=st2[:, 8 + t:9 + t]).then_inc(n_sq, 1)

        @block.vector
        def _(dve):
            V = Steps(dve, v_step)
            for first in (e_used, bu_used, ss_done, scaled, y_ready, sm_done, o_ev, step_free, ym_ready, rg_ready, on_ready, yr_ready):
                dve.sem_inc(first, 1)
            v = nc.vector
            MUL, ADD, SUB = ALU.mult, ALU.add, ALU.subtract
            V(v.memset(half_m, -0.5))
            V(v.memset(st[:, 36:40], 0.0))
            v.memset(st[:, 40:41], 0.0).then_inc(e_used, 1)

            def chain(ins):
                V(ins)
                V.wait()

            s_ = lambda k: ssp[:, k, :]
            dve.wait_ge(par_in, 32)
            dve.wait_ge(ssm_exp, 1)
            v.tensor_tensor(s_(4), lr, s_(3), MUL).then_inc(ssm_dt, 1)
            chain(v.tensor_tensor(s_(6), li, s_(3), MUL))
            chain(v.tensor_scalar(s_(7), s_(6), TURN, ROUND, MUL, ADD))
            chain(v.tensor_scalar(s_(7), s_(7), ROUND, None, SUB))
            chain(v.scalar_tensor_tensor(s_(6), s_(7), -PI2_A, s_(6), MUL, ADD))
            chain(v.scalar_tensor_tensor(s_(6), s_(7), -PI2_B, s_(6), MUL, ADD))
            chain(v.scalar_tensor_tensor(s_(6), s_(7), -PI2_C, s_(6), MUL, ADD))
            chain(v.tensor_scalar(s_(8), s_(6), TURN * 4096, ROUND, MUL, ADD))
            chain(v.tensor_scalar(s_(8), s_(8), ROUND, 1.0 / 4096, SUB, MUL))
            chain(v.scalar_tensor_tensor(s_(9), s_(8), -PI2_A, s_(6), MUL, ADD))
            chain(v.scalar_tensor_tensor(s_(9), s_(8), -(PI2_B + PI2_C), s_(9), MUL, ADD))
            chain(v.tensor_scalar(s_(9), s_(9), TURN, None, MUL))
            dve.wait_ge(x_sq, TT)
            v.tensor_scalar(st[:, 28:32], st[:, 24:28], 1.0 / D, EPS, MUL, ADD).then_inc(x_ms, 1)
            tvb = tv.unsqueeze(1).to_broadcast([P, NTILE, 48])

            def wide(k):
                return s_(k).unsqueeze(2).to_broadcast([P, NTILE, 48])

            V(v.tensor_tensor(tw[0], tvb, wide(8), MUL))
            chain(v.tensor_tensor(tw[1], tvb, wide(9), MUL))
            chain(v.tensor_scalar(tw[2], tw[0], ROUND, ROUND, ADD, SUB))
            chain(v.tensor_tensor(tw[0], tw[0], tw[2], SUB))
            chain(v.tensor_tensor(tw[0], tw[0], tw[1], ADD))
            chain(v.tensor_scalar(tw[2], tw[0], ROUND, ROUND, ADD, SUB))
            v.tensor_tensor(tw[0], tw[0], tw[2], SUB).then_inc(ang_in, 1)
            dve.wait_ge(const_in, 64)
            chain(v.tensor_copy(st[:, 16:20], st[:, 20:24].bitcast(mybir.dt.int32)))
            for t in range(TT):
                V(v.tensor_scalar(angA[:, 1, t, :], angA[:, 0, t, :], st[:, 16 + t:17 + t], None, MUL))
            V.wait()
            chain(v.tensor_scalar(angA[:, 2], angA[:, 1], TURN, ROUND, MUL, ADD))
            chain(v.tensor_scalar(angA[:, 2], angA[:, 2], ROUND, None, SUB))
            for part in (PI2_A, PI2_B, PI2_C):
                chain(v.scalar_tensor_tensor(angA[:, 1], angA[:, 2], -part, angA[:, 1], MUL, ADD))
            chain(v.tensor_scalar(angA[:, 3], angA[:, 1], TURN, 0.5, MUL, ALU.min))
            v.tensor_scalar(angA[:, 3], angA[:, 3], -0.5, None, ALU.max).then_inc(ang_in, 1)
            dve.wait_ge(trig_ready, 1)
            ptab = pack[:, :, 512:896].rearrange("p m (j c) -> p m j c", j=4)
            tw4 = [x.rearrange("p (m j) c -> p m j c", j=4) for x in tw]
            V(v.tensor_copy(ptab[:, :, :, 48:96], tw4[1]))
            chain(v.tensor_tensor(tw[3], tw[2], tw[2], MUL))
            chain(v.tensor_scalar(ptab[:, :, :, 0:48], tw4[3], -2.0, 1.0, MUL, ADD))
            dve.wait_ge(ssm_exp, 2)
            V(v.tensor_copy(pack[:, :, 896:900], s_(5).rearrange("p (m j) -> p m j", j=4)))
            pt32 = pack[:, :, 512:896].rearrange("p m (j c) -> p m j c", j=4)
            s4 = lambda k: s_(k).rearrange("p (m j) -> p m j", j=4)
            V(v.tensor_tensor(s4(10), s4(5), pt32[:, :, :, 33], MUL))
            V(v.tensor_tensor(s4(11), s4(5), pt32[:, :, :, 48 + 33], MUL))
            V(v.tensor_tensor(s_(12), lr, lr, MUL))
            chain(v.tensor_tensor(s_(13), li, li, MUL))
            chain(v.tensor_tensor(s_(12), s_(12), s_(13), ADD))
            V(v.reciprocal(s_(12), s_(12)))
            chain(v.tensor_scalar(s_(10), s_(10), -1.0, None, ADD))
            V(v.tensor_tensor(s_(13), s_(10), lr, MUL))
            V(v.tensor_tensor(s_(14), s_(11), li, MUL))
            V(v.tensor_tensor(s_(15), s_(11), lr, MUL))
            chain(v.tensor_tensor(s_(16), s_(10), li, MUL))
            V(v.tensor_tensor(s_(13), s_(13), s_(14), ADD))
            chain(v.tensor_tensor(s_(15), s_(15), s_(16), SUB))
            V(v.tensor_tensor(s_(13), s_(13), s_(12), MUL))
            chain(v.tensor_tensor(s_(15), s_(15), s_(12), MUL))
            fb = lambda k: s_(k).unsqueeze(2).to_broadcast([P, NTILE, 32])
            dve.wait_ge(ssm_in, 32)
            V(v.tensor_tensor(bbs[:, 0], b_nat[:, 0], fb(13), MUL))
            chain(v.tensor_tensor(bt_tmp, b_nat[:, 1], fb(15), MUL))
            v.tensor_tensor(bbs[:, 0], bbs[:, 0], bt_tmp, SUB).then_inc(bb_ready, 1)
            dve.wait_ge(bb_ready, 1)
            V(v.tensor_tensor(bbs[:, 1], b_nat[:, 1], fb(13), MUL))
            chain(v.tensor_tensor(bt_tmp, b_nat[:, 0], fb(15), MUL))
            v.tensor_tensor(bbs[:, 1], bbs[:, 1], bt_tmp, ADD).then_inc(bb_ready, 1)
            dve.wait_ge(trig_ready, 2)
            V(v.tensor_copy(csA[:, 1], angA[:, 1]))
            chain(v.tensor_tensor(angA[:, 3], angA[:, 2], angA[:, 2], MUL))
            chain(v.tensor_scalar(csA[:, 0], angA[:, 3], -2.0, 1.0, MUL, ADD))
            v.memset(st[:, 41:42], 0.0).then_inc(bb_ready, 1)

            def tile_step(i, j):
                n = i * 4 + (j + 1)
                dve.wait_ge(bu_mm, n)
                dve.wait_ge(e_ready, n)
                c, s = E[:, j % 2, 0], E[:, j % 2, 1]
                bre, bim = ps[5][:, :], ps[6][:, :]
                V(v.tensor_tensor(t_a[0], bre, c, MUL))
                k2 = V(v.tensor_tensor(t_a[1], bim, s, MUL))
                V(v.tensor_tensor(gs[:, 0], bim, c, MUL))
                v.tensor_tensor(gs[:, 1], bre, s, MUL).then_inc(bu_used, 1)
                V.wait(k2)
                k3 = V(v.tensor_tensor(bp[:, 0], t_a[0], t_a[1], ADD))
                dve.wait_ge(bu_used, n + 1)
                k4 = V(v.tensor_tensor(bp[:, 1], gs[:, 0], gs[:, 1], SUB))
                mag = pack[:, bass.ds(i, 1), 896 + j:897 + j].rearrange("p o n -> p (o n)").to_broadcast([P, 512])
                V.wait(k4)
                k5 = V(v.tensor_tensor_scan(gs[:, 0], mag, bp[:, 0], 0.0, MUL, ADD))
                k6 = V(v.tensor_tensor_scan(gs[:, 1], mag, bp[:, 1], 0.0, MUL, ADD))
                V.wait(k5)
                V(v.tensor_tensor(t_a[0], gs[:, 0], c, MUL))
                V.wait(k6)
                V(v.tensor_tensor(t_a[1], gs[:, 1], s, MUL))
                V(v.tensor_tensor(bp[:, 0], gs[:, 1], c, MUL))
                v.tensor_tensor(bp[:, 1], gs[:, 0], s, MUL).then_inc(e_used, 1)
                if j == 0:
                    dve.wait_ge(c_mm, i * 4 + 1)
                else:
                    dve.wait_ge(c_mm, i * 4 + (j - 1) + 1)
                dve.wait_ge(e_used, n + 1 + 1)
                V(v.tensor_tensor(hs[:, j % 2, 0], t_a[0], t_a[1], SUB))
                v.scalar_tensor_tensor(hs[:, j % 2, 1], bp[:, 0], -1.0, bp[:, 1], MUL, SUB).then_inc(h_ready, 1)
                dve.wait_ge(h_ready, n)

            def heads_ms(i, x):
                dve.wait_ge((q_ev, k_ev)[x], i * 2 + 2 + 1)
                so = 48 + 36 * x
                v.tensor_reduce(st[:, so:so + 12], sq, AX.X, ADD).then_inc(ss_done, 1)
                dve.wait_ge(ss_done, i * 2 + (x + 2))
                dve.wait_ge(rs_ready, i * 2 + x + 1)
                v.tensor_scalar(st[:, so + 12:so + 24], st[:, so:so + 12], 1.0 / HD, EPS, MUL, ADD).then_inc(ms_ready, 1)

            def heads_scale(i, x):
                so = 48 + 36 * x
                q = qkv_tok[x][:, :, bass.ds(i * PC, PC)]
                dve.wait_ge(rs_ready, i * 2 + (x + 2))
                rs = st[:, so + 24:so + 36].rearrange("p (t h) -> p t h", t=TT).unsqueeze(3).to_broadcast([P, TT, PH, HD])
                q4 = q.rearrange("p t (h d) -> p t h d", h=PH)
                kk = V(v.tensor_tensor(q4, q4, rs, MUL))
                dve.wait_ge(qkw_full, i * 16 + 16)
                V.wait(kk)
                v.tensor_tensor(q, q, qk_w[:, x, :].unsqueeze(1).to_broadcast([P, TT, PC]), MUL).then_inc(scaled, 1)

            with dve.Fori(0, KT) as i:
                V.loop(i, 46)
                tile_step(i, 0)
                tile_step(i, 1)
                heads_ms(i, 0)
                tile_step(i, 2)
                heads_scale(i, 0)
                tile_step(i, 3)
                heads_ms(i, 1)
                dve.wait_ge(c_mm, i * 4 + 4 + 1)
                dve.wait_ge(gelu_done, i + 1)
                v.scalar_tensor_tensor(y_sb, u_cur, cols[:, bass.ds(i + COLS["d_skip"], 1)], ps[7][:, :], MUL, ADD).then_inc(y_ready, 1)
                heads_scale(i, 1)
            V.end(KT)

            dve.wait_ge(mask_in, 16)
            with dve.Fori(0, 4) as p:
                V.loop(p, 32)

                def soft(u):
                    i = u % 4
                    dve.wait_ge(sc_mm, p * 8 + (u + 2))
                    dve.wait_ge(p_ready, p * 8 + max(u - 1, 0) + 1)
                    w0, w1 = min(i + 1, 2) * P, (i + 1) * P
                    b = u % 2
                    mask_at = [masks[:, 256 - w0:256], masks[:, 256 + 512 - w1:768], masks[:, 768 + 512 - w1:1280]]
                    x0 = 0
                    for g, w in enumerate((w0, w1, w1)):
                        ins = v.scalar_tensor_tensor(sm[:, b, x0:x0 + w], ps[g][:, 0:w], SCALE1, mask_at[g], MUL, ADD)
                        x0 += w
                        if g < 2:
                            V(ins)
                    ins.then_inc(sm_done, 1)
                    dve.wait_ge(sm_done, p * 8 + (u + 2))
                    k = V(v.tensor_reduce(mx[:, b:b + 1], sm[:, b, 0:x0], AX.X, ALU.max))
                    V.wait(k)
                    v.tensor_scalar(nmx[:, b:b + 1], mx[:, b:b + 1], -1.0, None, MUL).then_inc(nm_ready, 1)

                def o_out(u):
                    b = u % 2
                    dve.wait_ge(p_ready, p * 8 + (u + 2))
                    k = V(v.reciprocal(rden[:, u:u + 1], den[:, u:u + 1]))
                    dve.wait_ge(pv_mm, p * 8 + (u + 2))
                    V.wait(k)
                    v.tensor_scalar(o_tok[:, u % 4, bass.ds(p * 128 + (u // 4) * HD, HD)], ps[6 + b][:, (u // 4) * HD:(u // 4 + 1) * HD],
                                    rden[:, u:u + 1], None, MUL).then_inc(o_ev, 1)

                soft(0)
                soft(1)
                for u in range(8):
                    if u < 6:
                        soft(u + 2)
                    if u >= 1:
                        o_out(u - 1)
                o_out(7)
            V.end(4)

            def angles2():
                dve.wait_ge(misc_in, 32)
                dve.wait_ge(pos_in, 16)
                V(v.tensor_copy(pos2c, pos2i.bitcast(mybir.dt.int32)))
                V.wait()
                pi = turns[:, 0:T].bitcast(mybir.dt.int32)
                for k in range(2):
                    V(v.tensor_scalar(ang[:, k * T:(k + 1) * T], pi, inv_cols[:, k:k + 1], None, MUL))
                for t in range(TT):
                    V(v.tensor_scalar(ang[:, 1024 + 32 * t:1056 + 32 * t], inv_row, pos2c[:, t:t + 1], None, MUL))
                V.wait()
                chain(v.tensor_scalar(turns, ang, TURN, ROUND, MUL, ADD))
                chain(v.tensor_scalar(turns, turns, ROUND, None, SUB))
                for part in (PI2_A, PI2_B, PI2_C):
                    chain(v.scalar_tensor_tensor(ang, turns, -part, ang, MUL, ADD))
                chain(v.tensor_scalar(ang, ang, TURN, 0.5, MUL, ALU.min))
                v.tensor_scalar(ang, ang, -0.5, None, ALU.max).then_inc(ang2, 1)

            def tables2():
                dve.wait_ge(trig2, 1)
                chain(v.tensor_tensor(cosT, cosT, cosT, MUL))
                chain(v.tensor_scalar(cosT, cosT, -2.0, 1.0, MUL, ADD))
                chain(v.tensor_scalar(sinM, sinM, inv_cols[:, 2:3], None, MUL))

            def in_parts(dst, k, src):
                chain(v.tensor_copy(dst[0][:, k, :], src))
                return v.tensor_tensor(dst[1][:, k, :], src, dst[0][:, k, :], SUB)

            for h in range(2):
                dve.wait_ge(g_high, h + 1)
                v.tensor_tensor(gS[1][:, 4 * h:4 * h + 4, :], gT[:, 4 * h:4 * h + 4, :], gS[0][:, 4 * h:4 * h + 4, :], SUB
                                ).then_inc(g_low, 1)
            low_part(dve, 1)
            for s in range(13):
                b = 4 * (s % 2)
                sg = sig[:, s % 2]
                if s == 0:
                    v.memset(st[:, 42:43], 0.0).then_inc(step_free, 1)
                low_part(dve, 2 * s + 2)
                if s < 4:
                    for c in range(2):
                        dve.wait_ge(glu_sig, 4 * s + 1 + c)
                        kz = V(v.tensor_tensor(prod[:, 2 + c, :], ps[b + c][:, :], sg[:, c, :], MUL))
                    low_part(dve, 2 * s + 3)
                    for c in range(2):
                        dve.wait_ge(glu_sig, 4 * s + 3 + c)
                        chain(v.tensor_tensor(prod[:, c, :], gT[:, 2 * s + c, :], sg[:, 2 + c, :], MUL))
                        chain(v.tensor_tensor(prod[:, c, :], prod[:, c, :], prod[:, 2 + c, :], MUL))
                        in_parts(yS, 2 * s + c, prod[:, c, :]).then_inc(ys_ready, 1)
                    dve.wait_ge(ys_ready, 2 * s + 2)
                elif s < 8:
                    low_part(dve, 2 * s + 3)
                    for c in range(2):
                        dve.wait_ge(rs_sig, 2 * (s - 4) + c + 1)
                        dve.wait_ge(panel_mm, 2 * s + 2)
                        v.tensor_tensor(mT[:, 2 * (s - 4) + c, :], ps[b + 2 + c][:, :], sg[:, c, :], MUL).then_inc(m_ready, 1)
                elif s == 8:
                    for c in range(4):
                        if c == 2:
                            low_part(dve, 2 * s + 3)
                        dve.wait_ge(glu_sig, 16 + c + 1)
                        chain(v.tensor_tensor(prod[:, c, :], ps[b + c][:, :], sg[:, c, :], MUL))
                        dve.wait_ge(ot_mm, c + 1)
                        chain(v.tensor_tensor(prod[:, c, :], ps[4 + c][:, :], prod[:, c, :], MUL))
                        in_parts(oS, c, prod[:, c, :]).then_inc(ya_ready, 1)
                    dve.wait_ge(ya_ready, 4)
                else:
                    if s == 10:
                        angles2()
                    if s == 11:
                        tables2()
                    low_part(dve, 2 * s + 3)
                    for c in range(2):
                        dve.wait_ge(rs_sig, 8 + 2 * (s - 9) + c + 1)
                        dve.wait_ge(panel_mm, 2 * s + 2)
                        k = 2 * (s - 9) + c
                        chain(v.tensor_tensor(prod[:, c, :], ps[b + 2 + c][:, :], sg[:, c, :], MUL))
                        chain(v.tensor_tensor(prod[:, c, :], mT[:, k, :], prod[:, c, :], ADD))
                        in_parts(mS, k, prod[:, c, :]).then_inc(m_ready, 1)
                    dve.wait_ge(m_ready, 8 + 2 * (s - 9) + 2)
                v.memset(st[:, 43:44], 0.0).then_inc(step_free, 1)
                dve.wait_ge(step_free, s + 2 + 1)
            for s in (13, 14):
                for n in ((28, 29), (30,))[s - 13]:
                    low_part(dve, n)
                dve.wait_ge(xr_in, 16)
                dve.wait_ge(panel_mm, 2 * s + 2)
                for t in range(TT):
                    xs = x_res[:, t, (s - 13) * 512:(s - 12) * 512]
                    v.tensor_tensor(xs, ps[4 * (s % 2) + t][:, :], xs, ADD).then_inc(x1_ready, 1)
                v.memset(st[:, 43:44], 0.0).then_inc(step_free, 1)
                dve.wait_ge(step_free, s + 2 + 1)

            if upto == 1:
                return

            def mean_square(t0):
                dve.wait_ge(n_sq, t0 + TT)
                v.tensor_scalar(st2[:, 12:16], st2[:, 8:12], 1.0 / D, EPS, MUL, ADD).then_inc(n_ms, 1)

            def low_norm(n0, cname):
                for k in range(KT):
                    dve.wait_ge(nt_ev, n0 + k + 1)
                    v.scalar_tensor_tensor(hS[1][:, k, :], ps[k][:, :], col(cname, k), hS[0][:, k, :], MUL, SUB
                                           ).then_inc(nt_low, 1)

            mean_square(0)
            low_part(dve, 31)
            low_norm(0, "a_norm")
            dve.wait_ge(nt_mm, KT)
            V(v.memset(upad[:, :, :, 0:PAD], 0.0))
            v.memset(upad[:, :, :, PAD + T:2 * PAD + T], 0.0).then_inc(pads, 1)
            dve.wait_ge(pads, 1)
            n = first_of["lo"]
            low_part(dve, n + 2)
            low_part(dve, n + 3)
            dve.wait_ge(panel_mm, n + 3)
            kr = kr_tok[:, :, 64:128]
            v.tensor_copy(kr, ps[0][:, 0:256].rearrange("p (t c) -> p t c", t=TT)).then_inc(kr_raw, 1)
            dve.wait_ge(kr_raw, 1)
            tk = y2T[:, 0, :].rearrange("p (x t c) -> p x t c", x=4, t=TT)
            V(v.tensor_tensor(tk[:, 0], kr[:, :, 0:32], cosK, MUL))
            V(v.tensor_tensor(tk[:, 1], kr[:, :, 32:64], sinK, MUL))
            V(v.tensor_tensor(tk[:, 2], kr[:, :, 32:64], cosK, MUL))
            chain(v.tensor_tensor(tk[:, 3], kr[:, :, 0:32], sinK, MUL))
            V(v.tensor_tensor(kr_tok[:, :, 0:32], tk[:, 0], tk[:, 1], SUB))
            v.tensor_tensor(kr_tok[:, :, 32:64], tk[:, 2], tk[:, 3], ADD).then_inc(kr_rot, 1)
            dve.wait_ge(kr_rot, 1)
            v.tensor_copy(kr_tok[:, :, 64:128], kr_tok[:, :, 0:64]).then_inc(kr_rot, 1)
            low_part(dve, PU + 1)
            dve.wait_ge(lo_sq, 12)
            chain(v.tensor_tensor(st2[:, 40:44], st2[:, 32:36], st2[:, 36:40], ADD))
            chain(v.tensor_scalar(st2[:, 48:52], st2[:, 40:44], 1.0 / QL, EPS, MUL, ADD))
            v.tensor_scalar(st2[:, 52:56], st2[:, 44:48], 1.0 / KVL, EPS, MUL, ADD).then_inc(lo_ms, 1)
            dve.wait_ge(lo_ev, 12)
            v.memset(st2[:, 0:1], 0.0).then_inc(step_free, 1)
            dve.wait_ge(step_free, 18)

            def pool_gate(i):
                b = 4 * (i % 2)
                for c in range(2):
                    dve.wait_ge(gb_sig, 2 * i + c + 1)
                    k = V(v.tensor_tensor(prod2[:, c, :], ps[b + 2 + c][:, :], sig2[:, i % 2, c, :], MUL))
                    dve.wait_ge(pool_mm, i + 1)
                    V.wait(k)
                    v.scalar_tensor_tensor(y2T[:, 8 + 2 * i + c, :], ps[b + c][:, :], col("pool_scale", 2 * i + c),
                                           prod2[:, c, :], MUL, MUL).then_inc(y2_ready, 1)
                dve.wait_ge(y2_ready, 2 * i + 2)
                v.memset(st2[:, 0:1], 0.0).then_inc(step_free, 1)
                dve.wait_ge(step_free, 18 + i + 1)

            for i, wd in enumerate(POOLS):
                if i < 3:
                    low_part(dve, PU + 2 * i + 2)
                if i >= 1:
                    pool_gate(i - 1)
                dve.wait_ge(u_pad, 2 * i + 2)
                src, n = upad[:, i % 2], T + 2 * PAD
                for k in range(i + 1):
                    n -= 1 << k
                    dst = win[:, k % 2]
                    chain(v.tensor_tensor(dst[:, :, 0:n], src[:, :, 0:n], src[:, :, (1 << k):(1 << k) + n], ADD))
                    src = dst
                x0 = PAD - wd // 2
                sums = src[:, :, x0:x0 + T]
                for e in range(2):
                    edge = sums[:, :, e * (T - 8):e * (T - 8) + 8]
                    V(v.tensor_tensor(edge, edge, corr[:, i, 8 * e:8 * e + 8].unsqueeze(1).to_broadcast([P, 2, 8]), MUL))
                V.wait()
                if i >= 2:
                    dve.wait_ge(pool_mm, i - 1)
                v.scalar_tensor_tensor(pool_d[:, i % 2], sums, 1.0 / wd, upad[:, i % 2, :, PAD:PAD + T], MUL, SUB
                                       ).then_inc(d_ready, 1)
                dve.wait_ge(d_ready, i + 1)
                if i < 3:
                    low_part(dve, PU + 2 * i + 3)
            pool_gate(3)

            with dve.Fori(0, 2) as r:
                V.loop(r, MLA_STEPS)
                for q in range(2):
                    def cnt(c, k):
                        return r * (2 * c) + (q * c + k)

                    low_part(dve, UQ + 2 * q + 1, r, 4)
                    for c in range(2):
                        dve.wait_ge(pr_mm, cnt(7, 3 + c))
                        V(v.tensor_tensor(rot[:, c, :], ps[2 + c][:, :], (cosM, sinM)[c], MUL))
                    V.wait()
                    dve.wait_ge(s_mm, cnt(8, 0) + 1)
                    v.tensor_tensor(qrT, rot[:, 0, :], rot[:, 1, :], ADD).then_inc(rot_done, 1)
                    dve.wait_ge(rot_done, cnt(1, 1))

                    def row_max(u):
                        dve.wait_ge(s_mm, cnt(8, u + 2))
                        k = V(v.tensor_reduce(st2[:, 88 + u:89 + u], ps[4 + u % 3][:, :], AX.X, ALU.max))
                        V.wait(k)
                        if u == 0:
                            dve.wait_ge(e_done, cnt(8, 0) + 1)
                        v.tensor_scalar(st2[:, 72 + u:73 + u], st2[:, 88 + u:89 + u], -SCALE2, None, MUL).then_inc(nmax, 1)

                    def recip(u):
                        dve.wait_ge(e_done, cnt(8, u + 2))
                        if u == 0:
                            dve.wait_ge(p_norm, cnt(8, 0) + 1)
                        v.reciprocal(st2[:, 96 + u:97 + u], st2[:, 80 + u:81 + u]).then_inc(rcp, 1)

                    def gate():
                        for c in range(2):
                            dve.wait_ge(ga_sig, cnt(2, c + 1))
                            v.tensor_copy(gate_m[:, c, :], ps[c][:, :]).then_inc(ga_ready, 1)
                        V(v.tensor_scalar(sig_m, sig_m, 1.0, None, ADD))

                    def gate_half(c):
                        chain(v.reciprocal(sig_m[:, c, :], sig_m[:, c, :]))
                        dve.wait_ge(ga_ready, cnt(2, c + 1))
                        v.tensor_tensor(gate_m[:, c, :], gate_m[:, c, :], sig_m[:, c, :], MUL).then_inc(ga_done, 1)

                    def gated(h):
                        dve.wait_ge(ga_done, cnt(2, h + 1))
                        dve.wait_ge(o_mm, cnt(2, h + 2))
                        v.tensor_tensor(y2T[:, bass.ds(r * 4 + (2 * q + h), 1), :].rearrange("p o n -> p (o n)"),
                                        ps[2 + h][:, :], gate_m[:, h, :], MUL).then_inc(ym_ready, 1)

                    row_max(0)
                    row_max(1)
                    recip(0)
                    recip(1)
                    gate()
                    V.wait()
                    for u in range(2, 8):
                        row_max(u)
                        recip(u)
                        if u in HALVES:
                            gate_half(HALVES.index(u))
                        if u == 7:
                            gated(0)
                    gated(1)
                    dve.wait_ge(ym_ready, cnt(2, 2) + 1)
            V.end(2)

            dve.wait_ge(dec_abs, 2)
            dve.wait_ge(delta_in, 16)
            L = lambda k: lsg[:, k, :]
            chain(v.tensor_scalar(L(2), L(1), 2.0, None, ADD))
            chain(v.reciprocal(L(2), L(2)))
            chain(v.tensor_tensor(L(2), L(2), L(1), MUL))
            chain(v.tensor_tensor(L(3), L(2), L(2), MUL))
            chain(v.tensor_scalar(L(4), L(3), 1.0 / 15, None, MUL))
            for d in (13, 11, 9, 7, 5, 3):
                chain(v.scalar_tensor_tensor(L(4), L(4), 1.0 / d, L(3), ADD, MUL))
            chain(v.scalar_tensor_tensor(L(4), L(4), 1.0, L(2), ADD, MUL))
            chain(v.tensor_scalar(L(5), dec, 0.0, None, ALU.min))
            chain(v.scalar_tensor_tensor(L(5), L(4), -2.0, L(5), MUL, ADD))
            chain(v.tensor_scalar(L(4), L(5), -1.0, None, MUL))
            dve.wait_ge(t_ev, 33)
            dve.wait_ge(o_mm, 9)
            for h in range(RH):
                V(v.tensor_scalar(dt1, delta, 0.0, L(5)[:, h:h + 1], ALU.max, MUL))
                chain(v.tensor_scalar(dt2, delta, 0.0, L(4)[:, 4 + h:5 + h], ALU.min, MUL))
                v.tensor_tensor(decay[:, h, :], dt1, dt2, ADD).then_inc(dec_arg, 1)
                dve.wait_ge(dec_arg, h + 1)

            def residual(n0, s, ready):
                b = 4 * (s % 2)
                i = (s - 20) % 4
                dve.wait_ge(panel_mm, n0 + 2)
                for t in range(TT):
                    xs = x_res[:, t, i * 256:(i + 1) * 256]
                    v.tensor_tensor(xs, ps[b + t][:, 0:256], xs, ADD).then_inc(ready, 1)
                v.memset(st2[:, 0:1], 0.0).then_inc(step_free, 1)
                dve.wait_ge(step_free, s + 2 + 1)

            for i in range(4):
                residual(OA + 2 * i, 20 + i, x2_ready)
            if upto == 2:
                return
            mean_square(TT)
            low_part(dve, RQ)
            low_part(dve, RQ + 1)
            low_norm(KT, "r_norm")
            dve.wait_ge(dec_exp, RH)
            with dve.Fori(0, 2) as r:
                V.loop(r, RET_STEPS)
                for q in range(2):
                    def cnt(c, k):
                        return r * (2 * c) + (q * c + k)

                    for x, dst in enumerate((q_r, k_r)):
                        low_part(dve, RQ + 6 * q + 2 + x, r, 12)
                        dve.wait_ge(panel_mm, r * 12 + (RQ + 6 * q + 1 + x))
                        x1, x2 = ps[2 * x][:, :], ps[2 * x + 1][:, :]
                        V(v.tensor_tensor(rot_r[:, 0, :], x1, cosR, MUL))
                        V(v.tensor_tensor(rot_r[:, 1, :], x2, sinR, MUL))
                        V(v.tensor_tensor(rot_r[:, 2, :], x2, cosR, MUL))
                        V(v.tensor_tensor(rot_r[:, 3, :], x1, sinR, MUL))
                        V.wait()
                        V(v.tensor_tensor(dst[:, 0, :], rot_r[:, 0, :], rot_r[:, 1, :], SUB))
                        v.tensor_tensor(dst[:, 1, :], rot_r[:, 2, :], rot_r[:, 3, :], ADD).then_inc(rqk_rot, 1)
                        dve.wait_ge(rqk_rot, cnt(2, x + 1))
                    low_part(dve, RQ + 6 * q + 4, r, 12)
                    low_part(dve, RQ + 6 * q + 5, r, 12)
                    for j in range(TT):
                        dve.wait_ge(rs_mm, cnt(4, j + 1))
                        x0 = 3 * P - j * P
                        dj = decay[:, bass.ds(r * 2 + q, 1), x0:x0 + T].rearrange("p o n -> p (o n)")
                        v.scalar_tensor_tensor(sd[:, j, :], ps[j][:, :], RK ** -0.5, dj, MUL, MUL).then_inc(sd_ready, 1)

                    def gates(x):
                        low_part(dve, RQ + 6 * q + 6 + x, r, 12)
                        for c in range(2):
                            k = 2 * x + c
                            dve.wait_ge(rg_sig, cnt(4, k + 1))
                            gcol = cols[:, bass.ds(r * 8 + (COLS["gn"] + 4 * q + k), 1)]
                            v.scalar_tensor_tensor(gate_r[:, k, :], ps[(4, 2)[x] + c][:, :], gcol, sig_r[:, k, :], MUL, MUL
                                                   ).then_inc(rg_ready, 1)

                    gates(0)
                    for i in range(TT):
                        dve.wait_ge(ro_mm, cnt(4, i + 2))
                        k = V(v.bn_stats(st2[:, 104 + 6 * i:110 + 6 * i], ps[(6, 7, 0, 1)[i]][:, :]))
                    V.wait(k)
                    apart(dve)
                    for i in range(TT):
                        k = V(v.bn_aggr(st2[:, 128 + 2 * i:130 + 2 * i], st2[:, 104 + 6 * i:110 + 6 * i]))
                    V.wait(k)
                    mv = st2[:, 128:136].rearrange("p (i x) -> p i x", x=2)
                    v.tensor_scalar(st2[:, 136:140], mv[:, :, 1], EPS, None, ADD).then_inc(var_ready, 1)
                    dve.wait_ge(rstd, cnt(1, 1))
                    for i in range(TT):
                        v.tensor_scalar(on[:, i, :], ps[(6, 7, 0, 1)[i]][:, :], mv[:, i, 0:1], st2[:, 140 + i:141 + i], SUB, MUL
                                        ).then_inc(on_ready, 1)
                    gates(1)
                    dve.wait_ge(rg_ready, cnt(4, 4) + 1)
                    for i in range(TT):
                        dve.wait_ge(rt_mm, cnt(4, i + 1))
                        v.tensor_tensor(y2T[:, bass.ds(r * 8 + 4 * q, 4), i * P:(i + 1) * P],
                                        ps[4 + i][:, :].rearrange("p (k c) -> p k c", k=4),
                                        gate_r[:, :, i * P:(i + 1) * P], MUL).then_inc(yr_ready, 1)
                    dve.wait_ge(yr_ready, cnt(4, 4) + 1)
            V.end(2)
            for i in range(4):
                residual(TA + 2 * i, 24 + i, x3_ready)
            mean_square(2 * TT)
            dve.wait_ge(gain_in, 16)
            dve.wait_ge(n_rs, 3)
            for t in range(TT):
                v.scalar_tensor_tensor(x_res[:, t, :], x_res[:, t, :], st2[:, 16 + t:17 + t], gain, MUL, MUL).then_inc(f_out, 1)

        @block.gpsimd
        def _(pool):
            G = Steps(pool, g_step)
            for first in (rs_ready, p_norm):
                pool.sem_inc(first, 1)
            g = nc.gpsimd
            MUL, ADD, SUB = ALU.mult, ALU.add, ALU.subtract
            pool.wait_ge(v_step, 2)
            pool.wait_ge(x_ms, 1)
            g.tensor_tensor(st[:, 32:36], st[:, 28:32], half_m[:, 0:4], ALU.pow).then_inc(x_rs, 1)
            pool.wait_ge(bb_ready, 3)

            def phases(i, j):
                n = i * 4 + (j + 1)
                tab = pack[:, bass.ds(i, 1), 512 + 96 * j:608 + 96 * j].rearrange("p o n -> p (o n)")
                hi = lambda x: tab[:, 48 * x:48 * x + 32].unsqueeze(2).to_broadcast([P, 32, 16])
                lo = lambda x: tab[:, 48 * x + 32:48 * x + 48].unsqueeze(1).to_broadcast([P, 32, 16])
                r = lambda x: x.rearrange("p (a b) -> p a b", a=32)
                c, s = E[:, j % 2, 0], E[:, j % 2, 1]
                pool.wait_ge(e_used, i * 4 + j + 1)
                apart(pool)
                G(g.tensor_tensor(r(e_t[0]), hi(0), lo(0), MUL))
                k = G(g.tensor_tensor(r(e_t[1]), hi(1), lo(1), MUL))
                G.wait(k)
                k = G(g.tensor_tensor(c, e_t[0], e_t[1], SUB))
                G.wait(k)
                apart(pool)
                G(g.tensor_tensor(r(e_t[0]), hi(1), lo(0), MUL))
                k = G(g.tensor_tensor(r(e_t[1]), hi(0), lo(1), MUL))
                G.wait(k)
                g.tensor_tensor(s, e_t[0], e_t[1], ADD).then_inc(e_ready, 1)
                pool.wait_ge(e_ready, n)

            def power(i, x):
                so = 48 + 36 * x
                pool.wait_ge(ms_ready, i * 2 + (x + 1))
                g.tensor_tensor(st[:, so + 24:so + 36], st[:, so + 12:so + 24], half_m[:, 0:12], ALU.pow
                                ).then_inc(rs_ready, 1)

            def rope(i, x):
                pool.wait_ge(scaled, i * 2 + (x + 2))
                apart(pool)
                q = qkv_tok[x][:, :, bass.ds(i * PC, PC)].rearrange("p t (h d) -> p t h d", h=PH)
                x1, x2 = q[:, :, :, 0:ROPE1], q[:, :, :, ROPE1:2 * ROPE1]
                cb = csA[:, 0].unsqueeze(2).to_broadcast([P, TT, PH, ROPE1])
                sb = csA[:, 1].unsqueeze(2).to_broadcast([P, TT, PH, ROPE1])
                G(g.tensor_tensor(rt[0], x1, cb, MUL))
                G(g.tensor_tensor(rt[1], x2, sb, MUL))
                G(g.tensor_tensor(rt[2], x2, cb, MUL))
                k = G(g.tensor_tensor(rt[3], x1, sb, MUL))
                G.wait(k)
                apart(pool)
                G(g.tensor_tensor(x1, rt[0], rt[1], SUB))
                g.tensor_tensor(x2, rt[2], rt[3], ADD).then_inc(roped, 1)
                pool.wait_ge(roped, i * 2 + (x + 1))

            def turn(i, more):
                phases(i, 2)
                power(i, 0)
                phases(i, 3)
                rope(i, 0)
                if more:
                    phases(i + 1, 0)
                power(i, 1)
                if more:
                    phases(i + 1, 1)
                rope(i, 1)

            phases(0, 0)
            phases(0, 1)
            with pool.Fori(0, KT - 1) as i:
                G.loop(i, 30)
                turn(i, True)
            G.end(KT - 1)
            turn(KT - 1, False)
            with pool.Fori(1, 4) as p:
                pool.wait_ge(tr_mm, p * 6 + 1)
                apart(pool)
                for x in range(6):
                    src = qkv_tok[x // 3][:, :, bass.ds(p * 128 + (x % 3) * 512, P)]
                    ins = g.tensor_copy(qg[:, x], src)
                ins.then_inc(qg_ready, 1)
            pool.wait_ge(qg_ready, 4)
            pool.wait_ge(v_mm, 2 * KT + 1)
            g.tensor_copy(hS[0], hT).then_inc(h_split, 1)
            pool.wait_ge(h_split, 1)
            g.tensor_tensor(hS[1], hT, hS[0], SUB).then_inc(h_split, 1)
            pool.wait_ge(scaled, 2 * KT + 1)
            pool.wait_ge(w_full[0], 16)
            g.tensor_copy(split_w[:, 0, 0, :], raw[:, 0, :]).then_inc(w_first, 1)
            pool.wait_ge(w_first, 1)
            g.tensor_tensor(split_w[:, 0, 1, :], raw[:, 0, :], split_w[:, 0, 0, :], SUB).then_inc(w_first, 1)
            if upto == 1:
                return

            def power2(k):
                pool.wait_ge(n_ms, k + 1)
                g.tensor_tensor(st2[:, 16:20], st2[:, 12:16], half_m[:, 0:4], ALU.pow).then_inc(n_rs, 1)

            power2(0)
            pool.wait_ge(lo_ms, 1)
            g.tensor_tensor(st2[:, 56:64], st2[:, 48:56], half_m[:, 0:8], ALU.pow).then_inc(lo_rs, 1)
            with pool.Fori(0, 4) as p:
                for u in range(8):
                    pool.wait_ge(rcp, p * 8 + (u + 1))
                    apart(pool)
                    g.tensor_scalar(p_m[:, u % 3, :], p_m[:, u % 3, :], st2[:, 96 + u:97 + u], None, MUL).then_inc(p_norm, 1)
            if upto == 2:
                return
            power2(1)
            with pool.Fori(0, 4) as h:
                pool.wait_ge(var_ready, h + 1)
                g.tensor_tensor(st2[:, 140:144], st2[:, 136:140], half_m[:, 0:4], ALU.pow).then_inc(rstd, 1)
            power2(2)
def constants():
    p = np.arange(P)
    t = np.concatenate([16 * np.arange(32), np.arange(16)]).astype(np.float32)
    invA = (np.float32(500000.0) ** (-np.arange(0, 16, 2, dtype=np.float32) / np.float32(16))).astype(np.float32)
    k = np.arange(256)[None, :] - P
    q = p[:, None]
    m0 = (k <= q) & (k >= q - P)
    k = np.arange(512)[None, :] - 384
    masks = [m0] + [(k <= q) & ((q - k) % d == 0) for d in (4, 16)]
    masks = np.where(np.concatenate(masks, 1), 0.0, NEG).astype(np.float32)
    half = np.arange(0, 64, 2, dtype=np.float32) / np.float32(64)
    inv_m = np.float32(1.0) / np.float32(10000.0) ** half
    inv_r = np.float32(1.0) / np.float32(10000.0) ** (np.arange(0, RK, 2, dtype=np.float32) / np.float32(RK))
    misc = np.zeros((P, 99), np.float32)
    tt = np.arange(T)
    for g, w in enumerate(POOLS):
        count = np.clip(tt + w // 2 - 1, 0, T - 1) - np.clip(tt - w // 2, 0, T - 1) + 1
        c = w / count
        misc[:, 16 * g:16 * g + 16] = np.concatenate([c[:8], c[-8:]])
    misc[:, 64], misc[:, 65] = inv_r, inv_m[p % 32]
    misc[:, 66] = np.where(p % 64 < 32, -1.0, 1.0)
    misc[:, 67:99] = inv_m
    return {
        "c_misc": misc,
        "c_delta": (np.arange(DELTAS)[None, :] - 3 * P - p[:, None]).astype(np.float32),
        "c_ident": np.eye(P, dtype=np.float32),
        "c_t": np.tile(t, (P, 1)),
        "c_angA": np.ascontiguousarray(np.tile(invA, (P, TT, 1))),
        "c_masks": masks,
    }


def columns_of(w):
    return w.reshape(-1, P, w.shape[1]).transpose(1, 0, 2)


def layout(x):
    w_in = x["w_in"][0]
    at = {"u": 0, "zs": 1024, "q": 2048, "k": 3584, "v": 5120, "za": 6656, "rs": 7168, "ra": 8192}
    d = {"x": x["x"]}
    loop_w = []
    for m in range(KT):
        parts = [columns_of(w_in[:, at["u"] + m * P:at["u"] + (m + 1) * P])]
        parts += [columns_of(w_in[:, at[n] + m * PC:at[n] + (m + 1) * PC]) for n in "qkv"]
        loop_w.append(np.concatenate([v.reshape(P, -1) for v in parts], 1))
    d["loop_w"] = np.stack(loop_w)
    src = {"glu": x["w_glu"][0], "so": x["w_ssm_out"][0], "ao": x["w_attn_out"][0], "wo": x["w_o"][0]}
    for n in ("zs", "za", "rs", "ra"):
        src[n] = w_in[:, at[n]:]
    a_in, r_in = x["a_w_in_2"][0], x["r_w_in_2"][0]
    lora = QL + KVL + MR
    src.update(pu=a_in[:, lora:], ga=a_in[:, lora + D:], gb=a_in[:, lora + 2 * D:], rq=r_in, rk=r_in[:, D:], rv=r_in[:, 2 * D:],
               rg=r_in[:, 4 * D:])
    for n, w in (("o", x["a_w_out_2"][0]), ("t", x["r_w_out_2"][0])):
        src[n + "a"], src[n + "b"] = w[:D], w[D:]
    src["lo"] = a_in[:, :lora]
    uq = x["a_w_uq_2"][0].reshape(QL, MH, MN + MR)
    ukv = x["a_w_ukv_2"][0].reshape(KVL, MH, MN + MV)
    panels = []
    for kind, i in stage_plan():
        if kind == "uq":
            h = slice(2 * i, 2 * i + 2)
            rope = uq[:, h, MN:]
            swap = np.concatenate([rope[:, :, MR // 2:], rope[:, :, :MR // 2]], 2)
            q = np.concatenate([v.reshape(QL, -1) for v in (uq[:, h, :MN], rope, swap)], 1)
            kv = np.concatenate([ukv[:, h, :MN].reshape(KVL, -1), ukv[:, h, MN:].reshape(KVL, -1)], 1)
            panels.append(np.concatenate([columns_of(q).reshape(P, -1), kv], 1))
            continue
        if kind in ("wo", "rv"):
            v = src[kind][(i % 2) * T:(i % 2 + 1) * T, (i // 2) * 512:(i // 2 + 1) * 512]
            panels.append(columns_of(v).reshape(P, -1))
            continue
        v = columns_of(src[kind][:, i * 256:(i + 1) * 256]).reshape(P, -1)
        panels.append(np.pad(v, ((0, 0), (0, PANEL - v.shape[1]))))
    d["panels"] = np.stack(panels)
    lam = [x["lam_re"][0], x["lam_im"][0], np.repeat(x["log_dt"][0][:, None], NST, 1)]
    d["ssm_par"] = np.stack([v.reshape(NTILE, P).T for v in lam], 1)
    b = np.zeros((P, 2, NTILE, 2, GCH), np.float32)
    c = np.zeros((P, KT, 2, SPM, 2, GCH), np.float32)
    for n, (bx, cx) in enumerate(((x["b_re"][0], x["c_re"][0]), (x["b_im"][0], x["c_im"][0]))):
        b2 = bx.reshape(NTILE, 2, NST, GCH)
        c2 = cx.reshape(KT, SPM, 2, GCH, NST)
        for g in range(2):
            b[g * NST:(g + 1) * NST, n, :, g, :] = b2[:, g].transpose(1, 0, 2)
            c[g * NST:(g + 1) * NST, :, n, :, g, :] = c2[:, :, g].transpose(3, 0, 1, 2)
    d["ssm_b"] = b.reshape(P, 2, NTILE, 32)
    d["ssm_c"] = c.reshape(P, KT, 256)
    qk = [np.repeat(x[n][0], HEADS, 0).reshape(KT, PC) for n in ("q_norm_w", "k_norm_w")]
    d["qk_w"] = np.stack(qk, 1)
    d["pool_w"] = x["a_pool_w_2"][0].reshape(4, 2, P, 256).transpose(2, 0, 1, 3)
    d["positions_2"] = x["positions_2"].reshape(1, T)
    d["pos2"] = x["positions_2"].reshape(TT, P).T
    d["decays"] = np.concatenate([x["r_decay_fwd_2"], x["r_decay_bwd_2"]], 1)
    d["final_g"] = x["final_norm_g_2"].reshape(1, D)
    d["pos1"] = x["positions"].reshape(TT, P).T
    vec = {"norm_w": "norm_w", "d_skip": "d_skip", "a_norm": "a_norm_g_2", "q_norm": "a_q_norm_g_2",
           "kv_norm": "a_kv_norm_g_2", "pool_scale": "a_pool_scale_2", "r_norm": "r_norm_g_2", "gn": "r_gn_g_2"}
    cols = np.zeros((P, 64), np.float32)
    for n, at_ in COLS.items():
        v = x[vec[n]].reshape(-1, P).T
        cols[:, at_:at_ + v.shape[1]] = v
    d["cols"] = cols
    d.update(constants())
    return {n: np.ascontiguousarray(v) for n, v in d.items()}


def kernel(**inputs):
    import concourse.bacc as bacc
    from concourse.bass_utils import run_bass_kernel_spmd

    arrays = layout({n: np.asarray(v) for n, v in inputs.items()})
    nc = bacc.Bacc("TRN2", target_bir_lowering=False, num_devices=1)
    a = {n: nc.dram_tensor(n, v.shape, mybir.dt.from_np(v.dtype), kind="ExternalInput").ap() for n, v in arrays.items()}
    out = nc.dram_tensor("out", (1, T, D), f32, kind="ExternalOutput").ap()
    build(nc, a, out)
    r = run_bass_kernel_spmd(nc, [arrays], core_ids=[0])
    return r.results[0]["out"]
```

```python
import concourse.bass as bass
from concourse import mybir
from contextlib import ExitStack
import math
import numpy as np

f32, f32r = mybir.dt.float32, mybir.dt.float32r
ALU = mybir.AluOpType
ACT = mybir.ActivationFunctionType
AX = mybir.AxisListType

T, D, P = 512, 1024, 128
TT, KT = T // P, D // P
EPS = 1e-6
NEG = -1e30
ROUND = 12582912.0
PI2_A, PI2_B, PI2_C = 6.28125, 0.0019340515136718750, float(2 * math.pi - 6.28125 - 0.0019340515136718750)
TURN = float(np.float32(1.0 / (2 * math.pi)))
PI2_SAFE = 6.283185
PI_SAFE = 3.1415925
GROUPS, GCH, NST = 64, 16, 64
NTILE = GROUPS * NST // P
SPM = 4
PACKW = 512 + SPM * 96 + SPM
HEADS, HD, NG = 8, 64, 3
NH = NG * HEADS
PH = NH // KT
PC = PH * HD
ROPE1 = 8
SCALE1 = 1.0 / math.sqrt(HD)
QL, KVL, MH, MN, MR, MV = 384, 128, 8, 128, 64, 128
SCALE2 = (MN + MR) ** -0.5
POOLS = (2, 4, 8, 16)
PAD = 8
RH, RK, RV = 4, 256, 512
DELTAS = T + 3 * P
LOOPW = KT * (P + 3 * PC)
ARENA = 53200
PANEL = 2048

COL_WIDTHS = {"norm_w": 8, "d_skip": 8, "a_norm": 8, "q_norm": 3, "kv_norm": 1, "pool_scale": 8, "r_norm": 8, "gn": 16}
COLS = {name: sum(list(COL_WIDTHS.values())[:k]) for k, name in enumerate(COL_WIDTHS)}

GATE_AT = (5, 7)
CHANNEL_STEPS, ATT_STEPS, MLA_STEPS, RET_STEPS, PHASE_STEPS = 46, 32, 26, 36, 30


class Steps:

    def __init__(self, eng, sem):
        self.eng, self.sem, self.n, self.i, self.per, self.start = eng, sem, 0, None, 0, 0

    def __call__(self, ins):
        ins.then_inc(self.sem, 1)
        self.n += 1
        return self.n

    def wait(self, tok=None):
        tok = self.n if tok is None else tok
        self.eng.wait_ge(self.sem, tok if self.i is None else self.i * self.per + tok)

    def loop(self, i, per):
        self.i, self.per, self.start = i, per, self.n

    def end(self, count):
        assert self.n - self.start == self.per, f"steps per turn: {self.n - self.start}, said {self.per}"
        self.n = self.start + count * self.per
        self.i = None


def stage_plan():
    plan = []
    for i in range(4):
        plan += [("zs", i), ("glu", i)]
    for i in range(4):
        plan += [("rs", i), ("so", i)]
    plan += [("za", 0), ("za", 1)]
    for i in range(4):
        plan += [("ra", i), ("ao", i)]
    plan += [("wo", i) for i in range(4)]
    plan += [("lo", i) for i in range(3)]
    for i in range(4):
        plan += [("pu", i), ("gb", i)]
    for i in range(4):
        plan += [("ga", i), ("uq", i)]
    plan += [("oo", i) for i in range(8)]
    for h in range(RH):
        plan += [("rq", h), ("rk", h), ("rv", 2 * h), ("rv", 2 * h + 1), ("rg", 2 * h), ("rg", 2 * h + 1)]
    plan += [("tt", i) for i in range(8)]
    return plan


def build(nc, a, out):
    ctx = ExitStack()
    with ctx:
        ctx.enter_context(nc.sbuf_tensor("arena", [P, ARENA], f32))
        base, placed = nc.sbuf_base - 4 * ARENA, {}
        ps = [ctx.enter_context(nc.psum_tensor(f"bank{b}", [P, 512], f32)) for b in range(8)]

        def sem(name):
            return ctx.enter_context(nc.semaphore(name))

        def at(off, *dims):
            return view("words", f32, off, dims)

        def parts_at(off, *dims):
            return view("parts", f32r, off, dims)

        def view(kind, dtype, off, dims):
            n, skip = int(np.prod(dims)), off % 8
            key = f"{kind}_{off}_{n}"
            if key not in placed:
                placed[key] = nc.alloc_sbuf_tensor_at(key, [P, skip + n], dtype, offset=base + 4 * (off - skip))
            v = placed[key][:, skip:skip + n]
            if len(dims) == 1:
                return v
            names = [f"d{k}" for k in range(len(dims))]
            return v.rearrange(f"p ({' '.join(names)}) -> p {' '.join(names)}",
                               **{m: d for m, d in zip(names[1:], dims[1:])})

        W = 0
        wl = at(W, LOOPW)
        w_u = wl[:, 0:KT * P].rearrange("p (k c) -> p k c", k=KT)
        w_x = [wl[:, KT * P + x * KT * PC:KT * P + (x + 1) * KT * PC].rearrange("p (k c) -> p k c", k=KT)
               for x in range(3)]
        raw = at(W, 2, PANEL)
        split_w = parts_at(4096, 2, 2, PANEL)
        o = LOOPW
        t_a = [at(o, 512), at(o + 512, 512)]; o += 1024
        u_cur = at(o, 512); o += 512
        qk_w = at(o, 2, PC); o += 2 * PC
        hT = at(8192, KT, T)
        QTOK, KTOK, VTOK, GT = 12288, 18432, 24576, 30720
        qkv_tok = [at(b, TT, NH * HD) for b in (QTOK, KTOK, VTOK)]
        gT = at(GT, KT, T)
        pack = at(34816, KT, PACKW)
        lhs_cur = at(42016, 4, P)
        E = at(42528, 2, 2, 512)
        e_t = [at(44576, 512), at(45088, 512)]
        bp = at(45600, 2, 512)
        gs = at(46624, 2, 512)
        hs = at(47648, 2, 2, 512)
        sq = at(49696, TT * PH, HD)
        y_sb = at(50464, 512)
        CB = 52300
        ident = at(CB, P)
        cols = at(CB + 128, 64)
        csA = at(CB + 192, 2, TT, ROPE1)
        rt = [at(CB + 256 + 96 * k, TT, PH, ROPE1) for k in range(4)]
        st = at(CB + 640, 160)
        half_m = st[:, 0:16]

        def col(name, k=0):
            return cols[:, COLS[name] + k:COLS[name] + k + 1]

        const_in = sem("const_in"); x_in = [sem(f"x_in{t}") for t in range(TT)]; par_in = sem("par_in"); ssm_in = sem("ssm_in")
        v_step = sem("v_step"); a_step = sem("a_step"); g_step = sem("g_step")
        x_sq = sem("x_sq"); x_ms = sem("x_ms"); x_rs = sem("x_rs"); x_nrm = sem("x_nrm")
        xt_mm = sem("xt_mm"); xt_ev = sem("xt_ev")
        ang_in = sem("ang_in"); trig_ready = sem("trig_ready"); ssm_exp = sem("ssm_exp"); ssm_dt = sem("ssm_dt")
        bb_ready = sem("bb_ready"); bt_mm = sem("bt_mm"); pack_ready = sem("pack_ready")
        wu_full = sem("wu_full"); wq_full = sem("wq_full"); wk_full = sem("wk_full"); wv_full = sem("wv_full")
        qkw_full = sem("qkw_full")
        u_mm = sem("u_mm"); q_mm = sem("q_mm"); k_mm = sem("k_mm"); v_mm = sem("v_mm")
        u_ev = sem("u_ev"); q_ev = sem("q_ev"); k_ev = sem("k_ev"); v_ev = sem("v_ev"); lhs_ready = sem("lhs_ready")
        bu_mm = sem("bu_mm"); bu_used = sem("bu_used"); c_mm = sem("c_mm"); h_ready = sem("h_ready")
        e_ready = sem("e_ready"); e_used = sem("e_used"); y_ready = sem("y_ready"); gelu_done = sem("gelu_done")
        ss_done = sem("ss_done"); ms_ready = sem("ms_ready"); rs_ready = sem("rs_ready"); scaled = sem("scaled")
        roped = sem("roped")
        w_full = [sem(f"w_full{s}") for s in range(2)]
        w_high = sem("w_high"); w_low = sem("w_low"); w_first = sem("w_first")
        h_split = sem("h_split"); g_high = sem("g_high"); g_low = sem("g_low"); nt_low = sem("nt_low")
        panel_mm = sem("panel_mm"); step_free = sem("step_free")
        mask_in = sem("mask_in")
        qg_ready = sem("qg_ready"); tr_mm = sem("tr_mm"); tr_ev = sem("tr_ev"); sc_mm = sem("sc_mm")
        sm_done = sem("sm_done"); nm_ready = sem("nm_ready"); p_ready = sem("p_ready"); pt_mm = sem("pt_mm")
        pt_ev = sem("pt_ev"); pv_mm = sem("pv_mm"); o_ev = sem("o_ev")
        glu_sig = sem("glu_sig"); ys_ready = sem("ys_ready"); m_ready = sem("m_ready")
        rs_sig = sem("rs_sig"); ot_mm = sem("ot_mm"); ya_ready = sem("ya_ready")
        y_high = sem("y_high"); y_low = sem("y_low")
        xr_in = sem("xr_in"); x1_ready = sem("x1_ready")
        out_done = sem("out_done"); passed = sem("passed")
        plan = stage_plan()
        NP = len(plan)
        first_of = {}
        for n, (kind, i) in enumerate(plan):
            first_of.setdefault(kind, n)

        x_tok, xn_tok = at(QTOK, TT, D), at(KTOK, TT, D)
        ssp = at(49696, 24, 32)
        lr, li, ldt = ssp[:, 0, :], ssp[:, 1, :], ssp[:, 2, :]
        tv = at(50464, 48)
        b_nat = at(GT, 2, NTILE, 32)
        bbs = at(GT + 2048, 2, NTILE, 32)
        bt_tmp = at(44576, NTILE, 32)
        tw = [at(VTOK + 1536 * k, NTILE, 48) for k in range(4)]
        angA = at(46624, 4, TT, ROPE1)

        masks = at(34816, 1280)
        qg = at(36096, 6, TT, P)
        qkT = at(39168, 6, T)
        sm = at(42240, 2, 1280)
        pr = at(44800, 2, 1280)
        pT = at(47360, 10, P)
        o_tok = at(48640, TT, HEADS * HD)
        mx, nmx, den, rden = (at(50688 + 8 * k, n) for k, n in enumerate((2, 2, 8, 8)))
        def pair_at(off, kts):
            return parts_at(off, kts, T), parts_at(off + kts * T, kts, T)

        hS = pair_at(12288, KT)
        gS = pair_at(20480, KT)
        prod = at(28672, 4, T)
        yS = pair_at(35072, KT)
        sig = at(43264, 2, 4, T)
        mT = at(20480, KT, T)
        oS = pair_at(24576, 4)
        mS = pair_at(35072, KT)
        x_res = at(28672, TT, D)

        squares = at(45312, TT, T)
        y2T = at(20480, 16, T)
        cosT, sinT = at(32768, 1024), at(33920, 1024)
        xn2 = at(35072, TT, D)
        upad = at(35072, 2, 2, T + 2 * PAD)
        win = at(37184, 2, 2, T + 2 * PAD)
        l_tok = at(39296, TT, QL + KVL)
        sig2 = at(41856, 2, 2, T)
        prod2 = at(43904, 2, T)
        pool_d = at(44928, 2, 2, T)
        cT = at(47360, 4, T)
        krT = at(49408, T)
        pool_w = at(49920, 4, 2, 256)
        ang, turns = at(47360, 1024), at(48512, 1024)
        cosR, sinR = cosT[:, 0:512], sinT[:, 0:512]
        cosM, sinM = cosT[:, 512:1024], sinT[:, 512:1024]
        delta = at(50944, DELTAS)
        decay = at(47360, RH, DELTAS)
        MB = CB + 256
        misc = at(MB, 67)
        corr = misc[:, 0:64].rearrange("p (i e) -> p i e", i=4)
        inv_cols = misc[:, 64:67]
        dec = at(MB + 103, 8)
        lsg = at(MB + 111, 6, 8)
        st2 = at(MB + 164, 160)
        qnT, qrT, knT = at(35072, 2, T), at(36096, T), at(36608, 2, T)
        v_m = at(37632, TT, 256)
        p_m = at(38656, 3, T)
        rot = at(40192, 2, T)
        pT_m = at(41216, 2, 4, T)
        gate_m, sig_m = at(45312, 2, T), at(46336, 2, T)
        q_r, k_r = at(35072, 2, T), at(36096, 2, T)
        v_r = at(37120, TT, RV)
        sd = at(39168, TT, T)
        on = at(41216, TT, RV)
        rot_r = at(41216, 4, T)
        gate_r, sig_r = at(43264, 4, T), at(45312, 4, T)
        dt1, dt2 = at(43264, DELTAS), at(43264 + DELTAS, DELTAS)
        y2S = parts_at(35072, 16, T), parts_at(20480, 16, T)
        gain = at(43264, D)

        misc_in = sem("misc_in"); pos_in = sem("pos_in"); ang2 = sem("ang2"); trig2 = sem("trig2")
        n_sq = sem("n_sq"); n_ms = sem("n_ms"); n_rs = sem("n_rs"); n_nrm = sem("n_nrm"); n_nrm_v = sem("n_nrm_v"); nt_mm = sem("nt_mm")
        nt_ev = sem("nt_ev"); lo_sq = sem("lo_sq"); lo_ms = sem("lo_ms"); lo_rs = sem("lo_rs"); lo_ev = sem("lo_ev")
        kr_used = sem("kr_used"); kr_rot = sem("kr_rot"); ct_mm = sem("ct_mm"); ct_ev = sem("ct_ev")
        poolw_in = sem("poolw_in"); u_pad = sem("u_pad"); pads = sem("pads"); d_ready = sem("d_ready"); pool_mm = sem("pool_mm")
        gb_sig = sem("gb_sig"); y2_ready = sem("y2_ready")
        pr_mm = sem("pr_mm"); pr_ev = sem("pr_ev"); rot_done = sem("rot_done"); ga_sig = sem("ga_sig")
        ga_ready = sem("ga_ready"); ga_done = sem("ga_done"); s_mm = sem("s_mm"); nmax = sem("nmax"); e_done = sem("e_done"); rcp = sem("rcp")
        p_norm = sem("p_norm"); t_mm = sem("t_mm"); t_ev = sem("t_ev"); o_mm = sem("o_mm"); ym_ready = sem("ym_ready")
        delta_in = sem("delta_in"); dec_abs = sem("dec_abs"); dec_exp = sem("dec_exp"); dec_arg = sem("dec_arg")
        dec_in = sem("dec_in")
        x2_ready = sem("x2_ready"); rqk_rot = sem("rqk_rot"); v_cp = sem("v_cp"); rs_mm = sem("rs_mm")
        sd_ready = sem("sd_ready"); rg_sig = sem("rg_sig"); rg_ready = sem("rg_ready")
        ro_mm = sem("ro_mm"); var_ready = sem("var_ready"); rstd = sem("rstd"); on_ready = sem("on_ready")
        rt_mm = sem("rt_mm"); yr_ready = sem("yr_ready"); x3_ready = sem("x3_ready"); gain_in = sem("gain_in")
        f_out = sem("f_out")
        PU, UQ, OO, RQ, TT_OUT = (first_of[k] for k in ("pu", "uq", "oo", "rq", "tt"))

        NKEY = [min(i + 1, 2) + 2 * (i + 1) for i in range(TT)]
        CH = [(n + 3) // 4 for n in NKEY]
        CHU = [CH[u % 4] for u in range(8)]

        def key_blocks(i):
            return [(0, b) for b in range(max(i - 1, 0), i + 1)] + [(1, b) for b in range(i + 1)] + \
                   [(2, b) for b in range(i + 1)]

        is_split = [kind != "uq" for kind, _ in plan]
        order = [sum(is_split[:n]) for n in range(NP)]
        splits = [n for n in range(NP) if is_split[n]]
        done = [n + {"ga": 2, "uq": 0}.get(kind, 1) for n, (kind, _) in enumerate(plan)]

        def width(n):
            kind = plan[n][0]
            return 1024 if kind == "ao" else PANEL

        def full_at(n):
            return 16 * (n // 2 + 1)

        def high_part(act, n, r=None, per=0):
            k = order[n]
            if r is None:
                act.wait_ge(w_full[n % 2], full_at(n))
                if k >= 2:
                    act.wait_ge(panel_mm, done[splits[k - 2]])
            else:
                act.wait_ge(w_full[n % 2], r * (8 * per) + full_at(n))
                act.wait_ge(panel_mm, r * per + (done[splits[k - 2]] if per == 12 else n - 2))
            w = width(n)
            nc.scalar.activation(split_w[:, k % 2, 0, 0:w], raw[:, n % 2, 0:w], ACT.Copy).then_inc(w_high, 1)

        def low_part(dve, n, r=None, per=0):
            k, w = order[n], width(n)
            c = {0: 0, 4: 2, 12: 12}[per]
            if r is None:
                dve.wait_ge(w_full[n % 2], full_at(n))
                dve.wait_ge(w_high, k)
            else:
                dve.wait_ge(w_full[n % 2], r * (8 * per) + full_at(n))
                dve.wait_ge(w_high, r * c + k)
            nc.vector.tensor_tensor(split_w[:, k % 2, 1, 0:w], raw[:, n % 2, 0:w], split_w[:, k % 2, 0, 0:w],
                                    ALU.subtract).then_inc(w_low, 1)

        def apart(eng):
            eng.sem_inc(passed, 1)

        block = ctx.enter_context(nc.Block())

        @block.sync
        def _(sp):
            sp.dma_start(ssp[:, 0:3, :], a["ssm_par"]).then_inc(par_in, 16)
            sp.dma_start(tv, a["c_t"]).then_inc(par_in, 16)
            sp.dma_start(ident, a["c_ident"]).then_inc(const_in, 16)
            sp.dma_start(cols, a["cols"]).then_inc(const_in, 16)
            sp.dma_start(angA[:, 0], a["c_angA"]).then_inc(const_in, 16)
            sp.dma_start(st[:, 20:24].bitcast(mybir.dt.int32), a["pos1"]).then_inc(const_in, 16)
            def turn(i):
                src = a["loop_w"][bass.ds(i, 1), :, :].rearrange("o p n -> (o p) n")
                for x, (full, done) in enumerate(((wq_full, q_mm), (wk_full, k_mm), (wv_full, v_mm))):
                    sp.wait_ge(done, i * 2 + 1)
                    b = KT * P + x * KT * PC
                    sp.dma_start(wl[:, b:b + KT * PC], src[:, b:b + KT * PC]).then_inc(full, 16)
                sp.wait_ge(scaled, i * 2 + 1)
                sp.dma_start(qk_w, a["qk_w"][bass.ds(i, 1)].rearrange("o x c -> o (x c)").to_broadcast([P, 2 * PC])
                             ).then_inc(qkw_full, 16)

            sp.dma_start(wl[:, 0:KT * P], a["loop_w"][0, :, 0:KT * P]).then_inc(wu_full, 16)
            sp.dma_start(b_nat, a["ssm_b"]).then_inc(ssm_in, 16)
            sp.dma_start(pack[:, :, 256:512], a["ssm_c"]).then_inc(ssm_in, 16)
            with sp.Fori(0, KT - 1) as i:
                turn(i)
                sp.wait_ge(u_mm, i + 2)
                sp.dma_start(wl[:, 0:KT * P], a["loop_w"][bass.ds(i + 1, 1), :, 0:KT * P].rearrange("o p n -> (o p) n")
                             ).then_inc(wu_full, 16)
            turn(KT - 1)
            sp.wait_ge(gelu_done, KT + 1)
            sp.dma_start(masks, a["c_masks"]).then_inc(mask_in, 16)
            sp.wait_ge(v_mm, 2 * KT + 1)
            for n in range(NP):
                if RQ <= n < TT_OUT:
                    if n > RQ:
                        continue
                    with sp.Fori(0, 2) as r:
                        for k in range(12):
                            sp.wait_ge(w_low, r * 12 + (order[RQ] + k - 2))
                            sp.dma_start(raw[:, (RQ + k) % 2, :], a["panels"][bass.ds(r * 12 + (RQ + k), 1), :, :]
                                         .rearrange("o p n -> (o p) n")).then_inc(w_full[(RQ + k) % 2], 16)
                    continue
                if n == 2:
                    sp.wait_ge(w_first, 2)
                elif n > 2 and is_split[n - 2]:
                    sp.wait_ge(w_low, order[n - 2])
                elif n > 2:
                    sp.wait_ge(panel_mm, done[n - 2])
                if plan[n] == ("wo", 3):
                    sp.wait_ge(m_ready, 16)
                    sp.dma_start(x_res, a["x"].rearrange("o (t p) d -> p (o t) d", p=P)).then_inc(xr_in, 16)
                if n == UQ + 3:
                    sp.wait_ge(pool_mm, 4)
                    sp.dma_start(delta, a["c_delta"]).then_inc(delta_in, 16)
                w = width(n)
                sp.dma_start(raw[:, n % 2, 0:w], a["panels"][n, :, 0:w]).then_inc(w_full[n % 2], 16)
                if n == first_of["ra"] + 2:
                    sp.wait_ge(ya_ready, 4)
                    sp.dma_start(misc, a["c_misc"]).then_inc(misc_in, 16)
                    sp.dma_start(dec, a["decays"].to_broadcast([P, 8])).then_inc(dec_in, 16)
                    sp.dma_start(turns[:, 0:T].bitcast(mybir.dt.int32), a["positions_2"].to_broadcast([P, T])).then_inc(pos_in, 16)
                    sp.dma_start(pool_w, a["pool_w"]).then_inc(poolw_in, 16)
            sp.wait_ge(yr_ready, 17)
            sp.dma_start(gain, a["final_g"].to_broadcast([P, D])).then_inc(gain_in, 16)
            for t in range(TT):
                sp.wait_ge(f_out, t + 1)
                sp.dma_start(out[0, t * P:(t + 1) * P, :], x_res[:, t, :]).then_inc(out_done, 16)
            sp.wait_ge(out_done, 16 * TT)

        @block.tensor
        def _(pe):
            mm = nc.tensor.matmul
            for first in (u_mm, q_mm, k_mm, v_mm, c_mm, tr_mm, sc_mm, pt_mm, pv_mm, s_mm, t_mm, o_mm, ro_mm):
                pe.sem_inc(first, 1)
            pe.wait_ge(const_in, 64)
            for k in range(KT):
                if k == 0:
                    pe.wait_ge(x_nrm, TT)
                for t in range(TT):
                    last = nc.tensor.transpose(ps[k][:, t * P:(t + 1) * P], xn_tok[:, t, k * P:(k + 1) * P], ident)
                last.then_inc(xt_mm, 1)
            def input_matrices():
                pe.wait_ge(bb_ready, 2)
                for m in range(KT):
                    for c in range(2):
                        last = nc.tensor.transpose(ps[3 + m // 2][:, (m % 2) * 256 + c * P:(m % 2) * 256 + (c + 1) * P],
                                                   bbs[:, c, 4 * m:4 * m + 4, :].rearrange("p a b -> p (a b)"), ident)
                    if m % 2:
                        last.then_inc(bt_mm, 1)
                pe.wait_ge(pack_ready, KT // 2)

            def qkv(i, x, half, full, bank, done):
                if half == 0:
                    pe.wait_ge(full, i * 16 + 16)
                for t in (2 * half, 2 * half + 1):
                    for k in range(KT):
                        last = mm(ps[bank][:, (t % 2) * PC:(t % 2 + 1) * PC], hT[:, k, t * P:(t + 1) * P], w_x[x][:, k, :],
                                  start=(k == 0), stop=(k == KT - 1))
                last.then_inc(done, 1)

            def bu(i, j):
                if j == 0:
                    pe.wait_ge(u_ev, i + 1 + 1)
                    pe.wait_ge(lhs_ready, i + 1)
                pe.wait_ge(bu_used, i * 4 + j + 1)
                r = slice(32 * j, 32 * j + 32)
                for c in range(2):
                    last = mm(ps[5 + c][:, :], lhs_cur[r, c, :], u_cur[r, :], start=True, stop=True)
                last.then_inc(bu_mm, 1)

            def cy(i, j):
                pe.wait_ge(h_ready, i * 4 + (j + 1))
                if j == 0:
                    pe.wait_ge(y_ready, i + 1)
                for c in range(2):
                    last = mm(ps[7][32 * j:32 * j + 32, :], lhs_cur[:, 2 + c, 32 * j:32 * j + 32], hs[:, j % 2, c, :],
                              start=(c == 0), stop=(c == 1))
                last.then_inc(c_mm, 1)

            def channels(i):
                pe.wait_ge(wu_full, i * 16 + 16)
                pe.wait_ge(u_ev, i + 1)
                for k in range(KT):
                    last = mm(ps[0][:, :], w_u[:, k, :], hT[:, k, :], start=(k == 0), stop=(k == KT - 1))
                last.then_inc(u_mm, 1)

            def turn(i, more, first=False):
                pe.wait_ge(v_ev, i * 2 + 1)
                qkv(i, 0, 0, wq_full, 1, q_mm)
                if first:
                    qkv(i, 0, 1, wq_full, 2, q_mm)
                    input_matrices()
                bu(i, 0)
                if not first:
                    qkv(i, 0, 1, wq_full, 2, q_mm)
                bu(i, 1)
                pe.wait_ge(k_ev, i * 2 + 1)
                qkv(i, 1, 0, wk_full, 3, k_mm)
                cy(i, 0)
                bu(i, 2)
                qkv(i, 1, 1, wk_full, 4, k_mm)
                cy(i, 1)
                bu(i, 3)
                pe.wait_ge(q_ev, i * 2 + 3)
                qkv(i, 2, 0, wv_full, 1, v_mm)
                cy(i, 2)
                qkv(i, 2, 1, wv_full, 2, v_mm)
                if more:
                    channels(i + 1)
                cy(i, 3)

            pe.wait_ge(xt_ev, KT)
            channels(0)
            turn(0, True, first=True)
            with pe.Fori(1, KT - 1) as i:
                turn(i, True)
            turn(KT - 1, False)

            def heads_t(p, x):
                if x == 0:
                    pe.wait_ge(qg_ready, p + 1)
                    pe.wait_ge(sm_done, p * 8 + 1)
                if x >= 3:
                    pe.wait_ge(tr_ev, p * 6 + (x - 2))
                for t in range(TT):
                    last = nc.tensor.transpose(ps[x % 3][:, t * P:(t + 1) * P], qg[:, x, t, :], ident)
                last.then_inc(tr_mm, 1)

            def head_pair(p, more):
                pe.wait_ge(tr_ev, p * 6 + 6)

                def scores(u):
                    hh, i = u // 4, u % 4
                    r = slice(64 * hh, 64 * hh + 64)
                    pe.wait_ge(sm_done, p * 8 + u + 1)
                    lo = max(i - 1, 0) * P
                    q = slice(i * P, (i + 1) * P)
                    mm(ps[0][:, 0:(i + 1) * P - lo], qkT[r, 0, q], qkT[r, 3, lo:(i + 1) * P], start=True, stop=True)
                    for g in (1, 2):
                        last = mm(ps[g][:, 0:(i + 1) * P], qkT[r, g, q], qkT[r, 3 + g, 0:(i + 1) * P], start=True, stop=True)
                    last.then_inc(sc_mm, 1)

                def probs_t(u):
                    pe.wait_ge(p_ready, p * 8 + (u + 2))
                    pe.wait_ge(pt_ev, p * sum(CHU) + sum(CHU[:u]) + 1)
                    n = NKEY[u % 4]
                    for c in range(CHU[u]):
                        for b in range(4 * c, min(4 * c + 4, n)):
                            last = nc.tensor.transpose(ps[3 + c][:, (b % 4) * P:(b % 4 + 1) * P],
                                                       pr[:, u % 2, b * P:(b + 1) * P], ident)
                        last.then_inc(pt_mm, 1)

                def pv(u):
                    hh, i = u // 4, u % 4
                    pe.wait_ge(pt_ev, p * sum(CHU) + sum(CHU[:u + 1]) + 1)
                    pe.wait_ge(o_ev, p * 8 + max(u - 1, 0) + 1)
                    blocks = key_blocks(i)
                    for b, (g, kt) in enumerate(blocks):
                        c0 = p * 128 + g * HEADS * HD
                        last = mm(ps[6 + u % 2][:, 0:P], pT[:, b, :], qkv_tok[2][:, kt, bass.ds(c0, P)],
                                  start=(b == 0), stop=(b == len(blocks) - 1))
                    last.then_inc(pv_mm, 1)

                scores(0)
                scores(1)
                for u in range(8):
                    if u < 6:
                        scores(u + 2)
                    probs_t(u)
                    if u >= 1:
                        pv(u - 1)
                    if more and u >= 6:
                        for x in range(3 * (u - 6), 3 * (u - 5)):
                            heads_t(p + 1, x)
                pv(7)

            for x in range(6):
                heads_t(0, x)
            with pe.Fori(0, 3) as p:
                head_pair(p, True)
            head_pair(3, False)

            def mm3(dst, lhs, rhs, start, stop):
                mm(dst, lhs[0], rhs[0], start=start, stop=False)
                mm(dst, lhs[0], rhs[1], start=False, stop=False)
                return mm(dst, lhs[1], rhs[0], start=False, stop=stop)

            def parts(slot, kts, cols_of=256):
                return [split_w[:, slot, h, 0:kts * cols_of].rearrange("p (k c) -> p k c", k=kts) for h in range(2)]

            def split_panel(n, kts, cols_of=256):
                if n == 0:
                    pe.wait_ge(w_first, 2)
                else:
                    pe.wait_ge(w_low, order[n])
                return parts(order[n] % 2, kts, cols_of)

            def panel(n, bank0, x):
                kts = 4 if plan[n][0] == "ao" else 8
                w = split_panel(n, kts)
                for h in range(2):
                    for k in range(kts):
                        last = mm3(ps[bank0 + h][:, :], [v[:, k, h * P:(h + 1) * P] for v in w], [v[:, k, :] for v in x],
                                   start=(k == 0), stop=(k == kts - 1))
                last.then_inc(panel_mm, 1)

            def token_panel(n, bank0, x, k0, first, last_one):
                w = split_panel(n, 4, 512)
                for t in range(TT):
                    for k in range(4):
                        last = mm3(ps[bank0 + t][:, :], [v[:, k0 + k, t * P:(t + 1) * P] for v in x], [v[:, k, :] for v in w],
                                   start=(first and k == 0), stop=(last_one and k == 3))
                last.then_inc(panel_mm, 1)

            pe.wait_ge(o_ev, 33)
            pe.wait_ge(sm_done, 33)
            pe.wait_ge(h_split, 2)
            for s in range(15):
                b = 4 * (s % 2)
                pe.wait_ge(step_free, s + 1)
                if s < 13:
                    x = (hS, gS) if s < 4 else (hS, yS) if s < 8 else (hS, hS) if s == 8 else (hS, oS)
                    if s == 9:
                        pe.wait_ge(ya_ready, 2)
                    panel(2 * s, b, x[0])
                    if s == 0:
                        pe.wait_ge(g_low, 2)
                    if s == 4:
                        pe.wait_ge(ys_ready, 8)
                    if s == 9:
                        pe.wait_ge(ya_ready, 4)
                    if s == 8:
                        pe.wait_ge(step_free, 10)
                        for c in range(4):
                            for t in range(TT):
                                last = nc.tensor.transpose(ps[4 + c][:, t * P:(t + 1) * P], o_tok[:, t, c * P:(c + 1) * P], ident)
                            last.then_inc(ot_mm, 1)
                    panel(2 * s + 1, b + 2, x[1])
                else:
                    for h in range(2):
                        pe.wait_ge(m_ready, 8 + 4 * (h + 1))
                        token_panel(2 * s + h, b, mS, 4 * h, h == 0, h == 1)


            def transposes(t0, x, evac, n0):
                pe.wait_ge(n_nrm, (t0 + TT) // 2)
                pe.wait_ge(n_nrm_v, (t0 + TT) // 2)
                for k in range(KT):
                    if n0:
                        pe.wait_ge(evac, n0 - KT + k + 1)
                    for t in range(TT):
                        last = nc.tensor.transpose(ps[k][:, t * P:(t + 1) * P], x[:, t, k * P:(k + 1) * P], ident)
                    last.then_inc(nt_mm, 1)
                pe.wait_ge(nt_low, n0 + KT)

            transposes(0, xn2, nt_low, 0)

            def slot(n):
                pe.wait_ge(w_full[n % 2], full_at(n))
                return raw[:, n % 2, :]

            n = first_of["lo"]
            for x in range(2):
                w = split_panel(n + x, KT)
                for t in range(TT):
                    c0 = (t % 2) * 256
                    for k in range(KT):
                        last = mm3(ps[4 + 2 * x + t // 2][:, c0:c0 + 256], [v[:, k, t * P:(t + 1) * P] for v in hS],
                                   [v[:, k, :] for v in w], start=(k == 0), stop=(k == KT - 1))
                last.then_inc(panel_mm, 1)
            panel(n + 2, 0, hS)

            def pool_product(i):
                b = 4 * (i % 2)
                pe.wait_ge(d_ready, i + 1)
                for c in range(2):
                    for k in range(2):
                        last = mm(ps[b + c][:, :], pool_w[:, i, k, c * P:(c + 1) * P], pool_d[:, i % 2, k, :],
                                  start=(k == 0), stop=(k == 1))
                last.then_inc(pool_mm, 1)

            pe.wait_ge(poolw_in, 16)
            for i in range(4):
                b = 4 * (i % 2)
                if i == 0:
                    pe.wait_ge(kr_used, 2)
                if i == 1:
                    pe.wait_ge(lo_ev, 12)
                    for k in range(4):
                        for t in range(TT):
                            last = nc.tensor.transpose(ps[4 + k][:, t * P:(t + 1) * P], l_tok[:, t, k * P:(k + 1) * P], ident)
                        last.then_inc(ct_mm, 1)
                    pe.wait_ge(ct_ev, 4)
                if i >= 2:
                    pe.wait_ge(step_free, 16 + i + 1)
                panel(PU + 2 * i, b, hS)
                if i >= 1:
                    pool_product(i - 1)
                panel(PU + 2 * i + 1, b + 2, hS)
            pool_product(3)

            pe.wait_ge(kr_rot, 1)
            with pe.Fori(0, 2) as r:
                for q in range(2):
                    def cnt(c, k):
                        return r * (2 * c) + (q * c + k)

                    n = UQ + 2 * q
                    if q == 0:
                        pe.wait_ge(step_free, 22)
                    pe.wait_ge(ym_ready, cnt(2, 0) + 1)
                    pe.wait_ge(t_ev, cnt(8, 0) + 1)
                    pe.wait_ge(w_full[n % 2], r * 32 + full_at(n))
                    w = raw[:, n % 2, 0:3 * 512].rearrange("p (k c) -> p k c", k=3)
                    wkv = raw[:, n % 2, 3 * 512:2048]
                    for c in range(4):
                        for k in range(3):
                            last = mm(ps[c][:, :], w[:, k, c * P:(c + 1) * P], cT[:, k, :], start=(k == 0), stop=(k == 2))
                        last.then_inc(pr_mm, 1)
                    for c in range(2):
                        pe.wait_ge(pr_ev, cnt(6, c + 1))
                        mm(ps[c][:, :], wkv[:, c * P:(c + 1) * P], cT[:, 3, :], start=True, stop=True).then_inc(pr_mm, 1)
                    pe.wait_ge(rot_done, cnt(1, 1))
                    for h in range(2):
                        for t in range(2 * h, 2 * h + 2):
                            last = mm(ps[2 + h][:, (t % 2) * 256:(t % 2 + 1) * 256], cT[:, 3, t * P:(t + 1) * P],
                                      wkv[:, 256:512], start=True, stop=True)
                        if h == 0:
                            last.then_inc(pr_mm, 1)
                    last.then_inc(panel_mm, 1)

                    def s_block(u):
                        h, i = u // 4, u % 4
                        if u < 3:
                            pe.wait_ge(e_done, cnt(8, 0) + 1)
                        else:
                            pe.wait_ge(e_done, cnt(8, u - 2) + 1)
                        b = 4 + u % 3
                        qs = slice(i * P, (i + 1) * P)
                        hr = slice(64 * h, 64 * h + 64)
                        mm(ps[b][:, :], qnT[:, h, qs], knT[:, h, :], start=True, stop=False)
                        mm(ps[b][:, :], qrT[hr, qs], krT[hr, :], start=False, stop=True).then_inc(s_mm, 1)

                    def t_block(u):
                        b = (7, 0)[u % 2]
                        pe.wait_ge(p_norm, cnt(8, u + 2))
                        if u >= 2:
                            pe.wait_ge(t_ev, cnt(8, u - 1) + 1)
                        for k in range(4):
                            last = nc.tensor.transpose(ps[b][:, k * P:(k + 1) * P], p_m[:, u % 3, k * P:(k + 1) * P], ident)
                        last.then_inc(t_mm, 1)

                    def o_block(h):
                        pe.wait_ge(t_ev, cnt(8, 4 * h + 4) + 1)
                        for k in range(4):
                            last = mm(ps[2 + h][:, :], v_m[:, k, h * P:(h + 1) * P], pT_m[:, h, k, :],
                                      start=(k == 0), stop=(k == 3))
                        last.then_inc(o_mm, 1)

                    pe.wait_ge(pr_ev, cnt(6, 4))
                    s_block(0)
                    s_block(1)
                    pe.wait_ge(w_low, r * 2 + order[n - 1])
                    w = parts(order[n - 1] % 2, KT)
                    for c in range(2):
                        for k in range(KT):
                            last = mm3(ps[c][:, :], [v[:, k, c * P:(c + 1) * P] for v in w], [v[:, k, :] for v in hS],
                                       start=(k == 0), stop=(k == KT - 1))
                    last.then_inc(panel_mm, 1)
                    s_block(2)
                    t_block(0)
                    pe.wait_ge(ga_ready, cnt(2, 2))
                    for u in range(1, 8):
                        if u < 6:
                            s_block(u + 2)
                        t_block(u)
                        if u == 5:
                            pe.wait_ge(pr_ev, cnt(6, 6))
                            o_block(0)
                    o_block(1)

            def w_out(n, s, y0):
                pe.wait_ge(step_free, s + 1)
                for j in range(4):
                    pe.wait_ge(y_low, y0 + j + 1)
                    token_panel(n + j, 4 * (s % 2), y2S, 4 * j, j == 0, j == 3)

            pe.wait_ge(ym_ready, 9)
            pe.wait_ge(y2_ready, 8)
            w_out(OO, 20, 0)
            w_out(OO + 4, 21, 0)
            transposes(TT, xn2, nt_low, KT)
            with pe.Fori(0, 2) as r:
                for q in range(2):
                    def cnt(c, k):
                        return r * (2 * c) + (q * c + k)

                    def rpanel(x, kts, cols_of=256):
                        n = RQ + 6 * q + x
                        pe.wait_ge(w_low, r * 12 + order[n])
                        return parts(order[n] % 2, kts, cols_of)

                    def feature(x, bank):
                        w = rpanel(x, KT)
                        for c in range(2):
                            for k in range(KT):
                                last = mm3(ps[bank + c][:, :], [v[:, k, c * P:(c + 1) * P] for v in w],
                                           [v[:, k, :] for v in hS], start=(k == 0), stop=(k == KT - 1))
                        last.then_inc(panel_mm, 1)

                    pe.wait_ge(on_ready, cnt(4, 0) + 1)
                    feature(0, 0)
                    pe.wait_ge(rg_ready, cnt(4, 0) + 1)
                    feature(1, 2)
                    pe.wait_ge(yr_ready, cnt(4, 0) + 1)
                    for x in range(2):
                        w = rpanel(2 + x, 4, 512)
                        for t in range(TT):
                            for k in range(4):
                                last = mm3(ps[4 + t][:, :], [v[:, 4 * x + k, t * P:(t + 1) * P] for v in hS],
                                           [v[:, k, :] for v in w], start=(x == 0 and k == 0), stop=(x == 1 and k == 3))
                        last.then_inc(panel_mm, 1)
                    pe.wait_ge(rqk_rot, cnt(2, 2))
                    for j in range(TT):
                        for k in range(2):
                            last = mm(ps[j][:, :], k_r[:, k, j * P:(j + 1) * P], q_r[:, k, :], start=(k == 0), stop=(k == 1))
                        last.then_inc(rs_mm, 1)
                    pe.wait_ge(v_cp, cnt(4, 2))
                    feature(4, 4)
                    pe.wait_ge(v_cp, cnt(4, 4))
                    pe.wait_ge(sd_ready, cnt(4, 4))
                    for i in range(TT):
                        b = (6, 7, 0, 1)[i]
                        for j in range(TT):
                            last = mm(ps[b][:, :], sd[:, j, i * P:(i + 1) * P], v_r[:, j, :], start=(j == 0), stop=(j == 3))
                        last.then_inc(ro_mm, 1)
                    feature(5, 2)
                    pe.wait_ge(rg_ready, cnt(4, 2) + 1)
                    for i in range(TT):
                        pe.wait_ge(on_ready, cnt(4, i + 2))
                        for c in range(4):
                            last = nc.tensor.transpose(ps[4 + i][:, c * P:(c + 1) * P], on[:, i, c * P:(c + 1) * P], ident)
                        last.then_inc(rt_mm, 1)

            pe.wait_ge(yr_ready, 17)
            w_out(TT_OUT, 22, 4)
            w_out(TT_OUT + 4, 23, 4)

        @block.scalar
        def _(act):
            S = Steps(act, a_step)
            for first in (u_ev, q_ev, k_ev, v_ev, gelu_done, p_ready, pt_ev, e_done, t_ev):
                act.sem_inc(first, 1)
            av = nc.scalar.activation
            for t in range(TT):
                act.dma_start(x_tok[:, t, :], a["x"][0, t * P:(t + 1) * P, :]).then_inc(x_in[t], 16)
            act.wait_ge(par_in, 32)
            av(ssp[:, 3, :], ldt, ACT.Exp).then_inc(ssm_exp, 1)
            act.wait_ge(ssm_dt, 1)
            av(ssp[:, 5, :], ssp[:, 4, :], ACT.Exp).then_inc(ssm_exp, 1)
            for t in range(TT):
                act.wait_ge(x_in[t], 16)
                av(xn_tok[:, t, :], x_tok[:, t, :], ACT.Square, accum_out=st[:, 24 + t:25 + t]).then_inc(x_sq, 1)
            act.wait_ge(x_rs, 1)
            act.wait_ge(x_sq, TT)
            for t in range(TT):
                av(xn_tok[:, t, :], x_tok[:, t, :], ACT.Copy, scale=st[:, 32 + t:33 + t]).then_inc(x_nrm, 1)
            for k in range(KT):
                act.wait_ge(xt_mm, k + 1)
                av(hT[:, k, :], ps[k][:, :], ACT.Copy, scale=col("norm_w", k)).then_inc(xt_ev, 1)
            act.wait_ge(ang_in, 1)
            av(tw[1], tw[0], ACT.Sin, scale=PI2_SAFE)
            av(tw[2], tw[0], ACT.Sin, scale=PI_SAFE).then_inc(trig_ready, 1)
            act.wait_ge(ang_in, 2)
            av(angA[:, 1], angA[:, 3], ACT.Sin, scale=PI2_SAFE)
            av(angA[:, 2], angA[:, 3], ACT.Sin, scale=PI_SAFE).then_inc(trig_ready, 1)

            def split(x, i, half, bank, done, evac):
                act.wait_ge(done, i * 2 + (half + 2))
                src = ps[bank][:, 0:2 * PC].rearrange("p (t c) -> p t c", t=2)
                dst = qkv_tok[x][:, 2 * half:2 * half + 2, bass.ds(i * PC, PC)]
                if x == 2:
                    av(dst, src, ACT.Copy).then_inc(evac, 1)
                    return
                av(dst, src, ACT.Copy)
                if half == 0:
                    act.wait_ge(ss_done, i * 2 + x + 1)
                av(sq[:, 2 * half * PH:(2 * half + 2) * PH, :].rearrange("p a b -> p (a b)"), ps[bank][:, 0:2 * PC],
                   ACT.Square).then_inc(evac, 1)

            for m in range(KT // 2):
                act.wait_ge(bt_mm, m + 1)
                av(pack[:, 2 * m:2 * m + 2, 0:256], ps[3 + m][:, :].rearrange("p (m c) -> p m c", m=2), ACT.Copy).then_inc(pack_ready, 1)
            act.wait_ge(pack_ready, KT // 2)
            act.wait_ge(bb_ready, 3)
            with act.Fori(0, KT) as i:
                act.wait_ge(u_mm, i + 1 + 1)
                act.wait_ge(y_ready, i + 1)
                av(u_cur, ps[0][:, :], ACT.Copy).then_inc(u_ev, 1)
                act.wait_ge(c_mm, i * 4 + 1)
                av(lhs_cur.rearrange("p a b -> p (a b)"), pack[:, bass.ds(i, 1), 0:512].rearrange("p o n -> p (o n)"),
                   ACT.Copy).then_inc(lhs_ready, 1)
                split(0, i, 0, 1, q_mm, q_ev)
                split(0, i, 1, 2, q_mm, q_ev)
                split(1, i, 0, 3, k_mm, k_ev)
                split(1, i, 1, 4, k_mm, k_ev)
                split(2, i, 0, 1, v_mm, v_ev)
                split(2, i, 1, 2, v_mm, v_ev)
                act.wait_ge(y_ready, i + 1 + 1)
                av(gT[:, bass.ds(i, 1), :].rearrange("p o n -> p (o n)"), y_sb, ACT.Gelu_apprx_tanh).then_inc(gelu_done, 1)

            act.wait_ge(gelu_done, KT + 1)
            act.wait_ge(y_ready, KT + 1)
            for x in range(6):
                act.wait_ge(roped, 2 * KT - 1 + x // 3)
                ins = av(qg[:, x], qkv_tok[x // 3][:, :, (x % 3) * 512:(x % 3) * 512 + P], ACT.Copy)
            ins.then_inc(qg_ready, 1)
            def heads_evac(p, x):
                if x == 0:
                    act.wait_ge(sc_mm, p * 8 + 1)
                act.wait_ge(tr_mm, p * 6 + (x + 2))
                av(qkT[:, x, :], ps[x % 3][:, :], ACT.Copy).then_inc(tr_ev, 1)

            def head_pair(p, more):
                def exps(u):
                    act.wait_ge(nm_ready, p * 8 + (u + 1))
                    if u >= 2:
                        act.wait_ge(pt_mm, p * sum(CHU) + sum(CHU[:u - 1]) + 1)
                    if u < 2:
                        act.wait_ge(pt_mm, p * sum(CHU) + 1)
                    if u == 0:
                        act.wait_ge(o_ev, p * 8 + 1)
                    n = NKEY[u % 4] * P
                    av(pr[:, u % 2, 0:n], sm[:, u % 2, 0:n], ACT.Exp, bias=nmx[:, u % 2:u % 2 + 1],
                       accum_out=den[:, u:u + 1]).then_inc(p_ready, 1)

                def probs_evac(u):
                    act.wait_ge(pv_mm, p * 8 + u + 1)
                    for c in range(CHU[u]):
                        n = min(4, NKEY[u % 4] - 4 * c)
                        act.wait_ge(pt_mm, p * sum(CHU) + (sum(CHU[:u]) + c + 1) + 1)
                        av(pT[:, 4 * c:4 * c + n, :].rearrange("p a b -> p (a b)"), ps[3 + c][:, 0:n * P],
                           ACT.Copy).then_inc(pt_ev, 1)

                exps(0)
                for u in range(8):
                    if u < 7:
                        exps(u + 1)
                    probs_evac(u)
                    if more and u >= 6:
                        for x in range(3 * (u - 6), 3 * (u - 5)):
                            heads_evac(p + 1, x)

            for x in range(6):
                heads_evac(0, x)
            with act.Fori(0, 3) as p:
                head_pair(p, True)
            head_pair(3, False)

            act.wait_ge(sm_done, 33)
            act.wait_ge(o_ev, 33)
            gR = gT.rearrange("p a b -> p (a b)")
            for h in range(2):
                av(gS[0][:, 4 * h:4 * h + 4, :].rearrange("p a b -> p (a b)"), gR[:, 2048 * h:2048 * h + 2048], ACT.Copy).then_inc(g_high, 1)
            act.wait_ge(h_split, 2)
            high_part(act, 1)
            for s in range(13):
                act.wait_ge(step_free, s + 1)
                b = 4 * (s % 2)
                sg = sig[:, s % 2]
                if s < 4 or s == 8:
                    for c in range(4):
                        if c % 2 == 0:
                            act.wait_ge(panel_mm, 2 * s + 1 + c // 2)
                        if c == 0:
                            high_part(act, 2 * s + 2)
                        av(sg[:, c, :], ps[b + c][:, :], ACT.Sigmoid).then_inc(glu_sig, 1)
                    high_part(act, 2 * s + 3)
                else:
                    for c in range(2):
                        act.wait_ge(panel_mm, 2 * s + 1)
                        if c == 0:
                            high_part(act, 2 * s + 2)
                        av(sg[:, c, :], ps[b + c][:, :], ACT.Sigmoid).then_inc(rs_sig, 1)
                    high_part(act, 2 * s + 3)
                if s == 10:
                    act.wait_ge(ang2, 1)
                    av(sinT, ang, ACT.Sin, scale=PI2_SAFE)
                    av(cosT, ang, ACT.Sin, scale=PI_SAFE).then_inc(trig2, 1)
            def square(ready, k, c):
                act.wait_ge(ready, TT * (c + 1))
                if k or c:
                    act.wait_ge(n_sq, 2 * TT * k + TT * c)
                for t in range(TT):
                    av(squares[:, t, :], x_res[:, t, c * 512:(c + 1) * 512], ACT.Square,
                       accum_out=st2[:, (8, 20)[c] + t:(8, 20)[c] + t + 1]).then_inc(n_sq, 1)

            high_part(act, 28)
            high_part(act, 29)
            square(x1_ready, 0, 0)
            high_part(act, 30)

            def norm(n, ready, cname, ahead):
                square(ready, n, 1)
                high_part(act, ahead)
                act.wait_ge(n_rs, n + 1)
                act.wait_ge(n_sq, 2 * TT * (n + 1))
                for t in (0, 1):
                    av(xn2[:, t, :], x_res[:, t, :], ACT.Copy, scale=st2[:, 16 + t:17 + t]).then_inc(n_nrm, 1)
                for k in range(KT):
                    act.wait_ge(nt_mm, KT * n + k + 1)
                    av(hS[0][:, k, :], ps[k][:, :], ACT.Copy, scale=col(cname, k)).then_inc(nt_ev, 1)

            norm(0, x1_ready, "a_norm", 31)
            n = first_of["lo"]
            for h in range(2):
                act.wait_ge(panel_mm, n + 1 + h)
                high_part(act, n + 2 + h)
                for t in range(TT):
                    src = ps[4 + 2 * h + t // 2][:, (t % 2) * 256:(t % 2 + 1) * 256]
                    if h == 0:
                        av(l_tok[:, t, 0:256], src, ACT.Square, accum_out=st2[:, 32 + t:33 + t]).then_inc(lo_sq, 1)
                    else:
                        av(l_tok[:, t, 256:384], src[:, 0:P], ACT.Square, accum_out=st2[:, 36 + t:37 + t]).then_inc(lo_sq, 1)
                        av(l_tok[:, t, 384:512], src[:, P:2 * P], ACT.Square, accum_out=st2[:, 44 + t:45 + t]).then_inc(lo_sq, 1)
            high_part(act, PU + 1)
            act.wait_ge(lo_rs, 1)
            act.wait_ge(lo_sq, 12)
            for t in range(TT):
                a0 = ps[4 + t // 2][:, (t % 2) * 256:(t % 2 + 1) * 256]
                a1 = ps[6 + t // 2][:, (t % 2) * 256:(t % 2 + 1) * 256]
                av(l_tok[:, t, 0:256], a0, ACT.Copy, scale=st2[:, 56 + t:57 + t]).then_inc(lo_ev, 1)
                av(l_tok[:, t, 256:384], a1[:, 0:P], ACT.Copy, scale=st2[:, 56 + t:57 + t]).then_inc(lo_ev, 1)
                av(l_tok[:, t, 384:512], a1[:, P:2 * P], ACT.Copy, scale=st2[:, 60 + t:61 + t]).then_inc(lo_ev, 1)
            act.wait_ge(pads, 1)
            for i in range(4):
                b = 4 * (i % 2)
                act.wait_ge(step_free, 16 + i + 1)
                act.wait_ge(panel_mm, PU + 2 * i + 1)
                high_part(act, PU + 2 * i + 2)
                for c in range(2):
                    av(upad[:, i % 2, c, PAD:PAD + T], ps[b + c][:, :], ACT.Copy).then_inc(u_pad, 1)
                if i == 0:
                    for k in range(4):
                        act.wait_ge(ct_mm, k + 1)
                        av(cT[:, k, :], ps[4 + k][:, :], ACT.Copy, scale=col("q_norm", k) if k < 3 else col("kv_norm")).then_inc(ct_ev, 1)
                act.wait_ge(panel_mm, PU + 2 * i + 2)
                if i < 3:
                    high_part(act, PU + 2 * i + 3)
                for c in range(2):
                    av(sig2[:, i % 2, c, :], ps[b + 2 + c][:, :], ACT.Sigmoid).then_inc(gb_sig, 1)

            act.wait_ge(y2_ready, 8)
            with act.Fori(0, 2) as r:
                for q in range(2):
                    def cnt(c, k):
                        return r * (2 * c) + (q * c + k)

                    high_part(act, UQ + 2 * q + 1, r, 4)
                    act.wait_ge(s_mm, cnt(8, 0) + 1)
                    for c in range(2):
                        act.wait_ge(pr_mm, cnt(7, c + 1))
                        av(qnT[:, c, :], ps[c][:, :], ACT.Copy).then_inc(pr_ev, 1)
                    for c in range(2):
                        act.wait_ge(pr_mm, cnt(7, 4 + c + 1))
                        av(knT[:, c, :], ps[c][:, :], ACT.Copy).then_inc(pr_ev, 1)
                    act.wait_ge(o_mm, cnt(2, 0) + 1)
                    for h in range(2):
                        if h == 0:
                            act.wait_ge(pr_mm, cnt(7, 7))
                        else:
                            act.wait_ge(panel_mm, r * 4 + (UQ + 2 * q))
                        av(v_m[:, 2 * h:2 * h + 2, :], ps[2 + h][:, :].rearrange("p (t c) -> p t c", t=2), ACT.Copy).then_inc(pr_ev, 1)

                    def exps(u):
                        act.wait_ge(nmax, cnt(8, u + 1))
                        if u < 3:
                            act.wait_ge(t_mm, cnt(8, 0) + 1)
                        else:
                            act.wait_ge(t_mm, cnt(8, u - 2) + 1)
                        av(p_m[:, u % 3, :], ps[4 + u % 3][:, :], ACT.Exp, scale=SCALE2, bias=st2[:, 72 + u:73 + u],
                           accum_out=st2[:, 80 + u:81 + u]).then_inc(e_done, 1)

                    def evac(u):
                        b = (7, 0)[u % 2]
                        h, i = u // 4, u % 4
                        if i == 0:
                            act.wait_ge(o_mm, cnt(2, 0) + 1)
                        act.wait_ge(t_mm, cnt(8, u + 2))
                        av(pT_m[:, h, :, i * P:(i + 1) * P], ps[b][:, :].rearrange("p (k c) -> p k c", k=4), ACT.Copy).then_inc(t_ev, 1)

                    exps(0)
                    exps(1)
                    act.wait_ge(panel_mm, r * 4 + (UQ + 2 * q + 1))
                    for c in range(2):
                        av(sig_m[:, c, :], ps[c][:, :], ACT.Exp, scale=-1.0).then_inc(ga_sig, 1)
                    for u in range(2, 8):
                        exps(u)
                        evac(u - 2)
                    evac(6)
                    evac(7)
            def y_parts(j):
                av(y2S[0][:, 4 * j:4 * j + 4, :], y2T[:, 4 * j:4 * j + 4, :], ACT.Copy).then_inc(y_high, 1)

            act.wait_ge(s_mm, 33)
            y_parts(0)
            high_part(act, OO + 1)
            act.wait_ge(o_mm, 9)
            y_parts(1)
            for j in (2, 3):
                act.wait_ge(ym_ready, 4 * (j - 1) + 1)
                y_parts(j)
            act.wait_ge(dec_in, 16)
            av(lsg[:, 0, :], dec, ACT.Abs).then_inc(dec_abs, 1)
            act.wait_ge(dec_abs, 1)
            av(lsg[:, 1, :], lsg[:, 0, :], ACT.Exp, scale=-1.0).then_inc(dec_abs, 1)
            for j in range(2, 8):
                high_part(act, OO + j)
                if j < 2 + RH:
                    act.wait_ge(dec_arg, j - 1)
                    av(decay[:, j - 2, :], decay[:, j - 2, :], ACT.Exp).then_inc(dec_exp, 1)
                if j == 6:
                    square(x2_ready, 1, 0)

            norm(1, x2_ready, "r_norm", RQ)
            with act.Fori(0, 2) as r:
                for q in range(2):
                    def cnt(c, k):
                        return r * (2 * c) + (q * c + k)

                    n = RQ + 6 * q
                    high_part(act, n + 1, r, 12)
                    for x in range(4):
                        act.wait_ge(panel_mm, r * 12 + (n + x + 1))
                        high_part(act, n + x + 2, r, 12)
                    act.wait_ge(ro_mm, cnt(4, 0) + 1)
                    for t in range(TT):
                        av(v_r[:, t, :], ps[4 + t][:, :], ACT.Copy).then_inc(v_cp, 1)
                    for x in range(2):
                        act.wait_ge(panel_mm, r * 12 + (n + 5 + x))
                        if x == 0:
                            high_part(act, n + 6, r, 12)
                        act.wait_ge(rg_ready, cnt(4, 0) + 1)
                        for c in range(2):
                            av(sig_r[:, 2 * x + c, :], ps[(4, 2)[x] + c][:, :], ACT.Sigmoid).then_inc(rg_sig, 1)
            for j, (used, count) in enumerate(((rs_mm, 16), (ro_mm, 17), (ro_mm, 17), (rt_mm, 16))):
                act.wait_ge(used, count)
                act.wait_ge(yr_ready, 4 * (j + 1) + 1)
                y_parts(j)
                if j == 0:
                    high_part(act, TT_OUT + 1)
            for j in range(2, 8):
                high_part(act, TT_OUT + j)
                if j == 6:
                    square(x3_ready, 2, 0)
            square(x3_ready, 2, 1)

        @block.vector
        def _(dve):
            V = Steps(dve, v_step)
            for first in (e_used, bu_used, ss_done, scaled, y_ready, sm_done, o_ev, step_free, ym_ready, rg_ready, on_ready, yr_ready):
                dve.sem_inc(first, 1)
            v = nc.vector
            MUL, ADD, SUB = ALU.mult, ALU.add, ALU.subtract
            V(v.memset(half_m, -0.5))
            V(v.memset(st[:, 36:40], 0.0))
            v.memset(st[:, 40:41], 0.0).then_inc(e_used, 1)

            def chain(ins):
                V(ins)
                V.wait()

            s_ = lambda k: ssp[:, k, :]
            dve.wait_ge(par_in, 32)
            dve.wait_ge(ssm_exp, 1)
            v.tensor_tensor(s_(4), lr, s_(3), MUL).then_inc(ssm_dt, 1)
            chain(v.tensor_tensor(s_(6), li, s_(3), MUL))
            chain(v.tensor_scalar(s_(7), s_(6), TURN, ROUND, MUL, ADD))
            chain(v.tensor_scalar(s_(7), s_(7), ROUND, None, SUB))
            chain(v.scalar_tensor_tensor(s_(6), s_(7), -PI2_A, s_(6), MUL, ADD))
            chain(v.scalar_tensor_tensor(s_(6), s_(7), -PI2_B, s_(6), MUL, ADD))
            chain(v.scalar_tensor_tensor(s_(6), s_(7), -PI2_C, s_(6), MUL, ADD))
            chain(v.tensor_scalar(s_(8), s_(6), TURN * 4096, ROUND, MUL, ADD))
            chain(v.tensor_scalar(s_(8), s_(8), ROUND, 1.0 / 4096, SUB, MUL))
            chain(v.scalar_tensor_tensor(s_(9), s_(8), -PI2_A, s_(6), MUL, ADD))
            chain(v.scalar_tensor_tensor(s_(9), s_(8), -(PI2_B + PI2_C), s_(9), MUL, ADD))
            chain(v.tensor_scalar(s_(9), s_(9), TURN, None, MUL))
            dve.wait_ge(x_sq, TT)
            v.tensor_scalar(st[:, 28:32], st[:, 24:28], 1.0 / D, EPS, MUL, ADD).then_inc(x_ms, 1)
            tvb = tv.unsqueeze(1).to_broadcast([P, NTILE, 48])

            def wide(k):
                return s_(k).unsqueeze(2).to_broadcast([P, NTILE, 48])

            V(v.tensor_tensor(tw[0], tvb, wide(8), MUL))
            chain(v.tensor_tensor(tw[1], tvb, wide(9), MUL))
            chain(v.tensor_scalar(tw[2], tw[0], ROUND, ROUND, ADD, SUB))
            chain(v.tensor_tensor(tw[0], tw[0], tw[2], SUB))
            chain(v.tensor_tensor(tw[0], tw[0], tw[1], ADD))
            chain(v.tensor_scalar(tw[2], tw[0], ROUND, ROUND, ADD, SUB))
            v.tensor_tensor(tw[0], tw[0], tw[2], SUB).then_inc(ang_in, 1)
            dve.wait_ge(const_in, 64)
            chain(v.tensor_copy(st[:, 16:20], st[:, 20:24].bitcast(mybir.dt.int32)))
            for t in range(TT):
                V(v.tensor_scalar(angA[:, 1, t, :], angA[:, 0, t, :], st[:, 16 + t:17 + t], None, MUL))
            V.wait()
            chain(v.tensor_scalar(angA[:, 2], angA[:, 1], TURN, ROUND, MUL, ADD))
            chain(v.tensor_scalar(angA[:, 2], angA[:, 2], ROUND, None, SUB))
            for part in (PI2_A, PI2_B, PI2_C):
                chain(v.scalar_tensor_tensor(angA[:, 1], angA[:, 2], -part, angA[:, 1], MUL, ADD))
            chain(v.tensor_scalar(angA[:, 3], angA[:, 1], TURN, 0.5, MUL, ALU.min))
            v.tensor_scalar(angA[:, 3], angA[:, 3], -0.5, None, ALU.max).then_inc(ang_in, 1)
            dve.wait_ge(trig_ready, 1)
            ptab = pack[:, :, 512:896].rearrange("p m (j c) -> p m j c", j=4)
            tw4 = [x.rearrange("p (m j) c -> p m j c", j=4) for x in tw]
            V(v.tensor_copy(ptab[:, :, :, 48:96], tw4[1]))
            chain(v.tensor_tensor(tw[3], tw[2], tw[2], MUL))
            chain(v.tensor_scalar(ptab[:, :, :, 0:48], tw4[3], -2.0, 1.0, MUL, ADD))
            dve.wait_ge(ssm_exp, 2)
            V(v.tensor_copy(pack[:, :, 896:900], s_(5).rearrange("p (m j) -> p m j", j=4)))
            pt32 = pack[:, :, 512:896].rearrange("p m (j c) -> p m j c", j=4)
            s4 = lambda k: s_(k).rearrange("p (m j) -> p m j", j=4)
            V(v.tensor_tensor(s4(10), s4(5), pt32[:, :, :, 33], MUL))
            V(v.tensor_tensor(s4(11), s4(5), pt32[:, :, :, 48 + 33], MUL))
            V(v.tensor_tensor(s_(12), lr, lr, MUL))
            chain(v.tensor_tensor(s_(13), li, li, MUL))
            chain(v.tensor_tensor(s_(12), s_(12), s_(13), ADD))
            V(v.reciprocal(s_(12), s_(12)))
            chain(v.tensor_scalar(s_(10), s_(10), -1.0, None, ADD))
            V(v.tensor_tensor(s_(13), s_(10), lr, MUL))
            V(v.tensor_tensor(s_(14), s_(11), li, MUL))
            V(v.tensor_tensor(s_(15), s_(11), lr, MUL))
            chain(v.tensor_tensor(s_(16), s_(10), li, MUL))
            V(v.tensor_tensor(s_(13), s_(13), s_(14), ADD))
            chain(v.tensor_tensor(s_(15), s_(15), s_(16), SUB))
            V(v.tensor_tensor(s_(13), s_(13), s_(12), MUL))
            chain(v.tensor_tensor(s_(15), s_(15), s_(12), MUL))
            fb = lambda k: s_(k).unsqueeze(2).to_broadcast([P, NTILE, 32])
            dve.wait_ge(ssm_in, 32)
            V(v.tensor_tensor(bbs[:, 0], b_nat[:, 0], fb(13), MUL))
            chain(v.tensor_tensor(bt_tmp, b_nat[:, 1], fb(15), MUL))
            v.tensor_tensor(bbs[:, 0], bbs[:, 0], bt_tmp, SUB).then_inc(bb_ready, 1)
            dve.wait_ge(bb_ready, 1)
            V(v.tensor_tensor(bbs[:, 1], b_nat[:, 1], fb(13), MUL))
            chain(v.tensor_tensor(bt_tmp, b_nat[:, 0], fb(15), MUL))
            v.tensor_tensor(bbs[:, 1], bbs[:, 1], bt_tmp, ADD).then_inc(bb_ready, 1)
            dve.wait_ge(trig_ready, 2)
            V(v.tensor_copy(csA[:, 1], angA[:, 1]))
            chain(v.tensor_tensor(angA[:, 3], angA[:, 2], angA[:, 2], MUL))
            chain(v.tensor_scalar(csA[:, 0], angA[:, 3], -2.0, 1.0, MUL, ADD))
            v.memset(st[:, 41:42], 0.0).then_inc(bb_ready, 1)

            def tile_step(i, j):
                n = i * 4 + (j + 1)
                dve.wait_ge(bu_mm, n)
                dve.wait_ge(e_ready, n)
                c, s = E[:, j % 2, 0], E[:, j % 2, 1]
                bre, bim = ps[5][:, :], ps[6][:, :]
                V(v.tensor_tensor(t_a[0], bre, c, MUL))
                k2 = V(v.tensor_tensor(t_a[1], bim, s, MUL))
                V(v.tensor_tensor(gs[:, 0], bim, c, MUL))
                v.tensor_tensor(gs[:, 1], bre, s, MUL).then_inc(bu_used, 1)
                V.wait(k2)
                k3 = V(v.tensor_tensor(bp[:, 0], t_a[0], t_a[1], ADD))
                dve.wait_ge(bu_used, n + 1)
                k4 = V(v.tensor_tensor(bp[:, 1], gs[:, 0], gs[:, 1], SUB))
                mag = pack[:, bass.ds(i, 1), 896 + j:897 + j].rearrange("p o n -> p (o n)").to_broadcast([P, 512])
                V.wait(k4)
                k5 = V(v.tensor_tensor_scan(gs[:, 0], mag, bp[:, 0], 0.0, MUL, ADD))
                k6 = V(v.tensor_tensor_scan(gs[:, 1], mag, bp[:, 1], 0.0, MUL, ADD))
                V.wait(k5)
                V(v.tensor_tensor(t_a[0], gs[:, 0], c, MUL))
                V.wait(k6)
                V(v.tensor_tensor(t_a[1], gs[:, 1], s, MUL))
                V(v.tensor_tensor(bp[:, 0], gs[:, 1], c, MUL))
                v.tensor_tensor(bp[:, 1], gs[:, 0], s, MUL).then_inc(e_used, 1)
                if j == 0:
                    dve.wait_ge(c_mm, i * 4 + 1)
                else:
                    dve.wait_ge(c_mm, i * 4 + (j - 1) + 1)
                dve.wait_ge(e_used, n + 1 + 1)
                V(v.tensor_tensor(hs[:, j % 2, 0], t_a[0], t_a[1], SUB))
                v.scalar_tensor_tensor(hs[:, j % 2, 1], bp[:, 0], -1.0, bp[:, 1], MUL, SUB).then_inc(h_ready, 1)
                dve.wait_ge(h_ready, n)

            def heads_ms(i, x):
                dve.wait_ge((q_ev, k_ev)[x], i * 2 + 2 + 1)
                so = 48 + 36 * x
                v.tensor_reduce(st[:, so:so + 12], sq, AX.X, ADD).then_inc(ss_done, 1)
                dve.wait_ge(ss_done, i * 2 + (x + 2))
                dve.wait_ge(rs_ready, i * 2 + x + 1)
                v.tensor_scalar(st[:, so + 12:so + 24], st[:, so:so + 12], 1.0 / HD, EPS, MUL, ADD).then_inc(ms_ready, 1)

            def heads_scale(i, x):
                so = 48 + 36 * x
                q = qkv_tok[x][:, :, bass.ds(i * PC, PC)]
                dve.wait_ge(rs_ready, i * 2 + (x + 2))
                rs = st[:, so + 24:so + 36].rearrange("p (t h) -> p t h", t=TT).unsqueeze(3).to_broadcast([P, TT, PH, HD])
                q4 = q.rearrange("p t (h d) -> p t h d", h=PH)
                kk = V(v.tensor_tensor(q4, q4, rs, MUL))
                dve.wait_ge(qkw_full, i * 16 + 16)
                V.wait(kk)
                v.tensor_tensor(q, q, qk_w[:, x, :].unsqueeze(1).to_broadcast([P, TT, PC]), MUL).then_inc(scaled, 1)

            with dve.Fori(0, KT) as i:
                V.loop(i, CHANNEL_STEPS)
                tile_step(i, 0)
                tile_step(i, 1)
                heads_ms(i, 0)
                tile_step(i, 2)
                heads_scale(i, 0)
                tile_step(i, 3)
                heads_ms(i, 1)
                dve.wait_ge(c_mm, i * 4 + 4 + 1)
                dve.wait_ge(gelu_done, i + 1)
                v.scalar_tensor_tensor(y_sb, u_cur, cols[:, bass.ds(i + COLS["d_skip"], 1)], ps[7][:, :], MUL, ADD).then_inc(y_ready, 1)
                heads_scale(i, 1)
            V.end(KT)

            dve.wait_ge(mask_in, 16)
            with dve.Fori(0, 4) as p:
                V.loop(p, ATT_STEPS)

                def soft(u):
                    i = u % 4
                    dve.wait_ge(sc_mm, p * 8 + (u + 2))
                    dve.wait_ge(p_ready, p * 8 + max(u - 1, 0) + 1)
                    w0, w1 = min(i + 1, 2) * P, (i + 1) * P
                    b = u % 2
                    mask_at = [masks[:, 256 - w0:256], masks[:, 256 + 512 - w1:768], masks[:, 768 + 512 - w1:1280]]
                    x0 = 0
                    for g, w in enumerate((w0, w1, w1)):
                        ins = v.scalar_tensor_tensor(sm[:, b, x0:x0 + w], ps[g][:, 0:w], SCALE1, mask_at[g], MUL, ADD)
                        x0 += w
                        if g < 2:
                            V(ins)
                    ins.then_inc(sm_done, 1)
                    dve.wait_ge(sm_done, p * 8 + (u + 2))
                    k = V(v.tensor_reduce(mx[:, b:b + 1], sm[:, b, 0:x0], AX.X, ALU.max))
                    V.wait(k)
                    v.tensor_scalar(nmx[:, b:b + 1], mx[:, b:b + 1], -1.0, None, MUL).then_inc(nm_ready, 1)

                def o_out(u):
                    b = u % 2
                    dve.wait_ge(p_ready, p * 8 + (u + 2))
                    k = V(v.reciprocal(rden[:, u:u + 1], den[:, u:u + 1]))
                    dve.wait_ge(pv_mm, p * 8 + (u + 2))
                    V.wait(k)
                    v.tensor_scalar(o_tok[:, u % 4, bass.ds(p * 128 + (u // 4) * HD, HD)], ps[6 + b][:, (u // 4) * HD:(u // 4 + 1) * HD],
                                    rden[:, u:u + 1], None, MUL).then_inc(o_ev, 1)

                soft(0)
                soft(1)
                for u in range(8):
                    if u < 6:
                        soft(u + 2)
                    if u >= 1:
                        o_out(u - 1)
                o_out(7)
            V.end(4)

            def angles2():
                dve.wait_ge(misc_in, 16)
                dve.wait_ge(pos_in, 16)
                pi = turns[:, 0:T].bitcast(mybir.dt.int32)
                for k in range(2):
                    V(v.tensor_scalar(ang[:, k * T:(k + 1) * T], pi, inv_cols[:, k:k + 1], None, MUL))
                V.wait()
                chain(v.tensor_scalar(turns, ang, TURN, ROUND, MUL, ADD))
                chain(v.tensor_scalar(turns, turns, ROUND, None, SUB))
                for part in (PI2_A, PI2_B, PI2_C):
                    chain(v.scalar_tensor_tensor(ang, turns, -part, ang, MUL, ADD))
                chain(v.tensor_scalar(ang, ang, TURN, 0.5, MUL, ALU.min))
                v.tensor_scalar(ang, ang, -0.5, None, ALU.max).then_inc(ang2, 1)

            def tables2():
                dve.wait_ge(trig2, 1)
                chain(v.tensor_tensor(cosT, cosT, cosT, MUL))
                chain(v.tensor_scalar(cosT, cosT, -2.0, 1.0, MUL, ADD))
                chain(v.tensor_scalar(sinM, sinM, inv_cols[:, 2:3], None, MUL))

            def in_parts(dst, k, src):
                chain(v.tensor_copy(dst[0][:, k, :], src))
                return v.tensor_tensor(dst[1][:, k, :], src, dst[0][:, k, :], SUB)

            for h in range(2):
                dve.wait_ge(g_high, h + 1)
                v.tensor_tensor(gS[1][:, 4 * h:4 * h + 4, :], gT[:, 4 * h:4 * h + 4, :], gS[0][:, 4 * h:4 * h + 4, :], SUB
                                ).then_inc(g_low, 1)
            low_part(dve, 1)
            for s in range(13):
                b = 4 * (s % 2)
                sg = sig[:, s % 2]
                if s == 0:
                    v.memset(st[:, 42:43], 0.0).then_inc(step_free, 1)
                low_part(dve, 2 * s + 2)
                if s < 4:
                    for c in range(2):
                        dve.wait_ge(glu_sig, 4 * s + 1 + c)
                        V(v.tensor_tensor(prod[:, 2 + c, :], ps[b + c][:, :], sg[:, c, :], MUL))
                    for c in range(2):
                        dve.wait_ge(glu_sig, 4 * s + 3 + c)
                        chain(v.tensor_tensor(prod[:, c, :], gT[:, 2 * s + c, :], sg[:, 2 + c, :], MUL))
                        chain(v.tensor_tensor(prod[:, c, :], prod[:, c, :], prod[:, 2 + c, :], MUL))
                        in_parts(yS, 2 * s + c, prod[:, c, :]).then_inc(ys_ready, 1)
                    low_part(dve, 2 * s + 3)
                    dve.wait_ge(ys_ready, 2 * s + 2)
                elif s < 8:
                    low_part(dve, 2 * s + 3)
                    for c in range(2):
                        dve.wait_ge(rs_sig, 2 * (s - 4) + c + 1)
                        dve.wait_ge(panel_mm, 2 * s + 2)
                        v.tensor_tensor(mT[:, 2 * (s - 4) + c, :], ps[b + 2 + c][:, :], sg[:, c, :], MUL).then_inc(m_ready, 1)
                elif s == 8:
                    for c in range(4):
                        dve.wait_ge(glu_sig, 16 + c + 1)
                        chain(v.tensor_tensor(prod[:, c, :], ps[b + c][:, :], sg[:, c, :], MUL))
                        dve.wait_ge(ot_mm, c + 1)
                        chain(v.tensor_tensor(prod[:, c, :], ps[4 + c][:, :], prod[:, c, :], MUL))
                        in_parts(oS, c, prod[:, c, :]).then_inc(ya_ready, 1)
                    low_part(dve, 2 * s + 3)
                    dve.wait_ge(ya_ready, 4)
                else:
                    if s == 10:
                        angles2()
                    if s == 11:
                        tables2()
                    low_part(dve, 2 * s + 3)
                    for c in range(2):
                        dve.wait_ge(rs_sig, 8 + 2 * (s - 9) + c + 1)
                        dve.wait_ge(panel_mm, 2 * s + 2)
                        k = 2 * (s - 9) + c
                        chain(v.tensor_tensor(prod[:, c, :], ps[b + 2 + c][:, :], sg[:, c, :], MUL))
                        chain(v.tensor_tensor(prod[:, c, :], mT[:, k, :], prod[:, c, :], ADD))
                        in_parts(mS, k, prod[:, c, :]).then_inc(m_ready, 1)
                    dve.wait_ge(m_ready, 8 + 2 * (s - 9) + 2)
                v.memset(st[:, 43:44], 0.0).then_inc(step_free, 1)
                dve.wait_ge(step_free, s + 2 + 1)
            for s in (13, 14):
                for n in ((28, 29), (30,))[s - 13]:
                    low_part(dve, n)
                dve.wait_ge(xr_in, 16)
                dve.wait_ge(panel_mm, 2 * s + 2)
                for t in range(TT):
                    xs = x_res[:, t, (s - 13) * 512:(s - 12) * 512]
                    v.tensor_tensor(xs, ps[4 * (s % 2) + t][:, :], xs, ADD).then_inc(x1_ready, 1)
                v.memset(st[:, 43:44], 0.0).then_inc(step_free, 1)
                dve.wait_ge(step_free, s + 2 + 1)


            def mean_square(n):
                dve.wait_ge(n_sq, 2 * TT * (n + 1))
                chain(v.tensor_tensor(st2[:, 24:28], st2[:, 8:12], st2[:, 20:24], ADD))
                v.tensor_scalar(st2[:, 12:16], st2[:, 24:28], 1.0 / D, EPS, MUL, ADD).then_inc(n_ms, 1)

            def norm_rest(n):
                dve.wait_ge(n_rs, n + 1)
                for t in (2, 3):
                    v.tensor_scalar(xn2[:, t, :], x_res[:, t, :], st2[:, 16 + t:17 + t], None, MUL).then_inc(n_nrm_v, 1)

            def low_norm(n0, cname):
                for k in range(KT):
                    dve.wait_ge(nt_ev, n0 + k + 1)
                    v.scalar_tensor_tensor(hS[1][:, k, :], ps[k][:, :], col(cname, k), hS[0][:, k, :], MUL, SUB
                                           ).then_inc(nt_low, 1)

            mean_square(0)
            norm_rest(0)
            low_part(dve, 31)
            low_norm(0, "a_norm")
            dve.wait_ge(nt_mm, KT)
            V(v.memset(upad[:, :, :, 0:PAD], 0.0))
            v.memset(upad[:, :, :, PAD + T:2 * PAD + T], 0.0).then_inc(pads, 1)
            dve.wait_ge(pads, 1)
            n = first_of["lo"]
            low_part(dve, n + 2)
            low_part(dve, n + 3)
            dve.wait_ge(panel_mm, n + 3)
            for c in range(2):
                v.tensor_tensor(y2T[:, c, :], ps[c][:, :], (cosM, sinM)[c], MUL).then_inc(kr_used, 1)
            dve.wait_ge(kr_used, 2)
            v.tensor_tensor(krT, y2T[:, 0, :], y2T[:, 1, :], ADD).then_inc(kr_rot, 1)
            dve.wait_ge(kr_rot, 1)
            low_part(dve, PU + 1)
            dve.wait_ge(lo_sq, 12)
            chain(v.tensor_tensor(st2[:, 40:44], st2[:, 32:36], st2[:, 36:40], ADD))
            chain(v.tensor_scalar(st2[:, 48:52], st2[:, 40:44], 1.0 / QL, EPS, MUL, ADD))
            v.tensor_scalar(st2[:, 52:56], st2[:, 44:48], 1.0 / KVL, EPS, MUL, ADD).then_inc(lo_ms, 1)
            dve.wait_ge(lo_ev, 12)
            v.memset(st2[:, 0:1], 0.0).then_inc(step_free, 1)
            dve.wait_ge(step_free, 18)

            def pool_gate(i):
                b = 4 * (i % 2)
                for c in range(2):
                    dve.wait_ge(gb_sig, 2 * i + c + 1)
                    k = V(v.tensor_tensor(prod2[:, c, :], ps[b + 2 + c][:, :], sig2[:, i % 2, c, :], MUL))
                    dve.wait_ge(pool_mm, i + 1)
                    V.wait(k)
                    v.scalar_tensor_tensor(y2T[:, 2 * i + c, :], ps[b + c][:, :], col("pool_scale", 2 * i + c),
                                           prod2[:, c, :], MUL, MUL).then_inc(y2_ready, 1)
                dve.wait_ge(y2_ready, 2 * i + 2)
                v.memset(st2[:, 0:1], 0.0).then_inc(step_free, 1)
                dve.wait_ge(step_free, 18 + i + 1)

            for i, wd in enumerate(POOLS):
                low_part(dve, PU + 2 * i + 2)
                if i >= 1:
                    pool_gate(i - 1)
                dve.wait_ge(u_pad, 2 * i + 2)
                src, n = upad[:, i % 2], T + 2 * PAD
                for k in range(i + 1):
                    n -= 1 << k
                    dst = win[:, k % 2]
                    chain(v.tensor_tensor(dst[:, :, 0:n], src[:, :, 0:n], src[:, :, (1 << k):(1 << k) + n], ADD))
                    src = dst
                x0 = PAD - wd // 2
                sums = src[:, :, x0:x0 + T]
                for e in range(2):
                    edge = sums[:, :, e * (T - 8):e * (T - 8) + 8]
                    V(v.tensor_tensor(edge, edge, corr[:, i, 8 * e:8 * e + 8].unsqueeze(1).to_broadcast([P, 2, 8]), MUL))
                V.wait()
                if i >= 2:
                    dve.wait_ge(pool_mm, i - 1)
                v.scalar_tensor_tensor(pool_d[:, i % 2], sums, 1.0 / wd, upad[:, i % 2, :, PAD:PAD + T], MUL, SUB
                                       ).then_inc(d_ready, 1)
                dve.wait_ge(d_ready, i + 1)
                if i < 3:
                    low_part(dve, PU + 2 * i + 3)
            pool_gate(3)

            with dve.Fori(0, 2) as r:
                V.loop(r, MLA_STEPS)
                for q in range(2):
                    def cnt(c, k):
                        return r * (2 * c) + (q * c + k)

                    low_part(dve, UQ + 2 * q + 1, r, 4)
                    for c in range(2):
                        dve.wait_ge(pr_mm, cnt(7, 3 + c))
                        V(v.tensor_tensor(rot[:, c, :], ps[2 + c][:, :], (cosM, sinM)[c], MUL))
                    V.wait()
                    dve.wait_ge(s_mm, cnt(8, 0) + 1)
                    v.tensor_tensor(qrT, rot[:, 0, :], rot[:, 1, :], ADD).then_inc(rot_done, 1)
                    dve.wait_ge(rot_done, cnt(1, 1))

                    def row_max(u):
                        dve.wait_ge(s_mm, cnt(8, u + 2))
                        k = V(v.tensor_reduce(st2[:, 88 + u:89 + u], ps[4 + u % 3][:, :], AX.X, ALU.max))
                        V.wait(k)
                        if u == 0:
                            dve.wait_ge(e_done, cnt(8, 0) + 1)
                        v.tensor_scalar(st2[:, 72 + u:73 + u], st2[:, 88 + u:89 + u], -SCALE2, None, MUL).then_inc(nmax, 1)

                    def recip(u):
                        dve.wait_ge(e_done, cnt(8, u + 2))
                        if u == 0:
                            dve.wait_ge(p_norm, cnt(8, 0) + 1)
                        v.reciprocal(st2[:, 96 + u:97 + u], st2[:, 80 + u:81 + u]).then_inc(rcp, 1)

                    def gate():
                        for c in range(2):
                            dve.wait_ge(ga_sig, cnt(2, c + 1))
                            v.tensor_copy(gate_m[:, c, :], ps[c][:, :]).then_inc(ga_ready, 1)
                        V(v.tensor_scalar(sig_m, sig_m, 1.0, None, ADD))

                    def gate_half(c):
                        chain(v.reciprocal(sig_m[:, c, :], sig_m[:, c, :]))
                        dve.wait_ge(ga_ready, cnt(2, c + 1))
                        v.tensor_tensor(gate_m[:, c, :], gate_m[:, c, :], sig_m[:, c, :], MUL).then_inc(ga_done, 1)

                    def gated(h):
                        dve.wait_ge(ga_done, cnt(2, h + 1))
                        dve.wait_ge(o_mm, cnt(2, h + 2))
                        v.tensor_tensor(y2T[:, bass.ds(r * 4 + (8 + 2 * q + h), 1), :].rearrange("p o n -> p (o n)"),
                                        ps[2 + h][:, :], gate_m[:, h, :], MUL).then_inc(ym_ready, 1)

                    row_max(0)
                    row_max(1)
                    recip(0)
                    recip(1)
                    gate()
                    V.wait()
                    for u in range(2, 8):
                        row_max(u)
                        recip(u)
                        if u in GATE_AT:
                            gate_half(GATE_AT.index(u))
                        if u == 7:
                            gated(0)
                    gated(1)
                    dve.wait_ge(ym_ready, cnt(2, 2) + 1)
            V.end(2)

            def y_rest(j, y0):
                dve.wait_ge(y_high, y0 + j + 1)
                v.tensor_tensor(y2S[1][:, 4 * j:4 * j + 4, :], y2T[:, 4 * j:4 * j + 4, :], y2S[0][:, 4 * j:4 * j + 4, :], SUB
                                ).then_inc(y_low, 1)

            y_rest(0, 0)
            low_part(dve, OO + 1)
            for j in (1, 2, 3):
                y_rest(j, 0)
            dve.wait_ge(dec_abs, 2)
            dve.wait_ge(delta_in, 16)
            L = lambda k: lsg[:, k, :]
            chain(v.tensor_scalar(L(2), L(1), 2.0, None, ADD))
            chain(v.reciprocal(L(2), L(2)))
            chain(v.tensor_tensor(L(2), L(2), L(1), MUL))
            chain(v.tensor_tensor(L(3), L(2), L(2), MUL))
            chain(v.tensor_scalar(L(4), L(3), 1.0 / 15, None, MUL))
            for d in (13, 11, 9, 7, 5, 3):
                chain(v.scalar_tensor_tensor(L(4), L(4), 1.0 / d, L(3), ADD, MUL))
            chain(v.scalar_tensor_tensor(L(4), L(4), 1.0, L(2), ADD, MUL))
            chain(v.tensor_scalar(L(5), dec, 0.0, None, ALU.min))
            chain(v.scalar_tensor_tensor(L(5), L(4), -2.0, L(5), MUL, ADD))
            chain(v.tensor_scalar(L(4), L(5), -1.0, None, MUL))
            dve.wait_ge(t_ev, 33)
            dve.wait_ge(o_mm, 9)
            def w_out(n, s, y_done, beside=lambda j: None):
                for j in range(8):
                    if j < 6:
                        low_part(dve, n + j + 2)
                        beside(j)
                    if j % 4 == 3:
                        c, b = j // 4, 4 * ((s + j // 4) % 2)
                        dve.wait_ge(panel_mm, n + j + 1)
                        for t in range(TT):
                            xs = x_res[:, t, c * 512:(c + 1) * 512]
                            v.tensor_tensor(xs, ps[b + t][:, :], xs, ADD).then_inc(y_done, 1)
                        v.memset(st2[:, 0:1], 0.0).then_inc(step_free, 1)
                        dve.wait_ge(step_free, s + c + 2 + 1)

            def decay_table(h):
                if h < RH:
                    V(v.tensor_scalar(dt1, delta, 0.0, L(5)[:, h:h + 1], ALU.max, MUL))
                    chain(v.tensor_scalar(dt2, delta, 0.0, L(4)[:, 4 + h:5 + h], ALU.min, MUL))
                    v.tensor_tensor(decay[:, h, :], dt1, dt2, ADD).then_inc(dec_arg, 1)
                    dve.wait_ge(dec_arg, h + 1)

            w_out(OO, 20, x2_ready, decay_table)
            mean_square(1)
            norm_rest(1)
            low_part(dve, RQ)
            low_norm(KT, "r_norm")
            dve.wait_ge(dec_exp, RH)
            with dve.Fori(0, 2) as r:
                V.loop(r, RET_STEPS)
                for q in range(2):
                    def cnt(c, k):
                        return r * (2 * c) + (q * c + k)

                    low_part(dve, RQ + 6 * q + 1, r, 12)
                    for x, dst in enumerate((q_r, k_r)):
                        low_part(dve, RQ + 6 * q + 2 + x, r, 12)
                        dve.wait_ge(panel_mm, r * 12 + (RQ + 6 * q + 1 + x))
                        x1, x2 = ps[2 * x][:, :], ps[2 * x + 1][:, :]
                        V(v.tensor_tensor(rot_r[:, 0, :], x1, cosR, MUL))
                        V(v.tensor_tensor(rot_r[:, 1, :], x2, sinR, MUL))
                        V(v.tensor_tensor(rot_r[:, 2, :], x2, cosR, MUL))
                        V(v.tensor_tensor(rot_r[:, 3, :], x1, sinR, MUL))
                        V.wait()
                        V(v.tensor_tensor(dst[:, 0, :], rot_r[:, 0, :], rot_r[:, 1, :], SUB))
                        v.tensor_tensor(dst[:, 1, :], rot_r[:, 2, :], rot_r[:, 3, :], ADD).then_inc(rqk_rot, 1)
                        dve.wait_ge(rqk_rot, cnt(2, x + 1))
                    low_part(dve, RQ + 6 * q + 4, r, 12)
                    low_part(dve, RQ + 6 * q + 5, r, 12)
                    for j in range(TT):
                        dve.wait_ge(rs_mm, cnt(4, j + 1))
                        x0 = 3 * P - j * P
                        dj = decay[:, bass.ds(r * 2 + q, 1), x0:x0 + T].rearrange("p o n -> p (o n)")
                        v.scalar_tensor_tensor(sd[:, j, :], ps[j][:, :], RK ** -0.5, dj, MUL, MUL).then_inc(sd_ready, 1)

                    def gates(x):
                        if x == 0:
                            low_part(dve, RQ + 6 * q + 6, r, 12)
                        for c in range(2):
                            k = 2 * x + c
                            dve.wait_ge(rg_sig, cnt(4, k + 1))
                            gcol = cols[:, bass.ds(r * 8 + (COLS["gn"] + 4 * q + k), 1)]
                            v.scalar_tensor_tensor(gate_r[:, k, :], ps[(4, 2)[x] + c][:, :], gcol, sig_r[:, k, :], MUL, MUL
                                                   ).then_inc(rg_ready, 1)

                    gates(0)
                    for i in range(TT):
                        dve.wait_ge(ro_mm, cnt(4, i + 2))
                        k = V(v.bn_stats(st2[:, 104 + 6 * i:110 + 6 * i], ps[(6, 7, 0, 1)[i]][:, :]))
                    V.wait(k)
                    apart(dve)
                    for i in range(TT):
                        k = V(v.bn_aggr(st2[:, 128 + 2 * i:130 + 2 * i], st2[:, 104 + 6 * i:110 + 6 * i]))
                    V.wait(k)
                    mv = st2[:, 128:136].rearrange("p (i x) -> p i x", x=2)
                    v.tensor_scalar(st2[:, 136:140], mv[:, :, 1], EPS, None, ADD).then_inc(var_ready, 1)
                    dve.wait_ge(rstd, cnt(1, 1))
                    for i in range(TT):
                        v.tensor_scalar(on[:, i, :], ps[(6, 7, 0, 1)[i]][:, :], mv[:, i, 0:1], st2[:, 140 + i:141 + i], SUB, MUL
                                        ).then_inc(on_ready, 1)
                    gates(1)
                    dve.wait_ge(rg_ready, cnt(4, 4) + 1)
                    for i in range(TT):
                        dve.wait_ge(rt_mm, cnt(4, i + 1))
                        v.tensor_tensor(y2T[:, bass.ds(r * 8 + 4 * q, 4), i * P:(i + 1) * P],
                                        ps[4 + i][:, :].rearrange("p (k c) -> p k c", k=4),
                                        gate_r[:, :, i * P:(i + 1) * P], MUL).then_inc(yr_ready, 1)
                    dve.wait_ge(yr_ready, cnt(4, 4) + 1)
            V.end(2)
            for j in range(4):
                y_rest(j, 4)
                if j == 0:
                    low_part(dve, TT_OUT + 1)
            w_out(TT_OUT, 22, x3_ready)
            mean_square(2)
            dve.wait_ge(gain_in, 16)
            dve.wait_ge(n_rs, 3)
            for t in range(TT):
                v.scalar_tensor_tensor(x_res[:, t, :], x_res[:, t, :], st2[:, 16 + t:17 + t], gain, MUL, MUL).then_inc(f_out, 1)

        @block.gpsimd
        def _(pool):
            G = Steps(pool, g_step)
            for first in (rs_ready, p_norm):
                pool.sem_inc(first, 1)
            g = nc.gpsimd
            MUL, ADD, SUB = ALU.mult, ALU.add, ALU.subtract
            pool.wait_ge(v_step, 2)
            pool.wait_ge(x_ms, 1)
            g.tensor_tensor(st[:, 32:36], st[:, 28:32], half_m[:, 0:4], ALU.pow).then_inc(x_rs, 1)
            pool.wait_ge(bb_ready, 3)

            def phases(i, j):
                n = i * 4 + (j + 1)
                tab = pack[:, bass.ds(i, 1), 512 + 96 * j:608 + 96 * j].rearrange("p o n -> p (o n)")
                hi = lambda x: tab[:, 48 * x:48 * x + 32].unsqueeze(2).to_broadcast([P, 32, 16])
                lo = lambda x: tab[:, 48 * x + 32:48 * x + 48].unsqueeze(1).to_broadcast([P, 32, 16])
                r = lambda x: x.rearrange("p (a b) -> p a b", a=32)
                c, s = E[:, j % 2, 0], E[:, j % 2, 1]
                pool.wait_ge(e_used, i * 4 + j + 1)
                apart(pool)
                G(g.tensor_tensor(r(e_t[0]), hi(0), lo(0), MUL))
                k = G(g.tensor_tensor(r(e_t[1]), hi(1), lo(1), MUL))
                G.wait(k)
                k = G(g.tensor_tensor(c, e_t[0], e_t[1], SUB))
                G.wait(k)
                apart(pool)
                G(g.tensor_tensor(r(e_t[0]), hi(1), lo(0), MUL))
                k = G(g.tensor_tensor(r(e_t[1]), hi(0), lo(1), MUL))
                G.wait(k)
                g.tensor_tensor(s, e_t[0], e_t[1], ADD).then_inc(e_ready, 1)
                pool.wait_ge(e_ready, n)

            def power(i, x):
                so = 48 + 36 * x
                pool.wait_ge(ms_ready, i * 2 + (x + 1))
                g.tensor_tensor(st[:, so + 24:so + 36], st[:, so + 12:so + 24], half_m[:, 0:12], ALU.pow
                                ).then_inc(rs_ready, 1)

            def rope(i, x):
                pool.wait_ge(scaled, i * 2 + (x + 2))
                apart(pool)
                q = qkv_tok[x][:, :, bass.ds(i * PC, PC)].rearrange("p t (h d) -> p t h d", h=PH)
                x1, x2 = q[:, :, :, 0:ROPE1], q[:, :, :, ROPE1:2 * ROPE1]
                cb = csA[:, 0].unsqueeze(2).to_broadcast([P, TT, PH, ROPE1])
                sb = csA[:, 1].unsqueeze(2).to_broadcast([P, TT, PH, ROPE1])
                G(g.tensor_tensor(rt[0], x1, cb, MUL))
                G(g.tensor_tensor(rt[1], x2, sb, MUL))
                G(g.tensor_tensor(rt[2], x2, cb, MUL))
                k = G(g.tensor_tensor(rt[3], x1, sb, MUL))
                G.wait(k)
                apart(pool)
                G(g.tensor_tensor(x1, rt[0], rt[1], SUB))
                g.tensor_tensor(x2, rt[2], rt[3], ADD).then_inc(roped, 1)
                pool.wait_ge(roped, i * 2 + (x + 1))

            def turn(i, more):
                phases(i, 2)
                power(i, 0)
                phases(i, 3)
                rope(i, 0)
                if more:
                    phases(i + 1, 0)
                power(i, 1)
                if more:
                    phases(i + 1, 1)
                rope(i, 1)

            phases(0, 0)
            phases(0, 1)
            with pool.Fori(0, KT - 1) as i:
                G.loop(i, PHASE_STEPS)
                turn(i, True)
            G.end(KT - 1)
            turn(KT - 1, False)
            with pool.Fori(1, 4) as p:
                pool.wait_ge(tr_mm, p * 6 + 1)
                apart(pool)
                for x in range(6):
                    src = qkv_tok[x // 3][:, :, bass.ds(p * 128 + (x % 3) * 512, P)]
                    ins = g.tensor_copy(qg[:, x], src)
                ins.then_inc(qg_ready, 1)
            pool.wait_ge(qg_ready, 4)
            pool.wait_ge(v_mm, 2 * KT + 1)
            g.tensor_copy(hS[0], hT).then_inc(h_split, 1)
            pool.wait_ge(h_split, 1)
            g.tensor_tensor(hS[1], hT, hS[0], SUB).then_inc(h_split, 1)
            pool.wait_ge(scaled, 2 * KT + 1)
            pool.wait_ge(w_full[0], 16)
            g.tensor_copy(split_w[:, 0, 0, :], raw[:, 0, :]).then_inc(w_first, 1)
            pool.wait_ge(w_first, 1)
            g.tensor_tensor(split_w[:, 0, 1, :], raw[:, 0, :], split_w[:, 0, 0, :], SUB).then_inc(w_first, 1)

            def power2(k):
                pool.wait_ge(n_ms, k + 1)
                g.tensor_tensor(st2[:, 16:20], st2[:, 12:16], half_m[:, 0:4], ALU.pow).then_inc(n_rs, 1)

            power2(0)
            pool.wait_ge(lo_ms, 1)
            g.tensor_tensor(st2[:, 56:64], st2[:, 48:56], half_m[:, 0:8], ALU.pow).then_inc(lo_rs, 1)
            with pool.Fori(0, 4) as p:
                for u in range(8):
                    pool.wait_ge(rcp, p * 8 + (u + 1))
                    apart(pool)
                    g.tensor_scalar(p_m[:, u % 3, :], p_m[:, u % 3, :], st2[:, 96 + u:97 + u], None, MUL).then_inc(p_norm, 1)
            power2(1)
            with pool.Fori(0, 4) as h:
                pool.wait_ge(var_ready, h + 1)
                g.tensor_tensor(st2[:, 140:144], st2[:, 136:140], half_m[:, 0:4], ALU.pow).then_inc(rstd, 1)
            power2(2)
def constants():
    p = np.arange(P)
    t = np.concatenate([16 * np.arange(32), np.arange(16)]).astype(np.float32)
    invA = (np.float32(500000.0) ** (-np.arange(0, 16, 2, dtype=np.float32) / np.float32(16))).astype(np.float32)
    k = np.arange(256)[None, :] - P
    q = p[:, None]
    m0 = (k <= q) & (k >= q - P)
    k = np.arange(512)[None, :] - 384
    masks = [m0] + [(k <= q) & ((q - k) % d == 0) for d in (4, 16)]
    masks = np.where(np.concatenate(masks, 1), 0.0, NEG).astype(np.float32)
    half = np.arange(0, 64, 2, dtype=np.float32) / np.float32(64)
    inv_m = np.float32(1.0) / np.float32(10000.0) ** half
    inv_r = np.float32(1.0) / np.float32(10000.0) ** (np.arange(0, RK, 2, dtype=np.float32) / np.float32(RK))
    misc = np.zeros((P, 67), np.float32)
    tt = np.arange(T)
    for g, w in enumerate(POOLS):
        count = np.clip(tt + w // 2 - 1, 0, T - 1) - np.clip(tt - w // 2, 0, T - 1) + 1
        c = w / count
        misc[:, 16 * g:16 * g + 16] = np.concatenate([c[:8], c[-8:]])
    misc[:, 64], misc[:, 65] = inv_r, inv_m[p % 32]
    misc[:, 66] = np.where(p % 64 < 32, -1.0, 1.0)
    return {
        "c_misc": misc,
        "c_delta": (np.arange(DELTAS)[None, :] - 3 * P - p[:, None]).astype(np.float32),
        "c_ident": np.eye(P, dtype=np.float32),
        "c_t": np.tile(t, (P, 1)),
        "c_angA": np.ascontiguousarray(np.tile(invA, (P, TT, 1))),
        "c_masks": masks,
    }


def columns_of(w):
    return w.reshape(-1, P, w.shape[1]).transpose(1, 0, 2)


def layout(x):
    w_in = x["w_in"][0]
    at = {"u": 0, "zs": 1024, "q": 2048, "k": 3584, "v": 5120, "za": 6656, "rs": 7168, "ra": 8192}
    d = {"x": x["x"]}
    loop_w = []
    for m in range(KT):
        parts = [columns_of(w_in[:, at["u"] + m * P:at["u"] + (m + 1) * P])]
        parts += [columns_of(w_in[:, at[n] + m * PC:at[n] + (m + 1) * PC]) for n in "qkv"]
        loop_w.append(np.concatenate([v.reshape(P, -1) for v in parts], 1))
    d["loop_w"] = np.stack(loop_w)
    src = {"glu": x["w_glu"][0], "so": x["w_ssm_out"][0], "ao": x["w_attn_out"][0], "wo": x["w_o"][0]}
    for n in ("zs", "za", "rs", "ra"):
        src[n] = w_in[:, at[n]:]
    a_in, r_in = x["a_w_in_2"][0], x["r_w_in_2"][0]
    lora = QL + KVL + MR
    src.update(pu=a_in[:, lora:], ga=a_in[:, lora + D:], gb=a_in[:, lora + 2 * D:], rq=r_in, rk=r_in[:, D:], rv=r_in[:, 2 * D:],
               rg=r_in[:, 4 * D:])
    w_a = x["a_w_out_2"][0]
    src["oo"], src["tt"] = np.concatenate([w_a[D:], w_a[:D]]), x["r_w_out_2"][0]
    src["lo"] = a_in[:, :lora]
    uq = x["a_w_uq_2"][0].reshape(QL, MH, MN + MR)
    ukv = x["a_w_ukv_2"][0].reshape(KVL, MH, MN + MV)
    panels = []
    for kind, i in stage_plan():
        if kind == "uq":
            h = slice(2 * i, 2 * i + 2)
            rope = uq[:, h, MN:]
            swap = np.concatenate([rope[:, :, MR // 2:], rope[:, :, :MR // 2]], 2)
            q = np.concatenate([v.reshape(QL, -1) for v in (uq[:, h, :MN], rope, swap)], 1)
            kv = np.concatenate([ukv[:, h, :MN].reshape(KVL, -1), ukv[:, h, MN:].reshape(KVL, -1)], 1)
            panels.append(np.concatenate([columns_of(q).reshape(P, -1), kv], 1))
            continue
        if kind in ("wo", "rv", "oo", "tt"):
            rows = src[kind].shape[0] // 512
            r, c = i % rows, i // rows
            v = src[kind][r * 512:(r + 1) * 512, c * 512:(c + 1) * 512]
            panels.append(columns_of(v).reshape(P, -1))
            continue
        if (kind, i) == ("lo", 2):
            rope = a_in[:, QL + KVL:lora]
            swap = np.concatenate([rope[:, MR // 2:], rope[:, :MR // 2]], 1)
            panels.append(columns_of(np.concatenate([rope, rope, swap, swap], 1)).reshape(P, -1))
            continue
        v = columns_of(src[kind][:, i * 256:(i + 1) * 256]).reshape(P, -1)
        panels.append(np.pad(v, ((0, 0), (0, PANEL - v.shape[1]))))
    d["panels"] = np.stack(panels)
    lam = [x["lam_re"][0], x["lam_im"][0], np.repeat(x["log_dt"][0][:, None], NST, 1)]
    d["ssm_par"] = np.stack([v.reshape(NTILE, P).T for v in lam], 1)
    b = np.zeros((P, 2, NTILE, 2, GCH), np.float32)
    c = np.zeros((P, KT, 2, SPM, 2, GCH), np.float32)
    for n, (bx, cx) in enumerate(((x["b_re"][0], x["c_re"][0]), (x["b_im"][0], x["c_im"][0]))):
        b2 = bx.reshape(NTILE, 2, NST, GCH)
        c2 = cx.reshape(KT, SPM, 2, GCH, NST)
        for g in range(2):
            b[g * NST:(g + 1) * NST, n, :, g, :] = b2[:, g].transpose(1, 0, 2)
            c[g * NST:(g + 1) * NST, :, n, :, g, :] = c2[:, :, g].transpose(3, 0, 1, 2)
    d["ssm_b"] = b.reshape(P, 2, NTILE, 32)
    d["ssm_c"] = c.reshape(P, KT, 256)
    qk = [np.repeat(x[n][0], HEADS, 0).reshape(KT, PC) for n in ("q_norm_w", "k_norm_w")]
    d["qk_w"] = np.stack(qk, 1)
    d["pool_w"] = x["a_pool_w_2"][0].reshape(4, 2, P, 256).transpose(2, 0, 1, 3)
    d["positions_2"] = x["positions_2"].reshape(1, T)
    d["decays"] = np.concatenate([x["r_decay_fwd_2"], x["r_decay_bwd_2"]], 1)
    d["final_g"] = x["final_norm_g_2"].reshape(1, D)
    d["pos1"] = x["positions"].reshape(TT, P).T
    vec = {"norm_w": "norm_w", "d_skip": "d_skip", "a_norm": "a_norm_g_2", "q_norm": "a_q_norm_g_2",
           "kv_norm": "a_kv_norm_g_2", "pool_scale": "a_pool_scale_2", "r_norm": "r_norm_g_2", "gn": "r_gn_g_2"}
    cols = np.zeros((P, 64), np.float32)
    for n, at_ in COLS.items():
        v = x[vec[n]].reshape(-1, P).T
        cols[:, at_:at_ + v.shape[1]] = v
    d["cols"] = cols
    d.update(constants())
    return {n: np.ascontiguousarray(v) for n, v in d.items()}


def kernel(**inputs):
    import concourse.bacc as bacc
    from concourse.bass_utils import run_bass_kernel_spmd

    arrays = layout({n: np.asarray(v) for n, v in inputs.items()})
    nc = bacc.Bacc("TRN2", target_bir_lowering=False, num_devices=1)
    a = {n: nc.dram_tensor(n, v.shape, mybir.dt.from_np(v.dtype), kind="ExternalInput").ap() for n, v in arrays.items()}
    out = nc.dram_tensor("out", (1, T, D), f32, kind="ExternalOutput").ap()
    build(nc, a, out)
    r = run_bass_kernel_spmd(nc, [arrays], core_ids=[0])
    return r.results[0]["out"]
```
